# Optimizing a Trainium2 kernel written in Bass

```python
import math
import jax, jax.numpy as jnp
from jax import lax
import numpy as np

D_MODEL = 1024
BATCH = 1
SEQ = 1024
DEPTH = 1
DEC_BATCH = 8
DEC_SEQ = 8
PAST_LEN = 4096
PAGE_SIZE = 128

ATT_HEADS = 8
N_KV_HEADS = 2
HEAD_DIM = 64
ATT_WIDTH = ATT_HEADS * HEAD_DIM
ROPE_THETA = 500000.0
IDX_HEADS = 8
IDX_DIM = 64
TOPK_MAX = 256
Q_BLOCK = 128
GDN_HEADS = 4
GDN_DK = 128
GDN_DV = 128
GDN_WIDTH = GDN_HEADS * GDN_DV
GDN_CONV_DIM = 2 * GDN_HEADS * GDN_DK + GDN_WIDTH
CONV_K = 4
GDN_CHUNK = 64
MIX_WIDTH = ATT_WIDTH + GDN_WIDTH
D_FF = 2816
LN_EPS = 1e-5
NORM_EPS = 1e-6
DEEP_ALPHA = (2 * DEPTH) ** 0.25
DEEP_BETA = (8 * DEPTH) ** -0.25
SPLITS = (ATT_WIDTH, N_KV_HEADS * HEAD_DIM, N_KV_HEADS * HEAD_DIM, IDX_HEADS * IDX_DIM, IDX_DIM, IDX_HEADS,
          GDN_CONV_DIM, GDN_WIDTH, GDN_HEADS, GDN_HEADS)
IN_WIDTH = sum(SPLITS)
SPLIT_POINTS = tuple(int(s) for s in np.cumsum(SPLITS)[:-1])

kernel_name = 'dsa_gdn_macaron_deepnorm_step'

def layer_norm(x, g, b):
    xf = x.astype(jnp.float32)
    mu = jnp.mean(xf, -1, keepdims=True)
    var = jnp.mean(jnp.square(xf - mu), -1, keepdims=True)
    return ((xf - mu) * lax.rsqrt(var + LN_EPS) * g.astype(jnp.float32) + b.astype(jnp.float32)).astype(x.dtype)

def swiglu(x, w_gate, w_up, w_down):
    return (jax.nn.silu(x @ w_gate) * (x @ w_up)) @ w_down

def ffn_half_step(x, w_gate, w_up, w_down, g, b):
    return layer_norm(DEEP_ALPHA * x + 0.5 * swiglu(x, w_gate, w_up, w_down), g, b)

def mixer_residual(x, att, gdn, w_o, g, b):
    return layer_norm(DEEP_ALPHA * x + jnp.concatenate([att, gdn], -1) @ w_o, g, b)

def rope_partial(x, pos):
    d_rot = x.shape[-1] // 4
    half = d_rot // 2
    inv_freq = ROPE_THETA ** (-jnp.arange(half, dtype=jnp.float32) / half)
    ang = pos.astype(jnp.float32)[:, None] * inv_freq[None, :]
    cos = jnp.cos(ang)[None, :, None, :]
    sin = jnp.sin(ang)[None, :, None, :]
    xr = x[..., :d_rot].astype(jnp.float32)
    x1, x2 = xr[..., :half], xr[..., half:]
    rot = jnp.concatenate([x1 * cos - x2 * sin, x2 * cos + x1 * sin], -1).astype(x.dtype)
    return jnp.concatenate([rot, x[..., d_rot:]], -1)

def mix_projection(h, w_in, pos):
    B, T, _ = h.shape
    q, k, v, qi, ki, wi, qkv, z, b_g, a_g = jnp.split(h @ w_in, SPLIT_POINTS, axis=-1)
    q = rope_partial(q.reshape(B, T, ATT_HEADS, HEAD_DIM), pos)
    k = rope_partial(k.reshape(B, T, N_KV_HEADS, HEAD_DIM), pos)
    v = v.reshape(B, T, N_KV_HEADS, HEAD_DIM)
    qi = rope_partial(qi.reshape(B, T, IDX_HEADS, IDX_DIM), pos)
    ki = rope_partial(ki.reshape(B, T, 1, IDX_DIM), pos)[:, :, 0]
    wi = wi * IDX_HEADS ** -0.5
    return q, k, v, qi, ki, wi, qkv, z, b_g, a_g

def indexer_scores(qi, wi, ki):
    s = jnp.einsum('bqhd,bld->bqhl', qi.astype(jnp.float32), ki.astype(jnp.float32)) * IDX_DIM ** -0.5
    return jnp.einsum('bqhl,bqh->bql', jax.nn.relu(s), wi.astype(jnp.float32))

def sparse_attend(q, ks, vs, valid):
    B, Q, H, d = q.shape
    G = H // N_KV_HEADS
    qg = q.reshape(B, Q, N_KV_HEADS, G, d).astype(jnp.float32)
    s = jnp.einsum('bqkgd,bqnkd->bqkgn', qg, ks.astype(jnp.float32)) * d ** -0.5
    p = jax.nn.softmax(jnp.where(valid[:, :, None, None, :], s, -jnp.inf), axis=-1)
    o = jnp.einsum('bqkgn,bqnkd->bqkgd', p, vs.astype(jnp.float32))
    return o.reshape(B, Q, H * d).astype(q.dtype)

def dsa_prompt(q, k, v, qi, ki, wi):
    B, S = q.shape[:2]
    nblk = S // Q_BLOCK
    ksel = min(TOPK_MAX, S // 4)
    key_pos = jnp.arange(S)
    bidx = jnp.arange(B)[:, None, None]

    def blocks(a):
        return jnp.swapaxes(a.reshape((B, nblk, Q_BLOCK) + a.shape[2:]), 0, 1)

    def attend_block(args):
        q_b, qi_b, wi_b, pos_b = args
        score = indexer_scores(qi_b, wi_b, ki)
        score = jnp.where(key_pos[None, None, :] <= pos_b[None, :, None], score, -jnp.inf)
        _, idx = lax.top_k(score, ksel)
        return sparse_attend(q_b, k[bidx, idx], v[bidx, idx], idx <= pos_b[None, :, None])

    out = lax.map(attend_block, (blocks(q), blocks(qi), blocks(wi), key_pos.reshape(nblk, Q_BLOCK)))
    return jnp.swapaxes(out, 0, 1).reshape(B, S, ATT_WIDTH)

def dsa_sample(q, k, v, qi, ki, wi, cache_k, cache_v, cache_kidx, page_table, layer):
    B, T = q.shape[:2]
    page = cache_k.shape[2]
    past = page_table.shape[1] * page
    L = past + T
    ksel = min(TOPK_MAX, L // 4)
    ki_past = cache_kidx[layer, page_table].reshape(B, past, IDX_DIM)
    ki_all = jnp.concatenate([ki_past, ki.astype(ki_past.dtype)], 1)
    pos_q = past + jnp.arange(T)
    score = indexer_scores(qi, wi, ki_all)
    score = jnp.where(jnp.arange(L)[None, None, :] <= pos_q[None, :, None], score, -jnp.inf)
    _, idx = lax.top_k(score, ksel)
    bidx = jnp.arange(B)[:, None, None]
    from_past = (idx < past)[..., None, None]
    pidx = jnp.minimum(idx, past - 1)
    phys = page_table[bidx, pidx // page]
    off = pidx % page
    nidx = jnp.clip(idx - past, 0, T - 1)
    ks = jnp.where(from_past, cache_k[layer, phys, off], k[bidx, nidx].astype(cache_k.dtype))
    vs = jnp.where(from_past, cache_v[layer, phys, off], v[bidx, nidx].astype(cache_v.dtype))
    return sparse_attend(q, ks, vs, idx <= pos_q[None, :, None])

def l2norm(x):
    xf = x.astype(jnp.float32)
    return xf * lax.rsqrt(jnp.sum(jnp.square(xf), -1, keepdims=True) + NORM_EPS)

def gated_delta_chunked(q, k, v, g, beta, s0):
    B, T, H, dk = q.shape
    dv = v.shape[-1]
    C = GDN_CHUNK
    n = -(-T // C)
    pad = n * C - T

    def to_chunks(a):
        a = jnp.pad(a.astype(jnp.float32), [(0, 0), (0, pad)] + [(0, 0)] * (a.ndim - 2))
        return jnp.swapaxes(jnp.moveaxis(a.reshape((B, n, C) + a.shape[2:]), 1, 0), 2, 3)

    qc = to_chunks(q) * dk ** -0.5
    kc, vc, gc, bc = to_chunks(k), to_chunks(v), to_chunks(g), to_chunks(beta)
    gc = jnp.cumsum(gc, -1)
    causal = jnp.tril(jnp.ones((C, C), bool))
    strict = jnp.tril(jnp.ones((C, C), bool), -1)
    decay = jnp.exp(jnp.where(causal, gc[..., :, None] - gc[..., None, :], -jnp.inf))
    kb = kc * bc[..., None]
    m = jnp.where(strict, jnp.einsum('nbhid,nbhjd->nbhij', kb, kc) * decay, 0.0)
    rhs = jnp.concatenate([vc * bc[..., None], kb * jnp.exp(gc)[..., None]], -1)
    sol = lax.linalg.triangular_solve(m + jnp.eye(C, dtype=jnp.float32), rhs,
                                      left_side=True, lower=True, unit_diagonal=True)
    u, w = sol[..., :dv], sol[..., dv:]
    qk = jnp.where(causal, jnp.einsum('nbhid,nbhjd->nbhij', qc, kc) * decay, 0.0)

    def step(S, xs):
        q_i, k_i, u_i, w_i, g_i, qk_i = xs
        v_new = u_i - jnp.einsum('bhck,bhkv->bhcv', w_i, S)
        o_i = (jnp.einsum('bhck,bhkv->bhcv', q_i * jnp.exp(g_i)[..., None], S)
               + jnp.einsum('bhij,bhjv->bhiv', qk_i, v_new))
        g_last = g_i[..., -1]
        S = (S * jnp.exp(g_last)[..., None, None]
             + jnp.einsum('bhck,bhcv->bhkv', k_i * jnp.exp(g_last[..., None] - g_i)[..., None], v_new))
        return S, o_i

    S, o = lax.scan(step, s0.astype(jnp.float32), (qc, kc, u, w, gc, qk))
    o = jnp.moveaxis(jnp.swapaxes(o, 2, 3), 0, 1).reshape(B, n * C, H, dv)[:, :T]
    return o, S

def gdn_branch(qkv, z, b_g, a_g, conv_buf, s0, conv_w, a_log, dt_bias, norm_w):
    B, T, _ = qkv.shape
    xin = jnp.concatenate([conv_buf.astype(qkv.dtype), qkv], 1)
    y = lax.conv_general_dilated(xin, conv_w[:, None, :].astype(qkv.dtype), window_strides=(1,), padding='VALID',
                                 dimension_numbers=('NWC', 'WIO', 'NWC'), feature_group_count=GDN_CONV_DIM)
    y = jax.nn.silu(y)
    nq = GDN_HEADS * GDN_DK
    q = l2norm(y[..., :nq].reshape(B, T, GDN_HEADS, GDN_DK))
    k = l2norm(y[..., nq:2 * nq].reshape(B, T, GDN_HEADS, GDN_DK))
    v = y[..., 2 * nq:].reshape(B, T, GDN_HEADS, GDN_DV)
    beta = jax.nn.sigmoid(b_g.astype(jnp.float32))
    g = -jnp.exp(a_log.astype(jnp.float32)) * jax.nn.softplus(a_g.astype(jnp.float32) + dt_bias.astype(jnp.float32))
    o, s = gated_delta_chunked(q, k, v, g, beta, s0)
    o = o * lax.rsqrt(jnp.mean(jnp.square(o), -1, keepdims=True) + NORM_EPS) * norm_w.astype(jnp.float32)
    o = o * jax.nn.silu(z.reshape(B, T, GDN_HEADS, GDN_DV).astype(jnp.float32))
    return o.reshape(B, T, GDN_WIDTH).astype(qkv.dtype), s.astype(s0.dtype), xin[:, T:]

def setup_inputs(seed: int = 0) -> dict:
    key = jax.random.key(seed)
    ks = jax.random.split(key, 32)
    f32 = jnp.float32
    n_pages = PAST_LEN // PAGE_SIZE
    n_pool = (DEC_BATCH * n_pages * 5) // 4

    def nrm(k, shape, scale):
        return jax.random.normal(k, shape, f32) * scale

    def gain(k, n):
        return 1.0 + 0.02 * jax.random.normal(k, (DEPTH, n), f32)

    def bias(k, n):
        return 0.02 * jax.random.normal(k, (DEPTH, n), f32)

    dt = jnp.exp(jax.random.uniform(ks[14], (DEPTH, GDN_HEADS), f32, math.log(1e-3), math.log(1e-1)))
    page_table = jax.random.permutation(ks[7], n_pool)[:DEC_BATCH * n_pages].reshape(DEC_BATCH, n_pages).astype(jnp.int32)
    return {
        'x_prompt': nrm(ks[0], (BATCH, SEQ, D_MODEL), 1.0),
        'x_sample': nrm(ks[1], (DEC_BATCH, DEC_SEQ, D_MODEL), 1.0),
        'cache_k': nrm(ks[2], (DEPTH, n_pool, PAGE_SIZE, N_KV_HEADS, HEAD_DIM), 1.0),
        'cache_v': nrm(ks[3], (DEPTH, n_pool, PAGE_SIZE, N_KV_HEADS, HEAD_DIM), 1.0),
        'cache_kidx': nrm(ks[4], (DEPTH, n_pool, PAGE_SIZE, IDX_DIM), 1.0),
        'state_gdn': nrm(ks[5], (DEPTH, DEC_BATCH, GDN_HEADS, GDN_DK, GDN_DV), 0.1),
        'state_conv': nrm(ks[6], (DEPTH, DEC_BATCH, CONV_K - 1, GDN_CONV_DIM), 1.0),
        'page_table': page_table,
        'ffn1_w_gate': nrm(ks[8], (DEPTH, D_MODEL, D_FF), D_MODEL ** -0.5),
        'ffn1_w_up': nrm(ks[9], (DEPTH, D_MODEL, D_FF), D_MODEL ** -0.5),
        'ffn1_w_down': nrm(ks[10], (DEPTH, D_FF, D_MODEL), DEEP_BETA * D_FF ** -0.5),
        'ln1_g': gain(ks[11], D_MODEL),
        'ln1_b': bias(ks[12], D_MODEL),
        'w_in': nrm(ks[13], (DEPTH, D_MODEL, IN_WIDTH), D_MODEL ** -0.5),
        'conv_w': nrm(ks[15], (DEPTH, CONV_K, GDN_CONV_DIM), CONV_K ** -0.5),
        'a_log': jnp.log(jax.random.uniform(ks[16], (DEPTH, GDN_HEADS), f32, 1.0, 16.0)),
        'dt_bias': dt + jnp.log(-jnp.expm1(-dt)),
        'gdn_norm_w': gain(ks[17], GDN_DV),
        'w_o': nrm(ks[18], (DEPTH, MIX_WIDTH, D_MODEL), DEEP_BETA * MIX_WIDTH ** -0.5),
        'ln2_g': gain(ks[19], D_MODEL),
        'ln2_b': bias(ks[20], D_MODEL),
        'ffn2_w_gate': nrm(ks[21], (DEPTH, D_MODEL, D_FF), D_MODEL ** -0.5),
        'ffn2_w_up': nrm(ks[22], (DEPTH, D_MODEL, D_FF), D_MODEL ** -0.5),
        'ffn2_w_down': nrm(ks[23], (DEPTH, D_FF, D_MODEL), DEEP_BETA * D_FF ** -0.5),
        'ln3_g': gain(ks[24], D_MODEL),
        'ln3_b': bias(ks[25], D_MODEL),
    }

def reference(x_prompt, x_sample, cache_k, cache_v, cache_kidx, state_gdn, state_conv, page_table,
              ffn1_w_gate, ffn1_w_up, ffn1_w_down, ln1_g, ln1_b, w_in, conv_w, a_log, dt_bias, gdn_norm_w,
              w_o, ln2_g, ln2_b, ffn2_w_gate, ffn2_w_up, ffn2_w_down, ln3_g, ln3_b):
    B, S, _ = x_prompt.shape
    T = x_sample.shape[1]
    past = page_table.shape[1] * cache_k.shape[2]
    pos_p = jnp.arange(S)
    pos_s = past + jnp.arange(T)
    xp, xs = x_prompt, x_sample
    kp_l, vp_l, ip_l, sp_l, cp_l = [], [], [], [], []
    ks_l, vs_l, is_l, ss_l, cs_l = [], [], [], [], []
    for l in range(DEPTH):
        xp = ffn_half_step(xp, ffn1_w_gate[l], ffn1_w_up[l], ffn1_w_down[l], ln1_g[l], ln1_b[l])
        xs = ffn_half_step(xs, ffn1_w_gate[l], ffn1_w_up[l], ffn1_w_down[l], ln1_g[l], ln1_b[l])
        q, k, v, qi, ki, wi, qkv, z, b_g, a_g = mix_projection(xp, w_in[l], pos_p)
        att = dsa_prompt(q, k, v, qi, ki, wi)
        gdn, s_new, c_new = gdn_branch(qkv, z, b_g, a_g, jnp.zeros((B, CONV_K - 1, GDN_CONV_DIM), xp.dtype),
                                       jnp.zeros((B, GDN_HEADS, GDN_DK, GDN_DV), jnp.float32),
                                       conv_w[l], a_log[l], dt_bias[l], gdn_norm_w[l])
        xp = mixer_residual(xp, att, gdn, w_o[l], ln2_g[l], ln2_b[l])
        kp_l.append(k); vp_l.append(v); ip_l.append(ki); sp_l.append(s_new); cp_l.append(c_new)
        q, k, v, qi, ki, wi, qkv, z, b_g, a_g = mix_projection(xs, w_in[l], pos_s)
        att = dsa_sample(q, k, v, qi, ki, wi, cache_k, cache_v, cache_kidx, page_table, l)
        gdn, s_new, c_new = gdn_branch(qkv, z, b_g, a_g, state_conv[l], state_gdn[l],
                                       conv_w[l], a_log[l], dt_bias[l], gdn_norm_w[l])
        xs = mixer_residual(xs, att, gdn, w_o[l], ln2_g[l], ln2_b[l])
        ks_l.append(k); vs_l.append(v); is_l.append(ki); ss_l.append(s_new); cs_l.append(c_new)
        xp = ffn_half_step(xp, ffn2_w_gate[l], ffn2_w_up[l], ffn2_w_down[l], ln3_g[l], ln3_b[l])
        xs = ffn_half_step(xs, ffn2_w_gate[l], ffn2_w_up[l], ffn2_w_down[l], ln3_g[l], ln3_b[l])
    return (xp, xs,
            jnp.stack(kp_l), jnp.stack(vp_l), jnp.stack(ip_l), jnp.stack(sp_l), jnp.stack(cp_l),
            jnp.stack(ks_l), jnp.stack(vs_l), jnp.stack(is_l), jnp.stack(ss_l), jnp.stack(cs_l))


_drawn_inputs = setup_inputs


def setup_inputs(seed=0):
    import zlib

    import numpy as np

    out = dict(_drawn_inputs(seed))
    spreads = {}
    factors = {'gdn_norm_w': 66.427,
     'ln2_g': 2.806,
     'ln2_b': 2.911,
     'ln3_g': 23.42,
     'ln3_b': 22.96,
     'cache_k': 3.589,
     'cache_v': 2.828,
     'cache_kidx': 2.955}
    for name, (base, spread) in spreads.items():
        noise = np.random.default_rng([zlib.crc32(name.encode()), seed]).standard_normal(out[name].shape)
        drawn = base * np.exp(spread * noise) if base else spread * noise
        out[name] = __import__('jax').numpy.asarray(drawn.astype(out[name].dtype))
    for name, factor in factors.items():
        out[name] = (out[name] * factor).astype(out[name].dtype)
    return out
```

```python
from contextlib import ExitStack

import numpy as np

import concourse.bass as bass
from concourse import mybir

F32 = mybir.dt.float32
F32R = mybir.dt.float32r
BF16 = mybir.dt.bfloat16
I32 = mybir.dt.int32
ALU = mybir.AluOpType
ACT = mybir.ActivationFunctionType
AX = mybir.AxisListType

P = 128
D = 1024
KT = D // P
PROMPT = 1024
DEC_B, DEC_T = 8, 8
SAMPLE = DEC_B * DEC_T
NT = PROMPT + SAMPLE
SLICES = 3
SL = 364
TP = SLICES * SL
TILES = 9
D_FF = 2816
FB = D_FF // P
CHUNKS = FB // 2
ALPHA = 2.0 ** 0.25
LN_EPS = 1e-5
NORM_EPS = 1e-6


def tile_width(t):
    return P if t < PROMPT // P else SAMPLE


def slices(t):
    return [slice(s * SL, (s + 1) * SL) for s in range(t)]


class Scope:

    def __init__(self, nc, ctx, name):
        self.nc, self.ctx, self.name = nc, ctx, name

    def sb(self, name, shape, dt=F32):
        return self.ctx.enter_context(self.nc.sbuf_tensor(f"{self.name}_{name}", shape, dt))

    def ps(self, name, shape, dt=F32):
        return self.ctx.enter_context(self.nc.psum_tensor(f"{self.name}_{name}", shape, dt))

    def sem(self, name):
        return self.nc.alloc_semaphore(f"{self.name}_{name}")


def three_pass(pe, out, w_hi, w_lo, x_hi, x_lo, ks, start=True, stop=True):
    last = None
    for n, k in enumerate(ks):
        for p, (w, x) in enumerate(((w_hi, x_hi), (w_hi, x_lo), (w_lo, x_hi))):
            for s in range(SLICES):
                last = pe.matmul(out[:, s, 0:SL], w(k), x(k)[:, s * SL:(s + 1) * SL],
                                 start=start and n == 0 and p == 0, stop=stop and n == len(ks) - 1 and p == 2)
    return last


def load_tokens(nc, x_prompt, x_sample, ident, res, x_hi, x_lo):
    with ExitStack() as ctx:
        sc = Scope(nc, ctx, "load")
        rows = sc.sb("rows", [P, 2, D])
        turned = sc.ps("turned", [P, 2, KT, P])
        rows_in = [sc.sem("rows_in0"), sc.sem("rows_in1")]
        turned_done, hi_done, lo_done, res_done, pads = (sc.sem(n) for n in (
            "turned_done", "hi_done", "lo_done", "res_done", "pads"))
        block = ctx.enter_context(nc.Block())

        @block.sync
        def _(sp):
            for t in range(TILES):
                w = tile_width(t)
                src = x_prompt[0, t * P:(t + 1) * P, :] if t < TILES - 1 else x_sample.rearrange("b t d -> (b t) d")
                if t >= 2:
                    sp.wait_ge(turned_done, t - 1)
                sp.dma_start(rows[0:w, t % 2, :], src).then_inc(rows_in[t % 2], 16)

        @block.tensor
        def _(pe):
            for t in range(TILES):
                w = tile_width(t)
                pe.wait_ge(rows_in[t % 2], 16 * (t // 2 + 1))
                if t >= 2:
                    pe.wait_ge(lo_done, t - 1)
                    pe.wait_ge(res_done, t - 1)
                for k in range(KT):
                    last = pe.transpose(turned[:, t % 2, k, 0:w], rows[0:w, t % 2, k * P:(k + 1) * P],
                                        ident[0:w, 0:w])
                last.then_inc(turned_done, 1)

        @block.scalar
        def _(act):
            for t in range(TILES):
                w, c = tile_width(t), t * P
                act.wait_ge(turned_done, t + 1)
                act.activation(x_hi[:, :, c:c + w], turned[:, t % 2, :, 0:w], ACT.Copy).then_inc(hi_done, 1)

        @block.vector
        def _(dve):
            for buf in (x_hi, x_lo, res):
                dve.memset(buf[:, :, NT:TP].bitcast(F32) if buf is not res else buf[:, :, NT:TP], 0.0)
            for t in range(TILES):
                w, c = tile_width(t), t * P
                dve.wait_ge(hi_done, t + 1)
                dve.tensor_scalar(res[:, :, c:c + w], turned[:, t % 2, :, 0:w], ALPHA, None,
                                  ALU.mult).then_inc(res_done, 1)
                dve.tensor_tensor(x_lo[:, :, c:c + w], turned[:, t % 2, :, 0:w],
                                  x_hi[:, :, c:c + w].bitcast(F32), ALU.subtract).then_inc(lo_done, 1)


def ffn(nc, name, w_gate, w_up, w_down, res, x_hi, x_lo):
    with ExitStack() as ctx:
        sc = Scope(nc, ctx, name)
        raw = {k: sc.sb(f"raw_{k}", [P, 1024]) for k in "gud"}
        hi = {k: sc.sb(f"hi_{k}", [P, 1024], F32R) for k in "gu"}
        lo = {k: sc.sb(f"lo_{k}", [P, 1024], F32R) for k in "gu"}
        d_hi = sc.sb("hi_d", [P, 2, 1024], F32R)
        d_lo = sc.sb("lo_d", [P, 2, 1024], F32R)
        act_buf = sc.sb("hidden", [P, 2, TP])
        h_hi = sc.sb("h_hi", [P, 2, 2, TP], F32R)
        h_lo = sc.sb("h_lo", [P, 2, 2, TP], F32R)
        ps_a = sc.ps("ps_a", [P, SLICES, 512])
        ps_b = sc.ps("ps_b", [P, SLICES, 512])
        raw_in = {k: sc.sem(f"raw_in_{k}") for k in "gud"}
        whi_done = {k: sc.sem(f"whi_done_{k}") for k in "gud"}
        wlo_done = {k: sc.sem(f"wlo_done_{k}") for k in "gud"}
        gate_filled, up_filled, down_filled = (sc.sem(n) for n in ("gate_filled", "up_filled", "down_filled"))
        silu_done, mul_done, hhi_done, hlo_done, down_added = (sc.sem(n) for n in (
            "silu_done", "mul_done", "hhi_done", "hlo_done", "down_added"))
        filled = {"g": gate_filled, "u": up_filled}
        block = ctx.enter_context(nc.Block())

        def weight_block(w, n):
            return w[0, :, bass.ts(n, P)].rearrange("(k p) f -> p k f", p=P)

        def load(eng, kind, n, first):
            if not first:
                eng.wait_ge(wlo_done[kind], n)
            if kind == "d":
                src = w_down[0, bass.ts(n, P), :]
                dst = raw["d"][:, :]
            else:
                src = weight_block(w_gate if kind == "g" else w_up, n)
                dst = raw[kind][:, :].rearrange("p (k f) -> p k f", k=KT)
            eng.dma_start(dst, src).then_inc(raw_in[kind], 16)

        @block.sync
        def _(sp):
            load(sp, "g", 0, True)
            load(sp, "u", 0, True)
            with sp.Fori(1, FB) as n:
                load(sp, "g", n, False)
                load(sp, "u", n, False)

        @block.gpsimd
        def _(pool):
            load(pool, "d", 0, True)
            with pool.Fori(1, FB) as n:
                load(pool, "d", n, False)

        @block.tensor
        def _(pe):
            def gates(g, par, first=False):
                for fb in range(2):
                    n = g * 2 + fb
                    pe.wait_ge(wlo_done["g"], n + 1)
                    if fb == 1 or not first:
                        pe.wait_ge(silu_done, n)
                    if fb == 0 and not first:
                        pe.wait_ge(down_added, g * 8 - 8)
                    three_pass(pe, ps_a, lambda k: hi["g"][:, k * P:(k + 1) * P],
                               lambda k: lo["g"][:, k * P:(k + 1) * P],
                               lambda k: x_hi[:, k], lambda k: x_lo[:, k], range(KT)).then_inc(gate_filled, 1)
                    pe.wait_ge(wlo_done["u"], n + 1)
                    if fb == 1 or not first:
                        pe.wait_ge(mul_done, n)
                    three_pass(pe, ps_b, lambda k: hi["u"][:, k * P:(k + 1) * P],
                               lambda k: lo["u"][:, k * P:(k + 1) * P],
                               lambda k: x_hi[:, k], lambda k: x_lo[:, k], range(KT)).then_inc(up_filled, 1)

            def down(d, par, last=False):
                pe.wait_ge(wlo_done["d"], d * 2 + 2)
                pe.wait_ge(hlo_done, d * 2 + 2)
                if last:
                    pe.wait_ge(down_added, d * 8)
                for m in range(8):
                    if m == 0:
                        pe.wait_ge(silu_done, d * 2 + (2 if last else 4))
                    elif m == 1:
                        pe.wait_ge(mul_done, d * 2 + (2 if last else 4))
                    else:
                        pe.wait_ge(down_added, d * 8 + m - 1)
                    three_pass(pe, ps_a if m % 2 == 0 else ps_b,
                               lambda k: d_hi[:, k, m * P:(m + 1) * P], lambda k: d_lo[:, k, m * P:(m + 1) * P],
                               lambda k: h_hi[:, par, k], lambda k: h_lo[:, par, k], range(2)
                               ).then_inc(down_filled, 1)

            gates(0, 0, first=True)
            with pe.Fori(0, CHUNKS // 2) as i:
                gates(i * 2 + 1, 1)
                down(i * 2, 0)
                gates(i * 2 + 2, 0)
                down(i * 2 + 1, 1)
            down(CHUNKS - 1, 0, last=True)

        def per_chunk(eng, gates, down):
            gates(0, 0, True, False)
            with eng.Fori(0, CHUNKS // 2 - 1) as i:
                gates(i * 2 + 1, 1, False, False)
                down(i * 2, False)
                gates(i * 2 + 2, 0, False, False)
                down(i * 2 + 1, False)
            gates(CHUNKS - 2, 1, False, False)
            down(CHUNKS - 3, False)
            gates(CHUNKS - 1, 0, False, True)
            down(CHUNKS - 2, False)
            down(CHUNKS - 1, True)

        @block.scalar
        def _(act):
            def weight_hi(kind, n, first=False):
                act.wait_ge(raw_in[kind], (n + 1) * 16)
                if not first:
                    act.wait_ge(filled[kind], n)
                act.activation(hi[kind][:, :], raw[kind][:, :], ACT.Copy).then_inc(whi_done[kind], 1)

            def down_hi(d, first=False):
                for k in range(2):
                    act.wait_ge(raw_in["d"], (d * 2 + k + 1) * 16)
                    if not first:
                        act.wait_ge(down_filled, d * 8)
                    act.activation(d_hi[:, k, :], raw["d"][:, :], ACT.Copy).then_inc(whi_done["d"], 1)

            def gates(g, par, first, last):
                for fb in range(2):
                    n = g * 2 + fb
                    act.wait_ge(gate_filled, n + 1)
                    if not first:
                        act.wait_ge(hlo_done, n - 1)
                    act.activation(act_buf[:, fb, :].rearrange("p (s c) -> p s c", s=SLICES), ps_a[:, :, 0:SL],
                                   ACT.Silu).then_inc(silu_done, 1)
                    if not (last and fb == 1):
                        weight_hi("g", n + 1)
                    act.wait_ge(mul_done, n + 1)
                    if not first:
                        act.wait_ge(down_filled, g * 8 - 8)
                    act.activation(h_hi[:, par, fb, :], act_buf[:, fb, :], ACT.Copy).then_inc(hhi_done, 1)
                    if not (last and fb == 1):
                        weight_hi("u", n + 1)

            weight_hi("g", 0, first=True)
            weight_hi("u", 0, first=True)
            down_hi(0, first=True)
            per_chunk(act, gates, lambda d, last: None if last else down_hi(d + 1))

        @block.vector
        def _(dve):
            def weight_lo(kind, n):
                dve.wait_ge(whi_done[kind], n + 1)
                dve.tensor_tensor(lo[kind][:, :], raw[kind][:, :], hi[kind][:, :].bitcast(F32),
                                  ALU.subtract).then_inc(wlo_done[kind], 1)

            def down_lo(d):
                for k in range(2):
                    dve.wait_ge(whi_done["d"], d * 2 + k + 1)
                    dve.tensor_tensor(d_lo[:, k, :], raw["d"][:, :], d_hi[:, k, :].bitcast(F32),
                                      ALU.subtract).then_inc(wlo_done["d"], 1)

            def gates(g, par, first, last):
                for fb in range(2):
                    n = g * 2 + fb
                    if not (last and fb == 1):
                        weight_lo("g", n + 1)
                    dve.wait_ge(silu_done, n + 1)
                    dve.wait_ge(up_filled, n + 1)
                    hid = act_buf[:, fb, :].rearrange("p (s c) -> p s c", s=SLICES)
                    dve.tensor_tensor(hid, hid, ps_b[:, :, 0:SL], ALU.mult).then_inc(mul_done, 1)
                    dve.wait_ge(hhi_done, n + 1)
                    dve.tensor_tensor(h_lo[:, par, fb, :], act_buf[:, fb, :], h_hi[:, par, fb, :].bitcast(F32),
                                      ALU.subtract).then_inc(hlo_done, 1)
                    if not (last and fb == 1):
                        weight_lo("u", n + 1)

            def down(d, last):
                dve.wait_ge(down_added, d * 8)
                for m in range(8):
                    dve.wait_ge(down_filled, d * 8 + m + 1)
                    r = res[:, m, :].rearrange("p (s c) -> p s c", s=SLICES)
                    dve.scalar_tensor_tensor(r, (ps_a if m % 2 == 0 else ps_b)[:, :, 0:SL], 0.5, r,
                                             ALU.mult, ALU.add).then_inc(down_added, 1)
                if not last:
                    down_lo(d + 1)

            weight_lo("g", 0)
            weight_lo("u", 0)
            down_lo(0)
            per_chunk(dve, gates, down)


def column_load(eng, dst, vec, sem):
    with eng.bass.allow_non_contiguous_dma(reason="a kilobyte or so of scales"):
        eng.dma_start(dst, vec.rearrange("(k p) -> p k", p=P)).then_inc(sem, 16)


def norm(nc, name, g, b, ones_mean, res, x_hi, x_lo, resid_out=None):
    with ExitStack() as ctx:
        sc = Scope(nc, ctx, name)
        gb = sc.sb("gb", [P, 2, KT])
        sq = sc.sb("sq", [P, 2, TP])
        rstd = sc.sb("rstd", [P, TP])
        mean = sc.ps("mean", [P, SLICES, 512])
        var = sc.ps("var", [P, SLICES, 512])
        gb_in, mean_done, centred, squared, var_done, std_in, std_done, rstd_done, scaled, hi_done, lo_done, \
            res_done, res_out = (sc.sem(n) for n in (
                "gb_in", "mean_done", "centred", "squared", "var_done", "std_in", "std_done", "rstd_done",
                "scaled", "hi_done", "lo_done", "res_done", "res_out"))
        block = ctx.enter_context(nc.Block())

        def split(buf):
            return buf.rearrange("p (s c) -> p s c", s=SLICES)

        @block.sync
        def _(sp):
            column_load(sp, gb[:, 0, :], g[0], gb_in)
            column_load(sp, gb[:, 1, :], b[0], gb_in)
            if resid_out is not None:
                for k in range(KT):
                    sp.wait_ge(res_done, k + 1)
                    sp.dma_start(resid_out[k], res[:, k, :]).then_inc(res_out, 16)
                sp.wait_ge(res_out, 16 * KT)

        @block.tensor
        def _(pe):
            for k in range(KT):
                for s in range(SLICES):
                    last = pe.matmul(mean[:, s, 0:SL], ones_mean[:, :], res[:, k, s * SL:(s + 1) * SL],
                                     start=k == 0, stop=k == KT - 1)
            last.then_inc(mean_done, 1)
            for k in range(KT):
                pe.wait_ge(squared, k + 1)
                for s in range(SLICES):
                    last = pe.matmul(var[:, s, 0:SL], ones_mean[:, :], sq[:, k % 2, s * SL:(s + 1) * SL],
                                     start=k == 0, stop=k == KT - 1)
                last.then_inc(var_done, 1)

        @block.scalar
        def _(act):
            for k in range(KT):
                act.wait_ge(centred, k + 1)
                if k >= 2:
                    act.wait_ge(var_done, k - 1)
                act.activation(sq[:, k % 2, :], res[:, k, :], ACT.Square).then_inc(squared, 1)
            act.wait_ge(std_in, 1)
            act.activation(rstd[:, :], rstd[:, :], ACT.Sqrt).then_inc(std_done, 1)
            if x_hi is not None:
                for k in range(KT):
                    act.wait_ge(scaled, 2 * k + 2)
                    act.activation(x_hi[:, k, :], res[:, k, :], ACT.Copy).then_inc(hi_done, 1)
                for k in range(KT):
                    act.wait_ge(lo_done, k + 1)
                    act.activation(res[:, k, :], res[:, k, :], ACT.Copy, scale=ALPHA).then_inc(res_done, 1)

        @block.vector
        def _(dve):
            dve.wait_ge(mean_done, 1)
            for k in range(KT):
                dve.tensor_tensor(split(res[:, k, :]), split(res[:, k, :]), mean[:, :, 0:SL],
                                  ALU.subtract).then_inc(centred, 1)
            dve.wait_ge(var_done, KT)
            dve.tensor_scalar(split(rstd[:, :]), var[:, :, 0:SL], LN_EPS, None, ALU.add).then_inc(std_in, 1)
            dve.wait_ge(std_done, 1)
            dve.reciprocal(rstd[:, :], rstd[:, :]).then_inc(rstd_done, 1)
            dve.wait_ge(rstd_done, 1)
            dve.wait_ge(gb_in, 32)
            dve.wait_ge(centred, KT)
            dve.wait_ge(squared, KT)
            for k in range(KT):
                dve.tensor_tensor(res[:, k, :], res[:, k, :], rstd[:, :], ALU.mult).then_inc(scaled, 1)
                dve.wait_ge(scaled, 2 * k + 1)
                dve.tensor_scalar(res[:, k, :], res[:, k, :], gb[:, 0, k:k + 1], gb[:, 1, k:k + 1],
                                  ALU.mult, ALU.add).then_inc(scaled, 1)
                if x_hi is not None and k >= 1:
                    dve.wait_ge(hi_done, k)
                    dve.tensor_tensor(x_lo[:, k - 1, :], res[:, k - 1, :], x_hi[:, k - 1, :].bitcast(F32),
                                      ALU.subtract).then_inc(lo_done, 1)
            if x_hi is not None:
                dve.wait_ge(hi_done, KT)
                dve.tensor_tensor(x_lo[:, KT - 1, :], res[:, KT - 1, :], x_hi[:, KT - 1, :].bitcast(F32),
                                  ALU.subtract).then_inc(lo_done, 1)


def store_tokens(nc, ident, res, y_prompt, y_sample):
    with ExitStack() as ctx:
        sc = Scope(nc, ctx, "store")
        rows = sc.sb("rows", [P, 2, D])
        turned = sc.ps("turned", [P, 2, KT, P])
        turned_done, copied, out_done = (sc.sem(n) for n in ("turned_done", "copied", "out_done"))
        out_free = [sc.sem("out_even"), sc.sem("out_odd")]
        block = ctx.enter_context(nc.Block())

        @block.tensor
        def _(pe):
            for t in range(TILES):
                w = tile_width(t)
                if t >= 2:
                    pe.wait_ge(copied, t - 1)
                for k in range(KT):
                    last = pe.transpose(turned[0:w, t % 2, k, :], res[:, k, t * P:t * P + w], ident[:, :])
                last.then_inc(turned_done, 1)

        @block.vector
        def _(dve):
            for t in range(TILES):
                w = tile_width(t)
                dve.wait_ge(turned_done, t + 1)
                if t >= 2:
                    dve.wait_ge(out_free[t % 2], 16 * (t // 2))
                dve.tensor_copy(rows[0:w, t % 2, :].rearrange("p (k f) -> p k f", k=KT),
                                turned[0:w, t % 2, :, :]).then_inc(copied, 1)

        @block.sync
        def _(sp):
            for t in range(TILES):
                w = tile_width(t)
                dst = y_prompt[0, t * P:(t + 1) * P, :] if t < TILES - 1 else y_sample.rearrange("b t d -> (b t) d")
                sp.wait_ge(copied, t + 1)
                sp.dma_start(dst, rows[0:w, t % 2, :]).then_inc(out_free[t % 2], 16)
            sp.wait_ge(out_free[0], 16 * ((TILES + 1) // 2))
            sp.wait_ge(out_free[1], 16 * (TILES // 2))


HD = 64
ATT_H = 8
GH = 4
CONV_K = 4
QKV_BLOCKS = 12
W_Q, W_K, W_V, W_QI, W_KI, W_WI, W_QKV, W_Z, W_BA = 0, 512, 640, 768, 1280, 1344, 1352, 2888, 3400
ROT = HD // 4


def projection_plan():
    plan = [("ki", 0, [(0, W_KI, HD), (HD, W_KI, HD)])]
    plan += [("qi", j, [(0, W_QI + j * P, P)]) for j in range(4)]
    plan += [("wba", 0, [(0, W_WI, 8), (8, W_BA, 8)])]
    plan += [("k", 0, [(0, W_K, P)]), ("v", 0, [(0, W_V, P)])]
    plan += [("q", j, [(0, W_Q + j * HD, HD), (HD, W_Q + (4 + j) * HD, HD)]) for j in range(4)]
    plan += [("z", j, [(0, W_Z + j * P, P)]) for j in range(4)]
    plan += [("qkv", j, [(0, W_QKV + j * P, P)]) for j in range(QKV_BLOCKS)]
    return plan


def rope_tables():
    half = ROT // 2
    inv = (np.float32(500000.0) ** (-np.arange(half, dtype=np.float32) / np.float32(half))).astype(np.float32)
    pos = np.concatenate([np.arange(PROMPT), np.tile(4096 + np.arange(DEC_T), DEC_B)]).astype(np.float32)
    ang = (pos[None, :] * inv[:, None]).astype(np.float32)
    cos, sin = np.ones((P, NT), np.float32), np.zeros((P, NT), np.float32)
    for r in (0, HD):
        cos[r:r + half] = cos[r + half:r + ROT] = np.cos(ang)
        sin[r:r + half], sin[r + half:r + ROT] = -np.sin(ang), np.sin(ang)
    return cos, sin


ROPE_SWAP = list(range(8, 16)) + list(range(8)) + list(range(16, 32))


def conv_taps(nc, conv_w, state_conv, ident, taps, samp):
    with ExitStack() as ctx:
        sc = Scope(nc, ctx, "taps")
        rows = sc.sb("rows", [CONV_K, 12 * P])
        srows = sc.sb("srows", [24, 12 * P])
        turned = sc.ps("turned", [P, 12, CONV_K])
        sturned = sc.ps("sturned", [P, 12, 24])
        rows_in, turned_done = sc.sem("rows_in"), sc.sem("turned_done")
        block = ctx.enter_context(nc.Block())

        @block.sync
        def _(sp):
            sp.dma_start(rows[:, :], conv_w[0]).then_inc(rows_in, 16)
            sp.dma_start(srows[:, :], state_conv[0].rearrange("b r c -> (b r) c")).then_inc(rows_in, 16)

        @block.tensor
        def _(pe):
            pe.wait_ge(rows_in, 32)
            for j in range(12):
                pe.transpose(turned[:, j, :], rows[:, j * P:(j + 1) * P], ident[0:CONV_K, 0:CONV_K])
                last = pe.transpose(sturned[:, j, :], srows[:, j * P:(j + 1) * P], ident[0:24, 0:24])
            last.then_inc(turned_done, 1)

        @block.vector
        def _(dve):
            dve.wait_ge(turned_done, 1)
            dve.tensor_copy(taps[:, :, :], turned[:, :, :])
            for j in range(12):
                dve.tensor_copy(samp[:, j, :, 0:3], sturned[:, j, :].rearrange("p (b r) -> p b r", b=DEC_B))


def project(nc, w_in, cos_in, sin_in, x_hi, x_lo, taps, samp, k_t, v_t, ki_t, wba_t, qkv_t, conv_tail,
            q_out, qi_out, z_out):
    plan = projection_plan()
    n_blocks = len(plan)
    assert n_blocks % 2 == 0
    with ExitStack() as ctx:
        sc = Scope(nc, ctx, "proj")
        raw = sc.sb("raw", [P, 2, 1024])
        w_hi = sc.sb("w_hi", [P, 2, 1024], F32R)
        w_lo = sc.sb("w_lo", [P, 2, 1024], F32R)
        cos = sc.sb("cos", [P, NT])
        sin = sc.sb("sin", [P, NT])
        copied = sc.sb("copied", [P, 2, TP])
        swapped = sc.sb("swapped", [P, NT])
        stage = sc.sb("stage", [P, 2, TP])
        ps = [sc.ps("ps_a", [P, SLICES, 512]), sc.ps("ps_b", [P, SLICES, 512])]
        raw_in = [sc.sem("raw_in0"), sc.sem("raw_in1")]
        stored = [sc.sem("stored0"), sc.sem("stored1")]
        tables_in, whi_done, wlo_done, filled, evacuated, vector_step, silu_done = (sc.sem(n) for n in (
            "tables_in", "whi_done", "wlo_done", "filled", "evacuated", "vector_step", "silu_done"))
        block = ctx.enter_context(nc.Block())
        arrived, total, vector_steps, steps = [], [0, 0], [], 0
        for n, (kind, _, parts) in enumerate(plan):
            total[n % 2] += 16 * len(parts)
            arrived.append(total[n % 2])
            steps += {"q": 4, "qi": 4, "k": 4, "ki": 4, "qkv": 5}.get(kind, 0)
            vector_steps.append(steps)
        staged = [n for n, (kind, _, _) in enumerate(plan) if kind in ("q", "qi", "z")]

        @block.sync
        def _(sp):
            sp.dma_start(cos[:, :], cos_in).then_inc(tables_in, 16)
            sp.dma_start(sin[:, :], sin_in).then_inc(tables_in, 16)
            for n, (_, _, parts) in enumerate(plan):
                if n >= 2:
                    sp.wait_ge(wlo_done, n - 1)
                for row, col, width in parts:
                    dst = raw[:, n % 2, :].rearrange("p (k f) -> p k f", k=KT)[:, :, row:row + width]
                    src = w_in[0, :, col:col + width].rearrange("(k p) f -> p k f", p=P)
                    sp.dma_start(dst, src).then_inc(raw_in[n % 2], 16)

        @block.gpsimd
        def _(pool):
            for i, n in enumerate(staged):
                kind, j, _ = plan[n]
                if kind == "z":
                    pool.wait_ge(evacuated, n + 1)
                else:
                    pool.wait_ge(vector_step, vector_steps[n])
                out = {"q": q_out, "qi": qi_out, "z": z_out}[kind]
                pool.dma_start(out[j], stage[:, i % 2, 0:NT]).then_inc(stored[i % 2], 16)
            pool.wait_ge(stored[0], 16 * ((len(staged) + 1) // 2))
            pool.wait_ge(stored[1], 16 * (len(staged) // 2))

        @block.tensor
        def _(pe):
            with pe.Fori(0, n_blocks // 2) as i:
                for par in range(2):
                    pe.wait_ge(wlo_done, i * 2 + par + 1)
                    pe.wait_ge(evacuated, i * 2)
                    three_pass(pe, ps[par], lambda k: w_hi[:, par, k * P:(k + 1) * P],
                               lambda k: w_lo[:, par, k * P:(k + 1) * P], lambda k: x_hi[:, k],
                               lambda k: x_lo[:, k], range(KT)).then_inc(filled, 1)

        def whole(buf):
            return buf.rearrange("p (s c) -> p s c", s=SLICES)

        @block.scalar
        def _(act):
            def weight_hi(n):
                act.wait_ge(raw_in[n % 2], arrived[n])
                if n >= 2:
                    act.wait_ge(filled, n - 1)
                if plan[n][0] == "wba":
                    v = lambda b: b[:, n % 2, :].rearrange("p (k f) -> p k f", k=KT)[:, :, 0:16]
                    act.activation(v(w_hi), v(raw), ACT.Copy).then_inc(whi_done, 1)
                else:
                    act.activation(w_hi[:, n % 2, :], raw[:, n % 2, :], ACT.Copy).then_inc(whi_done, 1)

            weight_hi(0)
            weight_hi(1)
            for n, (kind, j, _) in enumerate(plan):
                src = ps[n % 2][:, :, 0:SL]
                act.wait_ge(filled, n + 1)
                if n >= 2 and vector_steps[n - 2]:
                    act.wait_ge(vector_step, vector_steps[n - 2])
                if kind == "wba":
                    act.activation(whole(wba_t[:, :]), ps[n % 2][0:16, :, 0:SL], ACT.Copy).then_inc(evacuated, 1)
                elif kind == "v":
                    act.activation(whole(v_t[:, :]), src, ACT.Copy).then_inc(evacuated, 1)
                elif kind == "z":
                    i = staged.index(n)
                    act.wait_ge(stored[i % 2], 16 * (i // 2))
                    act.activation(whole(stage[:, i % 2, :]), src, ACT.Silu).then_inc(evacuated, 1)
                elif kind == "qkv":
                    act.activation(samp[:, j, :, 3:11],
                                   ps[n % 2][:, 2, PROMPT - 2 * SL:NT - 2 * SL].rearrange("p (b t) -> p b t", b=DEC_B),
                                   ACT.Copy)
                    act.activation(whole(copied[:, n % 2, :]), src, ACT.Copy).then_inc(evacuated, 1)
                else:
                    act.activation(whole(copied[:, n % 2, :]), src, ACT.Copy).then_inc(evacuated, 1)
                if n + 2 < n_blocks:
                    weight_hi(n + 2)
                if kind == "qkv":
                    act.wait_ge(vector_step, vector_steps[n])
                    act.activation(qkv_t[:, j, 0:PROMPT], qkv_t[:, j, 0:PROMPT], ACT.Silu).then_inc(silu_done, 1)

        @block.vector
        def _(dve):
            count = [0]

            def step(ins, wait=True):
                count[0] += 1
                ins.then_inc(vector_step, 1)
                if wait:
                    dve.wait_ge(vector_step, count[0])

            def weight_lo(n):
                dve.wait_ge(whi_done, n + 1)
                if plan[n][0] == "wba":
                    v = lambda b: b[:, n % 2, :].rearrange("p (k f) -> p k f", k=KT)[:, :, 0:16]
                    dve.tensor_tensor(v(w_lo), v(raw), v(w_hi).bitcast(F32), ALU.subtract).then_inc(wlo_done, 1)
                else:
                    dve.tensor_tensor(w_lo[:, n % 2, :], raw[:, n % 2, :], w_hi[:, n % 2, :].bitcast(F32),
                                      ALU.subtract).then_inc(wlo_done, 1)

            weight_lo(0)
            weight_lo(1)
            dve.wait_ge(tables_in, 32)
            for n, (kind, j, _) in enumerate(plan):
                if n + 2 < n_blocks:
                    weight_lo(n + 2)
                if kind in ("v", "wba", "z"):
                    continue
                dve.wait_ge(evacuated, n + 1)
                c = copied[:, n % 2, 0:NT]
                if kind == "qkv":
                    y = qkv_t[:, j, 0:PROMPT]
                    step(dve.tensor_copy(conv_tail[:, j, :], c[:, PROMPT - 3:PROMPT]), wait=False)
                    step(dve.tensor_scalar(y, c[:, 0:PROMPT], taps[:, j, 3:4], None, ALU.mult))
                    for back in (1, 2, 3):
                        step(dve.scalar_tensor_tensor(qkv_t[:, j, back:PROMPT], c[:, 0:PROMPT - back],
                                                      taps[:, j, 3 - back:4 - back], qkv_t[:, j, back:PROMPT],
                                                      ALU.mult, ALU.add))
                    continue
                if kind in ("k", "ki"):
                    dst = {"k": k_t, "ki": ki_t}[kind][:, 0:NT]
                else:
                    i = staged.index(n)
                    dst = stage[:, i % 2, 0:NT]
                    if i >= 2:
                        dve.wait_ge(stored[i % 2], 16 * (i // 2))
                step(dve.stream_shuffle(swapped[:, :], c, ROPE_SWAP), wait=False)
                step(dve.tensor_tensor(dst, c, cos[:, :], ALU.mult))
                step(dve.tensor_tensor(swapped[:, :], swapped[:, :], sin[:, :], ALU.mult))
                step(dve.tensor_tensor(dst, dst, swapped[:, :], ALU.add))


def projection_tail(nc, ident, ones, k_t, v_t, ki_t, wba_t, qkv_t, conv_tail, samp, taps, a_log, dt_bias,
                    v_tok, wi_tok, beta, gate, unit, k_out, v_out, ki_out, conv_out, qkv_out):
    with ExitStack() as ctx:
        sc = Scope(nc, ctx, "tail")
        k_tok = sc.sb("k_tok", [P, TILES, P])
        ki_tok = sc.sb("ki_tok", [P, TILES, HD])
        wba = sc.sb("wba", [P, TILES, 16])
        ab = sc.sb("ab", [P, 2, GH])
        sums = sc.sb("sums", [P, TILES, 8])
        sq = sc.sb("sq", [P, 2, NT])
        acc = sc.sb("acc", [P, 12, DEC_B, DEC_T])
        tmp = sc.sb("tmp", [P, 12, DEC_B, DEC_T])
        g1 = sc.sb("g1", [P, TILES, GH])
        g2 = sc.sb("g2", [P, TILES, GH])
        rows = sc.sb("rows", [27, 12 * P])
        saved = sc.sb("saved", [P, 12, 27])
        turned = sc.ps("turned", [P, 4, 4, P])
        sum_ps = sc.ps("sum_ps", [P, 512])
        wba_ps = sc.ps("wba_ps", [P, 512])
        saved_ps = sc.ps("saved_ps", [27, 2, 512])
        consts_in, turned_done, tok_done, wba_done, squared, summed, vs, act_step, stored, saved_done, rows_done, \
            conv_ready, sums_ready, roots, gate_in, saved_turned = (
                sc.sem(n) for n in ("consts_in", "turned_done", "tok_done", "wba_done", "squared", "summed",
                                    "vector_step", "act_step", "stored", "saved_done", "rows_done", "conv_ready",
                                    "sums_ready", "roots", "gate_in", "saved_turned"))
        block = ctx.enter_context(nc.Block())
        kinds = [(k_t, P, k_tok), (v_t, P, v_tok), (ki_t, HD, ki_tok)]

        @block.sync
        def _(sp):
            sp.dma_start(ab[:, 0, :], a_log.partition_broadcast(P)[:, 0, :]).then_inc(consts_in, 16)
            sp.dma_start(ab[:, 1, :], dt_bias.partition_broadcast(P)[:, 0, :]).then_inc(consts_in, 16)
            sp.wait_ge(tok_done, 3 * 3)
            for tok, (prompt, sample) in ((k_tok, k_out), (v_tok, v_out), (ki_tok, ki_out)):
                sp.dma_start(prompt.rearrange("(t p) f -> p t f", p=P), tok[:, 0:TILES - 1, :]).then_inc(stored, 16)
                sp.dma_start(sample, tok[0:SAMPLE, TILES - 1, :]).then_inc(stored, 16)
            sp.wait_ge(act_step, 1)
            for j in range(12):
                sp.dma_start(qkv_out[:, j, :], qkv_t[:, j, :]).then_inc(stored, 16)
            sp.wait_ge(rows_done, 3)
            sp.dma_start(conv_out[0], rows[0:3, :]).then_inc(stored, 16)
            sp.dma_start(conv_out[1], rows[3:27, :]).then_inc(stored, 16)
            sp.wait_ge(stored, 16 * 20)

        @block.tensor
        def _(pe):
            for t in range(TILES):
                w = tile_width(t)
                last = pe.transpose(wba_ps[0:w, t * 16:(t + 1) * 16], wba_t[:, t * P:t * P + w], ident[0:16, 0:16])
            last.then_inc(wba_done, 1)
            n = 0
            for src, width, _ in kinds:
                for lo in (0, 4, 8):
                    if n >= 4:
                        pe.wait_ge(tok_done, n - 3)
                    for t in range(lo, min(lo + 4, TILES)):
                        w = tile_width(t)
                        last = pe.transpose(turned[0:w, n % 4, t - lo, 0:width], src[0:width, t * P:t * P + w],
                                            ident[0:width, 0:width])
                    last.then_inc(turned_done, 1)
                    n += 1
            for j in range(8):
                pe.wait_ge(squared, j + 1)
                for t in range(TILES):
                    w = tile_width(t)
                    last = pe.matmul(sum_ps[0:w, t * 8 + j:t * 8 + j + 1], sq[:, j % 2, t * P:t * P + w],
                                     ones[:, 0:1], start=True, stop=True)
                last.then_inc(summed, 1)
            for g in range(3):
                pe.wait_ge(saved_done, 1)
                if g == 2:
                    pe.wait_ge(rows_done, 1)
                for j in range(4 * g, 4 * g + 4):
                    last = pe.transpose(saved_ps[:, g % 2, (j % 4) * P:(j % 4 + 1) * P], saved[:, j, :], ident[:, :])
                last.then_inc(saved_turned, 1)

        @block.scalar
        def _(act):
            n = 0
            for _, width, tok in kinds:
                for lo in (0, 4, 8):
                    act.wait_ge(turned_done, n + 1)
                    if lo < 8:
                        act.activation(tok[:, lo:lo + 4, 0:width], turned[:, n % 4, :, 0:width],
                                       ACT.Copy).then_inc(tok_done, 1)
                    else:
                        act.activation(tok[0:SAMPLE, 8, 0:width], turned[0:SAMPLE, n % 4, 0, 0:width],
                                       ACT.Copy).then_inc(tok_done, 1)
                    n += 1
            act.wait_ge(conv_ready, 1)
            act.activation(qkv_t[:, :, PROMPT:NT], acc[:, :, :, :].rearrange("p j b t -> p j (b t)"),
                           ACT.Silu).then_inc(act_step, 1)
            act.wait_ge(act_step, 1)
            for j in range(8):
                if j >= 2:
                    act.wait_ge(summed, j - 1)
                act.activation(sq[:, j % 2, :], qkv_t[:, j, :], ACT.Square).then_inc(squared, 1)
            act.wait_ge(sums_ready, 1)
            act.activation(unit[:, :, :], sums[:, :, :], ACT.Sqrt).then_inc(roots, 1)
            act.wait_ge(consts_in, 32)
            act.wait_ge(gate_in, 1)
            act.activation(ab[:, 0, :], ab[:, 0, :], ACT.Exp)
            act.activation(beta[:, :, :], wba[:, :, 8:12], ACT.Exp, scale=-1.0).then_inc(act_step, 1)
            act.activation(g2[:, :, :], g1[:, :, :], ACT.Abs).then_inc(act_step, 1)
            act.wait_ge(act_step, 3)
            act.activation(g2[:, :, :], g2[:, :, :], ACT.Exp, scale=-1.0).then_inc(act_step, 1)
            act.wait_ge(act_step, 4)
            act.activation(g2[:, :, :], g2[:, :, :], ACT.Ln, bias=1.0).then_inc(act_step, 1)

        @block.vector
        def _(dve):
            count = [0]

            def step(ins, wait=True):
                count[0] += 1
                ins.then_inc(vs, 1)
                if wait:
                    dve.wait_ge(vs, count[0])

            def tap(k):
                return taps[:, :, k:k + 1].unsqueeze(3).to_broadcast([P, 12, DEC_B, DEC_T])

            def heads(v):
                return v.unsqueeze(1).to_broadcast([P, TILES, GH])

            step(dve.memset(wba[:, :, :], 0.0), wait=False)
            step(dve.memset(sums[:, :, :], 1.0), wait=False)
            step(dve.tensor_tensor(acc[:, :, :, :], samp[:, :, :, 3:11], tap(3), ALU.mult))
            for back in (1, 2, 3):
                step(dve.tensor_tensor(tmp[:, :, :, :], samp[:, :, :, 3 - back:11 - back], tap(3 - back), ALU.mult))
                ins = dve.tensor_tensor(acc[:, :, :, :], acc[:, :, :, :], tmp[:, :, :, :], ALU.add)
                if back < 3:
                    step(ins)
                else:
                    ins.then_inc(conv_ready, 1)
            dve.tensor_copy(saved[:, :, 0:3], conv_tail[:, :, :])
            for j in range(12):
                ins = dve.tensor_copy(saved[:, j, 3:27].rearrange("p (b r) -> p b r", b=DEC_B), samp[:, j, :, 8:11])
            ins.then_inc(saved_done, 1)
            dve.wait_ge(wba_done, 1)
            w9 = wba_ps[:, 0:TILES * 16].rearrange("p (t c) -> p t c", t=TILES)
            step(dve.tensor_copy(wba[:, 0:TILES - 1, :], w9[:, 0:TILES - 1, :]), wait=False)
            step(dve.tensor_copy(wba[0:SAMPLE, TILES - 1, :], w9[0:SAMPLE, TILES - 1, :]))
            step(dve.tensor_scalar(wi_tok[:, :, :], wba[:, :, 0:8], 8.0 ** -0.5, None, ALU.mult), wait=False)
            dve.wait_ge(consts_in, 32)
            dve.tensor_tensor(g1[:, :, :], wba[:, :, 12:16], heads(ab[:, 1, :]), ALU.add).then_inc(gate_in, 1)
            dve.wait_ge(summed, 8)
            s9 = sum_ps[:, 0:TILES * 8].rearrange("p (t c) -> p t c", t=TILES)
            step(dve.tensor_scalar(sums[:, 0:TILES - 1, :], s9[:, 0:TILES - 1, :], NORM_EPS, None, ALU.add),
                 wait=False)
            dve.tensor_scalar(sums[0:SAMPLE, TILES - 1, :], s9[0:SAMPLE, TILES - 1, :], NORM_EPS, None,
                              ALU.add).then_inc(sums_ready, 1)
            dve.wait_ge(act_step, 3)
            step(dve.tensor_scalar(beta[:, :, :], beta[:, :, :], 1.0, None, ALU.add))
            step(dve.reciprocal(beta[:, :, :], beta[:, :, :]), wait=False)
            step(dve.tensor_scalar(g1[:, :, :], g1[:, :, :], 0.0, None, ALU.max))
            dve.wait_ge(act_step, 5)
            step(dve.tensor_tensor(g1[:, :, :], g1[:, :, :], g2[:, :, :], ALU.add))
            step(dve.tensor_tensor(g1[:, :, :], g1[:, :, :], heads(ab[:, 0, :]), ALU.mult))
            step(dve.tensor_scalar(gate[:, :, :], g1[:, :, :], -1.0, None, ALU.mult), wait=False)
            for g in range(3):
                dve.wait_ge(saved_turned, g + 1)
                dve.tensor_copy(rows[:, g * 512:(g + 1) * 512], saved_ps[:, g % 2, :]).then_inc(rows_done, 1)
            dve.wait_ge(roots, 1)
            step(dve.reciprocal(unit[:, :, :], unit[:, :, :]))
            step(dve.tensor_scalar(unit[:, :, 0:4], unit[:, :, 0:4], float(P) ** -0.5, None, ALU.mult))


BIG = 1e30
LEVELS = 7


def delta_masks(n, group):
    i, j = np.arange(n)[:, None], np.arange(n)[None, :]
    same = (i // group) == (j // group)
    upper = ((i <= j) & same).astype(np.float32)
    strict = np.where((i > j) & same, 0.0, -BIG).astype(np.float32)
    causal_t = np.where((i <= j) & same, 0.0, -BIG).astype(np.float32)
    levels = [((i // (2 << l) == j // (2 << l)) & (i // (1 << l) % 2 == 1) & (j // (1 << l) % 2 == 0))
              for l in range(int(np.log2(group)))]
    return upper, strict, causal_t, [m.astype(np.float32) for m in levels]


def over_heads(m):
    return m.unsqueeze(1).to_broadcast([m.shape[0], GH, m.shape[1]])


def over_cols(v, n):
    return v.unsqueeze(2).to_broadcast([v.shape[0], v.shape[1], n])


def delta_prompt(nc, ident, ones, masks, qkv_in, beta, gate, unit, state, o_all):
    n_chunks = PROMPT // P
    upper, strict, causal_t, levels = masks
    with ExitStack() as ctx:
        sc = Scope(nc, ctx, "delta")
        cur = sc.sb("cur", [P, 12, P])
        q_n, k_n, q_t, k_t, v_b, m, pt, x, y, tt, r, o1, vn, vs = (sc.sb(n, [P, GH, P]) for n in (
            "q_n", "k_n", "q_t", "k_t", "v_b", "m", "pt", "x", "y", "tt", "r", "o1", "vn", "vs"))
        gu, x1 = vs, vn
        decay = sc.sb("decay", [P, 2, GH, P])
        ml = sc.sb("ml", [P, LEVELS, GH, P])
        sums = sc.sb("sums", [P, 3, GH])
        exps = sc.sb("exps", [P, 3, GH])
        eb = sc.sb("eb", [P, GH])
        b = [sc.ps(f"b{i}", [P, GH, P]) for i in range(8)]
        names = ("staged", "turned", "qk_scaled", "qk_turned", "qk_ready", "gu_ready", "gates_summed", "sums_done",
                 "exps_done", "decay_in", "decay_done", "grams_done", "m_done", "pt_done", "level_ready", "x0_done",
                 "x_turned", "y0_done", "state_read", "t_done", "t_copied", "u_done", "y_upd", "x_upd", "r_done",
                 "o1_done", "v_done", "vn_done", "vs_done", "o2_done", "su_done", "o_done", "state_done", "own")
        s = {n: sc.sem(n) for n in names}
        block = ctx.enter_context(nc.Block())

        @block.sync
        def _(sp):
            with sp.Fori(0, n_chunks) as c:
                sp.wait_ge(s["turned"], c)
                sp.dma_start(cur[:, :, :], qkv_in[:, :, bass.ts(c, P)]).then_inc(s["staged"], 16)

        @block.gpsimd
        def _(pool):
            with pool.Fori(0, n_chunks) as c:
                pool.wait_ge(s["m_done"], c + 1)
                pool.wait_ge(s["u_done"], c * 6)
                for l in range(LEVELS):
                    pool.tensor_tensor(ml[:, l], m[:, :, :], over_heads(levels[l]), ALU.mult
                                       ).then_inc(s["level_ready"], 1)

        @block.tensor
        def _(pe):
            with pe.Fori(0, n_chunks) as c:
                pe.wait_ge(s["staged"], c * 16 + 16)
                pe.wait_ge(s["t_copied"], c * 6)
                pe.wait_ge(s["y_upd"], c * 6)
                pe.wait_ge(s["x_upd"], c * 5)
                for part in range(3):
                    for h in range(GH):
                        last = pe.transpose(b[part][:, h, :], cur[:, part * GH + h, :], ident[:, :])
                last.then_inc(s["turned"], 1)
                pe.wait_ge(s["gu_ready"], c + 1)
                pe.wait_ge(s["vn_done"], c)
                pe.wait_ge(s["state_done"], c)
                pe.matmul(b[3][:, :, :], ones[:, :], gu[:, :, :], start=True, stop=True)
                pe.matmul(b[4][:, 0, 0:GH], upper[:, :], gate[:, c, :], start=True, stop=True)
                pe.matmul(b[4][:, 0, GH:2 * GH], ones[:, :], gate[:, c, :], start=True,
                          stop=True).then_inc(s["gates_summed"], 1)
                pe.wait_ge(s["qk_scaled"], c * 2 + 2)
                for h in range(GH):
                    pe.transpose(b[0][:, h, :], q_n[:, h, :], ident[:, :])
                for h in range(GH):
                    last = pe.transpose(b[1][:, h, :], k_n[:, h, :], ident[:, :])
                last.then_inc(s["qk_turned"], 1)
                pe.wait_ge(s["qk_ready"], c * 2 + 2)
                pe.wait_ge(s["r_done"], c)
                pe.wait_ge(s["o1_done"], c)
                for h in range(GH):
                    pe.matmul(b[5][:, h, :], k_t[:, h, :], k_t[:, h, :], start=True, stop=True)
                for h in range(GH):
                    last = pe.matmul(b[6][:, h, :], k_t[:, h, :], q_t[:, h, :], start=True, stop=True)
                last.then_inc(s["grams_done"], 1)
                pe.wait_ge(s["x0_done"], c + 1)
                for h in range(GH):
                    last = pe.transpose(b[0][:, h, :], x[:, h, :], ident[:, :])
                last.then_inc(s["x_turned"], 1)
                pe.wait_ge(s["m_done"], c + 1)
                pe.wait_ge(s["pt_done"], c + 1)
                for h in range(GH):
                    pe.matmul(b[5][:, h, :], k_t[:, h, :], state[:, h, :], start=True, stop=True)
                for h in range(GH):
                    last = pe.matmul(b[6][:, h, :], q_t[:, h, :], state[:, h, :], start=True, stop=True)
                last.then_inc(s["state_read"], 1)
                for l in range(1, LEVELS):
                    pe.wait_ge(s["level_ready"], c * 7 + l + 1)
                    if l == 1:
                        pe.wait_ge(s["y0_done"], c + 1)
                    else:
                        pe.wait_ge(s["y_upd"], c * 6 + l - 1)
                        pe.wait_ge(s["x_upd"], c * 5 + l - 1)
                    for h in range(GH):
                        last = pe.matmul(b[0][:, h, :], ml[:, l, h, :], y[:, h, :], start=True, stop=True)
                    last.then_inc(s["t_done"], 1)
                    pe.wait_ge(s["t_copied"], c * 6 + l)
                    for h in range(GH):
                        last = pe.matmul(b[1][:, h, :], x[:, h, :], tt[:, h, :], start=True, stop=True)
                    if l < LEVELS - 1:
                        for h in range(GH):
                            last = pe.matmul(b[2][:, h, :], tt[:, h, :], x[:, h, :], start=True, stop=True)
                    last.then_inc(s["u_done"], 1)
                pe.wait_ge(s["y_upd"], c * 6 + 6)
                pe.wait_ge(s["r_done"], c + 1)
                pe.wait_ge(s["decay_in"], c + 1)
                for h in range(GH):
                    last = pe.matmul(b[3][:, h, :], y[:, h, :], r[:, h, :], start=True, stop=True)
                last.then_inc(s["v_done"], 1)
                pe.wait_ge(s["vn_done"], c + 1)
                pe.wait_ge(s["o_done"], c)
                for h in range(GH):
                    last = pe.matmul(b[7][:, h, :], pt[:, h, :], vn[:, h, :], start=True, stop=True)
                last.then_inc(s["o2_done"], 1)
                pe.wait_ge(s["vs_done"], c + 1)
                pe.wait_ge(s["sums_done"], c + 1)
                for h in range(GH):
                    last = pe.matmul(b[4][:, h, :], k_n[:, h, :], vs[:, h, :], start=True, stop=True)
                last.then_inc(s["su_done"], 1)

        @block.scalar
        def _(act):
            with act.Fori(0, n_chunks) as c:
                act.wait_ge(s["sums_done"], c + 1)
                act.activation(exps[:, :, :], sums[:, :, :], ACT.Exp).then_inc(s["exps_done"], 1)
                act.wait_ge(s["qk_turned"], c + 1)
                act.wait_ge(s["state_read"], c)
                act.activation(q_t[:, :, :], b[0][:, :, :], ACT.Copy).then_inc(s["qk_ready"], 1)
                act.activation(k_t[:, :, :], b[1][:, :, :], ACT.Copy).then_inc(s["qk_ready"], 1)
                act.wait_ge(s["decay_in"], c + 1)
                act.activation(decay[:, :, :, :], decay[:, :, :, :], ACT.Exp).then_inc(s["decay_done"], 1)
                act.wait_ge(s["x_turned"], c + 1)
                act.wait_ge(s["v_done"], c)
                act.activation(y[:, :, :], b[0][:, :, :], ACT.Copy).then_inc(s["y0_done"], 1)
                for l in range(1, LEVELS):
                    act.wait_ge(s["t_done"], c * 6 + l)
                    act.wait_ge(s["u_done"], c * 6 + l - 1)
                    act.activation(tt[:, :, :], b[0][:, :, :], ACT.Copy).then_inc(s["t_copied"], 1)
                act.wait_ge(s["v_done"], c + 1)
                act.wait_ge(s["o2_done"], c)
                act.activation(vn[:, :, :], b[3][:, :, :], ACT.Copy).then_inc(s["vn_done"], 1)

        @block.vector
        def _(dve):
            per_chunk = 7
            with dve.Fori(0, n_chunks) as c:
                count = [0]

                def own(ins):
                    count[0] += 1
                    ins.then_inc(s["own"], 1)
                    dve.wait_ge(s["own"], c * per_chunk + count[0])

                dve.wait_ge(s["su_done"], c)
                dve.wait_ge(s["o_done"], c)
                dve.tensor_tensor(gu[:, :, :], over_heads(upper[:, :]), over_cols(gate[:, c, :], P), ALU.mult
                                  ).then_inc(s["gu_ready"], 1)
                dve.wait_ge(s["turned"], c + 1)
                dve.tensor_tensor(q_n[:, :, :], b[0][:, :, :], over_cols(unit[:, c, 0:GH], P), ALU.mult
                                  ).then_inc(s["qk_scaled"], 1)
                dve.tensor_tensor(k_n[:, :, :], b[1][:, :, :], over_cols(unit[:, c, GH:2 * GH], P), ALU.mult
                                  ).then_inc(s["qk_scaled"], 1)
                dve.tensor_tensor(v_b[:, :, :], b[2][:, :, :], over_cols(beta[:, c, :], P), ALU.mult)
                dve.wait_ge(s["gates_summed"], c + 1)
                own(dve.tensor_copy(sums[:, 0:2, :], b[4][:, 0, 0:2 * GH].rearrange("p (a h) -> p a h", a=2)))
                dve.tensor_tensor(sums[:, 2, :], sums[:, 1, :], sums[:, 0, :], ALU.subtract
                                  ).then_inc(s["sums_done"], 1)
                own(dve.tensor_tensor(x1[:, :, :], b[3][:, :, :], over_cols(sums[:, 0, :], P), ALU.subtract))
                dve.tensor_tensor(decay[:, 1], x1[:, :, :], over_heads(causal_t[:, :]), ALU.add)
                dve.scalar_tensor_tensor(decay[:, 0], x1[:, :, :], -1.0, over_heads(strict[:, :]),
                                         ALU.mult, ALU.add).then_inc(s["decay_in"], 1)
                dve.wait_ge(s["exps_done"], c + 1)
                own(dve.tensor_tensor(eb[:, :], exps[:, 0, :], beta[:, c, :], ALU.mult))
                dve.wait_ge(s["grams_done"], c + 1)
                dve.wait_ge(s["decay_done"], c + 1)
                dve.wait_ge(s["level_ready"], c * 7)
                own(dve.tensor_tensor(m[:, :, :], b[5][:, :, :], decay[:, 0], ALU.mult))
                dve.tensor_tensor(m[:, :, :], m[:, :, :], over_cols(beta[:, c, :], P), ALU.mult
                                  ).then_inc(s["m_done"], 1)
                dve.tensor_tensor(pt[:, :, :], b[6][:, :, :], decay[:, 1], ALU.mult).then_inc(s["pt_done"], 1)
                dve.wait_ge(s["level_ready"], c * 7 + 1)
                dve.tensor_tensor(x[:, :, :], over_heads(ident[:, :]), ml[:, 0], ALU.subtract
                                  ).then_inc(s["x0_done"], 1)
                dve.wait_ge(s["state_read"], c + 1)
                own(dve.tensor_tensor(r[:, :, :], b[5][:, :, :], over_cols(eb[:, :], P), ALU.mult))
                dve.tensor_tensor(r[:, :, :], v_b[:, :, :], r[:, :, :], ALU.subtract).then_inc(s["r_done"], 1)
                dve.tensor_tensor(o1[:, :, :], b[6][:, :, :], over_cols(exps[:, 0, :], P), ALU.mult
                                  ).then_inc(s["o1_done"], 1)
                own(dve.tensor_tensor(state[:, :, :], state[:, :, :], over_cols(exps[:, 1, :], P), ALU.mult))
                for l in range(1, LEVELS):
                    if l == 1:
                        dve.wait_ge(s["y0_done"], c + 1)
                        dve.wait_ge(s["x0_done"], c + 1)
                    else:
                        dve.wait_ge(s["y_upd"], c * 6 + l - 1)
                        dve.wait_ge(s["x_upd"], c * 5 + l - 1)
                    dve.wait_ge(s["u_done"], c * 6 + l)
                    dve.tensor_tensor(y[:, :, :], y[:, :, :], b[1][:, :, :], ALU.subtract).then_inc(s["y_upd"], 1)
                    if l < LEVELS - 1:
                        dve.tensor_tensor(x[:, :, :], x[:, :, :], b[2][:, :, :], ALU.subtract
                                          ).then_inc(s["x_upd"], 1)
                dve.wait_ge(s["vn_done"], c + 1)
                dve.tensor_tensor(vs[:, :, :], vn[:, :, :], over_cols(exps[:, 2, :], P), ALU.mult
                                  ).then_inc(s["vs_done"], 1)
                dve.wait_ge(s["o2_done"], c + 1)
                dve.tensor_tensor(o_all[:, c], o1[:, :, :], b[7][:, :, :], ALU.add).then_inc(s["o_done"], 1)
                dve.wait_ge(s["su_done"], c + 1)
                dve.tensor_tensor(state[:, :, :], state[:, :, :], b[4][:, :, :], ALU.add
                                  ).then_inc(s["state_done"], 1)
                assert count[0] <= per_chunk, count
                while count[0] < per_chunk:
                    own(dve.engine_nop())


class Named(dict):

    def __init__(self, sc):
        super().__init__()
        self.sc = sc

    def __missing__(self, name):
        self[name] = self.sc.sem(name)
        return self[name]


def delta_sample(nc, ident, ones, masks, same, member, qkv_in, beta, gate, unit, state_in, state_out, o_all):
    n, t0 = SAMPLE, TILES - 1
    cols = slice(PROMPT, NT)
    upper, strict, causal_t, levels = masks
    with ExitStack() as ctx:
        sc = Scope(nc, ctx, "sdelta")
        state = sc.sb("state", [P, DEC_B, GH, P])
        cur = sc.sb("cur", [P, 12, SAMPLE])
        q_n, k_n, v_b, r, o1, vn, vs = (sc.sb(i, [n, GH, P]) for i in ("q_n", "k_n", "v_b", "r", "o1", "vn", "vs"))
        q_t, k_t, ks_t, qs_t = (sc.sb(i, [P, GH, n]) for i in ("q_t", "k_t", "ks_t", "qs_t"))
        gu, x1, m, pt, x, y, tt = (sc.sb(i, [n, GH, n]) for i in ("gu", "x1", "m", "pt", "x", "y", "tt"))
        gm = sc.sb("gm", [n, DEC_B, GH])
        decay = sc.sb("decay", [n, 2, GH, n])
        ml = sc.sb("ml", [n, 3, GH, n])
        sums, exps = sc.sb("sums", [n, 3, GH]), sc.sb("exps", [n, 3, GH])
        totals = sc.sb("totals", [P, DEC_B * GH])
        eb = sc.sb("eb", [n, GH])
        vsb = sc.sb("vsb", [n, 2, DEC_B, P])
        wide = sc.ps("wide", [P, 2, DEC_B, P])
        b = [wide[:, 0, 0:4, :], wide[:, 0, 4:8, :], wide[:, 1, 0:4, :], wide[:, 1, 4:8, :]] + \
            [sc.ps(f"b{i}", [P, GH, P])[:, :, :] for i in range(4)]
        s = Named(sc)
        block = ctx.enter_context(nc.Block())
        state_rows = state[:, :, :, :].rearrange("p b h v -> p (b h) v")

        @block.sync
        def _(sp):
            sp.dma_start(cur[:, :, :], qkv_in[:, :, cols]).then_inc(s["staged"], 16)
            sp.dma_start(state_rows, state_in.rearrange("b h k v -> k (b h) v")).then_inc(s["state_loaded"], 16)
            sp.wait_ge(s["state_added"], GH)
            sp.dma_start(state_out.rearrange("b h k v -> k (b h) v"), state_rows).then_inc(s["stored"], 16)
            sp.wait_ge(s["stored"], 16)

        @block.tensor
        def _(pe):
            pe.wait_ge(s["staged"], 16)
            for part in range(3):
                for h in range(GH):
                    last = pe.transpose(b[part][0:n, h, :], cur[:, part * GH + h, :], ident[:, :])
            last.then_inc(s["turned"], 1)
            pe.wait_ge(s["gu_ready"], 1)
            pe.matmul(b[3][0:n, :, 0:n], ones[0:n, 0:n], gu[:, :, :], start=True, stop=True)
            pe.matmul(b[4][0:n, 0, 0:GH], upper, gate[0:n, t0, :], start=True, stop=True)
            pe.matmul(b[4][0:n, 0, GH:2 * GH], same, gate[0:n, t0, :], start=True, stop=True)
            pe.matmul(b[4][:, 1, 0:DEC_B * GH], ones[0:n, :], gm[:, :, :].rearrange("p b h -> p (b h)"),
                      start=True, stop=True).then_inc(s["gates_summed"], 1)
            pe.wait_ge(s["scaled"], 3)
            for h in range(GH):
                pe.transpose(b[0][:, h, 0:n], q_n[:, h, :], ident[0:n, 0:n])
            for h in range(GH):
                last = pe.transpose(b[1][:, h, 0:n], k_n[:, h, :], ident[0:n, 0:n])
            last.then_inc(s["qk_turned"], 1)
            pe.wait_ge(s["qk_ready"], 2)
            for h in range(GH):
                pe.matmul(b[5][0:n, h, 0:n], k_t[:, h, :], k_t[:, h, :], start=True, stop=True)
            for h in range(GH):
                last = pe.matmul(b[6][0:n, h, 0:n], k_t[:, h, :], q_t[:, h, :], start=True, stop=True)
            last.then_inc(s["grams_done"], 1)
            pe.wait_ge(s["state_loaded"], 16)
            for i in range(DEC_B):
                ts = slice(i * DEC_T, (i + 1) * DEC_T)
                for h in range(GH):
                    pe.matmul(b[2][:, h, ts], state[:, i, h, :], k_t[:, h, ts], start=True, stop=True)
                    last = pe.matmul(b[7][:, h, ts], state[:, i, h, :], q_t[:, h, ts], start=True, stop=True)
            last.then_inc(s["state_read"], 1)
            pe.wait_ge(s["x0_done"], 1)
            for h in range(GH):
                last = pe.transpose(b[0][0:n, h, 0:n], x[:, h, :], ident[0:n, 0:n])
            last.then_inc(s["x_turned"], 1)
            pe.wait_ge(s["reads_copied"], 2)
            pe.wait_ge(s["pt_done"], 1)
            for h in range(GH):
                pe.transpose(b[5][0:n, h, :], ks_t[:, h, :], ident[:, :])
            for h in range(GH):
                last = pe.transpose(b[6][0:n, h, :], qs_t[:, h, :], ident[:, :])
            last.then_inc(s["reads_turned"], 1)
            pe.wait_ge(s["y0_done"], 1)
            pe.wait_ge(s["sums_done"], 1)
            for l in (1, 2):
                pe.wait_ge(s["level_ready"], l + 1)
                if l == 2:
                    pe.wait_ge(s["xy_upd"], 2)
                for h in range(GH):
                    last = pe.matmul(b[0][0:n, h, 0:n], ml[:, l, h, :], y[:, h, :], start=True, stop=True)
                last.then_inc(s["t_done"], 1)
                pe.wait_ge(s["t_copied"], l)
                for h in range(GH):
                    pe.matmul(b[1][0:n, h, 0:n], x[:, h, :], tt[:, h, :], start=True, stop=True)
                for h in range(GH):
                    last = pe.matmul(b[4][0:n, h, 0:n], tt[:, h, :], x[:, h, :], start=True, stop=True)
                last.then_inc(s["u_done"], 1)
            pe.wait_ge(s["xy_upd"], 4)
            pe.wait_ge(s["r_done"], 1)
            for h in range(GH):
                last = pe.matmul(b[3][0:n, h, :], y[:, h, :], r[:, h, :], start=True, stop=True)
            last.then_inc(s["v_done"], 1)
            pe.wait_ge(s["vn_done"], 1)
            for h in range(GH):
                last = pe.matmul(b[5][0:n, h, :], pt[:, h, :], vn[:, h, :], start=True, stop=True)
            last.then_inc(s["o2_done"], 1)
            for h in range(GH):
                pe.wait_ge(s["masked"], h + 1)
                if h >= 2:
                    pe.wait_ge(s["state_added"], h - 1)
                for half in range(2):
                    last = pe.matmul(wide[:, h % 2, 4 * half:4 * half + 4, :], k_n[:, h, :],
                                     vsb[:, h % 2, 4 * half:4 * half + 4, :], start=True, stop=True)
                last.then_inc(s["su_done"], 1)

        @block.scalar
        def _(act):
            act.wait_ge(s["sums_done"], 1)
            act.activation(exps[:, :, :], sums[:, :, :], ACT.Exp)
            act.activation(totals[:, :], totals[:, :], ACT.Exp).then_inc(s["exps_done"], 1)
            act.wait_ge(s["qk_turned"], 1)
            act.activation(q_t[:, :, :], b[0][:, :, 0:n], ACT.Copy).then_inc(s["qk_ready"], 1)
            act.activation(k_t[:, :, :], b[1][:, :, 0:n], ACT.Copy).then_inc(s["qk_ready"], 1)
            act.wait_ge(s["decay_in"], 1)
            act.activation(decay[:, :, :, :], decay[:, :, :, :], ACT.Exp).then_inc(s["decay_done"], 1)
            act.wait_ge(s["state_read"], 1)
            act.activation(ks_t[:, :, :], b[2][:, :, 0:n], ACT.Copy).then_inc(s["reads_copied"], 1)
            act.activation(qs_t[:, :, :], b[7][:, :, 0:n], ACT.Copy).then_inc(s["reads_copied"], 1)
            act.wait_ge(s["x_turned"], 1)
            act.activation(y[:, :, :], b[0][0:n, :, 0:n], ACT.Copy).then_inc(s["y0_done"], 1)
            for l in (1, 2):
                act.wait_ge(s["t_done"], l)
                if l == 2:
                    act.wait_ge(s["u_done"], 1)
                act.activation(tt[:, :, :], b[0][0:n, :, 0:n], ACT.Copy).then_inc(s["t_copied"], 1)
            act.wait_ge(s["v_done"], 1)
            act.activation(vn[:, :, :], b[3][0:n, :, :], ACT.Copy).then_inc(s["vn_done"], 1)

        @block.vector
        def _(dve):
            count = [0]

            def own(ins):
                count[0] += 1
                ins.then_inc(s["own"], 1)
                dve.wait_ge(s["own"], count[0])

            g = gate[0:n, t0, :]
            own(dve.tensor_tensor(gm[:, :, :], g.unsqueeze(1).to_broadcast([n, DEC_B, GH]), over_cols(member, GH),
                                  ALU.mult))
            dve.tensor_tensor(gu[:, :, :], over_heads(upper), over_cols(g, n), ALU.mult).then_inc(s["gu_ready"], 1)
            dve.wait_ge(s["turned"], 1)
            for dst, src, scale in ((q_n, b[0], unit[0:n, t0, 0:GH]), (k_n, b[1], unit[0:n, t0, GH:2 * GH]),
                                    (v_b, b[2], beta[0:n, t0, :])):
                dve.tensor_tensor(dst[:, :, :], src[0:n], over_cols(scale, P), ALU.mult).then_inc(s["scaled"], 1)
            dve.wait_ge(s["gates_summed"], 1)
            dve.tensor_copy(totals[:, :], b[4][:, 1, 0:DEC_B * GH])
            own(dve.tensor_copy(sums[:, 0:2, :], b[4][0:n, 0, 0:2 * GH].rearrange("p (a h) -> p a h", a=2)))
            dve.tensor_tensor(sums[:, 2, :], sums[:, 1, :], sums[:, 0, :], ALU.subtract).then_inc(s["sums_done"], 1)
            own(dve.tensor_tensor(x1[:, :, :], b[3][0:n, :, 0:n], over_cols(sums[:, 0, :], n), ALU.subtract))
            dve.tensor_tensor(decay[:, 1], x1[:, :, :], over_heads(causal_t), ALU.add)
            dve.scalar_tensor_tensor(decay[:, 0], x1[:, :, :], -1.0, over_heads(strict), ALU.mult, ALU.add
                                     ).then_inc(s["decay_in"], 1)
            dve.wait_ge(s["exps_done"], 1)
            own(dve.tensor_tensor(eb[:, :], exps[:, 0, :], beta[0:n, t0, :], ALU.mult))
            dve.wait_ge(s["grams_done"], 1)
            dve.wait_ge(s["decay_done"], 1)
            own(dve.tensor_tensor(m[:, :, :], b[5][0:n, :, 0:n], decay[:, 0], ALU.mult))
            own(dve.tensor_tensor(m[:, :, :], m[:, :, :], over_cols(beta[0:n, t0, :], n), ALU.mult))
            dve.tensor_tensor(pt[:, :, :], b[6][0:n, :, 0:n], decay[:, 1], ALU.mult).then_inc(s["pt_done"], 1)
            for l in range(3):
                dve.tensor_tensor(ml[:, l], m[:, :, :], over_heads(levels[l]), ALU.mult
                                  ).then_inc(s["level_ready"], 1)
            dve.wait_ge(s["level_ready"], 3)
            dve.tensor_tensor(x[:, :, :], over_heads(ident[0:n, 0:n]), ml[:, 0], ALU.subtract
                              ).then_inc(s["x0_done"], 1)
            dve.wait_ge(s["reads_turned"], 1)
            own(dve.tensor_tensor(r[:, :, :], b[5][0:n], over_cols(eb[:, :], P), ALU.mult))
            dve.tensor_tensor(r[:, :, :], v_b[:, :, :], r[:, :, :], ALU.subtract).then_inc(s["r_done"], 1)
            own(dve.tensor_tensor(o1[:, :, :], b[6][0:n], over_cols(exps[:, 0, :], P), ALU.mult))
            own(dve.tensor_tensor(state_rows, state_rows, over_cols(totals[:, :], P), ALU.mult))
            for l in (1, 2):
                dve.wait_ge(s["u_done"], l)
                dve.tensor_tensor(y[:, :, :], y[:, :, :], b[1][0:n, :, 0:n], ALU.subtract).then_inc(s["xy_upd"], 1)
                dve.tensor_tensor(x[:, :, :], x[:, :, :], b[4][0:n, :, 0:n], ALU.subtract).then_inc(s["xy_upd"], 1)
                dve.wait_ge(s["xy_upd"], 2 * l)
            dve.wait_ge(s["vn_done"], 1)
            own(dve.tensor_tensor(vs[:, :, :], vn[:, :, :], over_cols(exps[:, 2, :], P), ALU.mult))
            dve.wait_ge(s["o2_done"], 1)
            dve.tensor_tensor(o_all[0:n, t0], o1[:, :, :], b[5][0:n], ALU.add)
            for h in range(GH + 2):
                if h < GH:
                    if h >= 2:
                        dve.wait_ge(s["su_done"], h - 1)
                    dve.tensor_tensor(vsb[:, h % 2], vs[:, h, :].unsqueeze(1).to_broadcast([n, DEC_B, P]),
                                      over_cols(member, P), ALU.mult).then_inc(s["masked"], 1)
                if h >= 1 and h - 1 < GH:
                    g_ = h - 1
                    dve.wait_ge(s["su_done"], g_ + 1)
                    dve.tensor_tensor(state[:, :, g_, :], state[:, :, g_, :], wide[:, g_ % 2], ALU.add
                                      ).then_inc(s["state_added"], 1)


def delta_finish(nc, ident, norm_w, z_in, o_all, mix_hi, mix_lo):
    with ExitStack() as ctx:
        sc = Scope(nc, ctx, "fin")
        sq = sc.sb("sq", [P, 2, GH, P])
        ms = sc.sb("ms", [P, TILES, GH])
        nw = sc.sb("nw", [P, 1])
        z = sc.sb("z", [P, GH, TP])
        b = sc.ps("turned", [P, 4, GH, P])
        s = Named(sc)
        block = ctx.enter_context(nc.Block())

        @block.sync
        def _(sp):
            with nc.allow_non_contiguous_dma(reason="128 weights"):
                sp.dma_start(nw[:, :], norm_w.rearrange("o p -> p o")).then_inc(s["nw_in"], 16)
            for h in range(GH):
                sp.dma_start(z[:, h, 0:NT], z_in[h]).then_inc(s["z_in"], 16)

        @block.scalar
        def _(act):
            act.wait_ge(s["means"], 1)
            act.activation(ms[:, :, :], ms[:, :, :], ACT.Sqrt).then_inc(s["roots"], 1)
            for h in range(GH):
                act.wait_ge(s["gated"], TILES)
                act.activation(mix_hi[:, GH + h, :], z[:, h, :], ACT.Copy).then_inc(s["hi_done"], 1)

        @block.tensor
        def _(pe):
            for t in range(TILES):
                w = tile_width(t)
                pe.wait_ge(s["scaled"], t + 1)
                if t >= 4:
                    pe.wait_ge(s["gated"], t - 3)
                for h in range(GH):
                    last = pe.transpose(b[:, t % 4, h, 0:w], o_all[0:w, t, h, :], ident[0:w, 0:w])
                last.then_inc(s["turned"], 1)

        @block.vector
        def _(dve):
            count = [0]

            def own(ins):
                count[0] += 1
                ins.then_inc(s["own"], 1)
                dve.wait_ge(s["own"], count[0])

            own(dve.memset(o_all[SAMPLE:P, TILES - 1], 1.0))
            own(dve.memset(z[:, :, NT:TP], 0.0))
            for t in range(TILES):
                own(dve.tensor_tensor(sq[:, t % 2], o_all[:, t], o_all[:, t], ALU.mult))
                own(dve.tensor_reduce(ms[:, t, :], sq[:, t % 2], AX.X, ALU.add))
            dve.tensor_scalar(ms[:, :, :], ms[:, :, :], 1.0 / P, NORM_EPS, ALU.mult, ALU.add).then_inc(s["means"], 1)
            dve.wait_ge(s["roots"], 1)
            own(dve.reciprocal(ms[:, :, :], ms[:, :, :]))
            dve.wait_ge(s["nw_in"], 16)
            dve.wait_ge(s["z_in"], 16 * GH)
            for t in range(TILES + 1):
                if t < TILES:
                    dve.tensor_tensor(o_all[:, t], o_all[:, t], over_cols(ms[:, t, :], P), ALU.mult
                                      ).then_inc(s["scaled"], 1)
                if t >= 1:
                    u, w = t - 1, tile_width(t - 1)
                    dve.wait_ge(s["turned"], t)
                    zt = z[:, :, u * P:u * P + w]
                    dve.scalar_tensor_tensor(zt, b[:, u % 4, :, 0:w], nw[:, 0:1], zt, ALU.mult, ALU.mult
                                             ).then_inc(s["gated"], 1)
            for h in range(GH):
                dve.wait_ge(s["hi_done"], h + 1)
                dve.tensor_tensor(mix_lo[:, GH + h, :], z[:, h, :], mix_hi[:, GH + h, :].bitcast(F32),
                                  ALU.subtract)


TOPK = 256
PAST = 4096
PAGES = 32
N_POOL = 320
KEYS = PAST + DEC_T
LOWEST = -3e38
TOP_TILES = list(range(2, TILES - 1))
WIDTHS = [(t + 1) * P for t in TOP_TILES]
STARTS = [sum(WIDTHS[:i]) for i in range(len(WIDTHS))]


def index_prompt(nc, q_in, ki_t, wi_tok, causal, qi, scores):
    with ExitStack() as ctx:
        sc = Scope(nc, ctx, "ixp")
        rel = sc.sb("rel", [P, 3, PROMPT])
        ps = sc.ps("ps", [P, 3, PROMPT])
        s = Named(sc)
        block = ctx.enter_context(nc.Block())
        work = [(t, h) for t in TOP_TILES for h in range(8)]

        @block.sync
        def _(sp):
            for j in range(4):
                sp.dma_start(qi[:, j, :], q_in[j]).then_inc(s["qi_in"], 16)

        @block.tensor
        def _(pe):
            pe.wait_ge(s["qi_in"], 64)
            for n, (t, h) in enumerate(work):
                rows = slice(h % 2 * HD, h % 2 * HD + HD)
                if n >= 3:
                    pe.wait_ge(s["rectified"], n - 2)
                for lo in range(0, (t + 1) * P, 512):
                    hi = min(lo + 512, (t + 1) * P)
                    last = pe.matmul(ps[:, n % 3, lo:hi], qi[rows, h // 2, t * P:(t + 1) * P], ki_t[rows, lo:hi],
                                     start=True, stop=True)
                last.then_inc(s["dotted"], 1)

        @block.scalar
        def _(act):
            for n, (t, h) in enumerate(work):
                act.wait_ge(s["dotted"], n + 1)
                if n >= 3:
                    act.wait_ge(s["summed"], n - 2)
                act.activation(rel[:, n % 3, 0:(t + 1) * P], ps[:, n % 3, 0:(t + 1) * P], ACT.Relu,
                               scale=HD ** -0.5).then_inc(s["rectified"], 1)

        @block.vector
        def _(dve):
            for n, (t, h) in enumerate(work):
                w = (t + 1) * P
                out = scores[:, STARTS[t - 2]:STARTS[t - 2] + w]
                dve.wait_ge(s["rectified"], n + 1)
                if h == 0:
                    dve.tensor_scalar(out, rel[:, n % 3, 0:w], wi_tok[:, t, 0:1], None, ALU.mult
                                      ).then_inc(s["summed"], 1)
                else:
                    dve.wait_ge(s["summed"], n)
                    dve.scalar_tensor_tensor(out, rel[:, n % 3, 0:w], wi_tok[:, t, h:h + 1], out,
                                             ALU.mult, ALU.add).then_inc(s["summed"], 1)
                if h == 7:
                    dve.wait_ge(s["summed"], n + 1)
                    diag = scores[:, STARTS[t - 2] + t * P:STARTS[t - 2] + w]
                    dve.tensor_tensor(diag, diag, causal, ALU.add)


def own_chain(eng, s, name):
    count = [0]

    def own(ins):
        count[0] += 1
        ins.then_inc(s[name], 1)
        eng.wait_ge(s[name], count[0])

    return own


def sample_tables():
    bt, row = np.arange(SAMPLE), np.arange(P)
    sel = np.stack([((bt[:, None] // DEC_T == 2 * p + row[None, :] // SAMPLE) &
                     (bt[:, None] % DEC_T == row[None, :] % DEC_T)) for p in range(4)], 1).astype(np.float32)
    head_of = (row[:, None] // DEC_T % 8 == np.arange(8)[None, :]).astype(np.float32)
    later = np.where(np.arange(DEC_T)[None, :] > bt[:, None] % DEC_T, LOWEST, 0.0).astype(np.float32)
    return sel, np.ascontiguousarray(sel.transpose(2, 1, 0)), head_of, later


def load_page(eng, cache, pages, slot, dst, sem):
    page = eng.value_load(pages[0:1, bass.ds(slot, 1)], min_val=0, max_val=N_POOL - 1)
    eng.dma_start(dst, cache[0, bass.ds(page, 1)].rearrange("o p ... -> (o p) ...")).then_inc(sem, 16)


def index_sample(nc, ident, cache_kidx, qi, ki_t, wi_tok, sel, sel_t, head_of, later, pages, scores):
    pairs, chunks = DEC_B // 2, PAGES // 4
    with ExitStack() as ctx:
        sc = Scope(nc, ctx, "ixs")
        raw = sc.sb("raw", [P, pairs, 4, P])
        kt = sc.sb("kt", [P, 2, 512])
        rel = sc.sb("rel", [P, 2, 512])
        qd = sc.sb("qd", [P, pairs, 2, 8, DEC_T])
        kn = sc.sb("kn", [P, pairs, DEC_T])
        wpick = sc.sb("wpick", [P, pairs, 8])
        wcol = sc.sb("wcol", [P, pairs])
        wsel = sc.sb("wsel", [P, pairs, SAMPLE])
        turned = sc.ps("turned", [P, 2, 512])
        dots = sc.ps("dots", [P, 2, 512])
        total = sc.ps("total", [P, 512])
        small = sc.ps("small", [P, pairs, 8])
        s = Named(sc)
        block = ctx.enter_context(nc.Block())

        def loads(eng, b2, c):
            for p in range(pairs):
                if c is not None:
                    eng.wait_ge(s["turned"], c * pairs + p - pairs + 1)
                for g in range(4):
                    load_page(eng, cache_kidx, pages, (p * 2 + b2) * PAGES + (0 if c is None else c * 4) + g,
                              raw[:, p, g, b2 * HD:(b2 + 1) * HD], s[f"raw_in{b2}{p}"])

        @block.sync
        def _(sp):
            loads(sp, 0, None)
            with sp.Fori(1, chunks) as c:
                loads(sp, 0, c)

        @block.gpsimd
        def _(pool):
            loads(pool, 1, None)
            with pool.Fori(1, chunks) as c:
                loads(pool, 1, c)

        @block.tensor
        def _(pe):
            for p in range(pairs):
                last = pe.matmul(small[:, p, :], sel[:, p, :], wi_tok[0:SAMPLE, TILES - 1, :], start=True, stop=True)
            last.then_inc(s["picked"], 1)
            pe.wait_ge(s["tables_made"], 1)

            def weigh(n, p):
                pe.wait_ge(s["rectified"], n + 1)
                pe.matmul(total[0:SAMPLE, :], wsel[:, p, :], rel[:, p % 2, :], start=p == 0, stop=p == pairs - 1
                          ).then_inc(s["weighed"], 1)

            with pe.Fori(0, chunks) as c:
                for p in range(pairs):
                    n = c * pairs + p
                    pe.wait_ge(s[f"raw_in0{p}"], c * 64 + 64)
                    pe.wait_ge(s[f"raw_in1{p}"], c * 64 + 64)
                    if p >= 2:
                        pe.wait_ge(s["kt_copied"], n - 1)
                    else:
                        pe.wait_ge(s["kt_copied"], c * pairs)
                    for g in range(4):
                        last = pe.transpose(turned[:, p % 2, g * P:(g + 1) * P], raw[:, p, g, :], ident)
                    last.then_inc(s["turned"], 1)
                    if p >= 1:
                        if p == 1:
                            pe.wait_ge(s["total_copied"], c)
                        weigh(n - 1, p - 1)
                    pe.wait_ge(s["kt_copied"], n + 1)
                    pe.matmul(dots[:, p % 2, :], qd[:, p, :, :, :].rearrange("p b h t -> p (b h t)"), kt[:, p % 2, :],
                              start=True, stop=True).then_inc(s["dotted"], 1)
                weigh(c * pairs + pairs - 1, pairs - 1)
            for p in range(pairs):
                last = pe.matmul(dots[:, 0, p * DEC_T:(p + 1) * DEC_T],
                                 qd[:, p, :, :, :].rearrange("p b h t -> p (b h t)"), kn[:, p, :],
                                 start=True, stop=True)
            last.then_inc(s["new_dotted"], 1)
            pe.wait_ge(s["new_rectified"], 1)
            pe.wait_ge(s["total_copied"], chunks)
            for p in range(pairs):
                last = pe.matmul(total[0:SAMPLE, 0:DEC_T], wsel[:, p, :], rel[:, 0, p * DEC_T:(p + 1) * DEC_T],
                                 start=p == 0, stop=p == pairs - 1)
            last.then_inc(s["new_weighed"], 1)

        @block.scalar
        def _(act):
            with act.Fori(0, chunks) as c:
                for p in range(pairs):
                    n = c * pairs + p
                    act.wait_ge(s["dotted"], n + 1)
                    act.wait_ge(s["weighed"], n - 1 if p >= 2 else c * pairs)
                    act.activation(rel[:, p % 2, :], dots[:, p % 2, :], ACT.Relu, scale=HD ** -0.5
                                   ).then_inc(s["rectified"], 1)
            act.wait_ge(s["new_dotted"], 1)
            act.wait_ge(s["weighed"], chunks * pairs)
            act.activation(rel[:, 0, 0:pairs * DEC_T], dots[:, 0, 0:pairs * DEC_T], ACT.Relu, scale=HD ** -0.5
                           ).then_inc(s["new_rectified"], 1)

        @block.vector
        def _(dve):
            own = own_chain(dve, s, "own")
            own(dve.memset(qd[:, :, :, :, :], 0.0))
            for b2 in range(2):
                rows = slice(b2 * HD, (b2 + 1) * HD)
                q8 = qi[:, :, PROMPT:NT].rearrange("d j (p b t) -> d j p b t", p=pairs, b=2)
                for hp in range(2):
                    for p in range(pairs):
                        dst = qd[rows, p, b2, :, :].rearrange("d (j e) t -> d j e t", e=2)[:, :, hp, :]
                        dve.tensor_copy(dst, q8[hp * HD:(hp + 1) * HD, :, p, b2, :])
                k8 = ki_t[:, PROMPT:NT].rearrange("d (p b t) -> d p b t", p=pairs, b=2)
                dve.tensor_copy(kn[rows, :, :], k8[rows, :, b2, :])
            dve.wait_ge(s["picked"], 1)
            own(dve.tensor_tensor(wpick[:, :, :], small[:, :, :], head_of.unsqueeze(1).to_broadcast([P, pairs, 8]),
                                  ALU.mult))
            own(dve.tensor_reduce(wcol[:, :], wpick[:, :, :], AX.X, ALU.add))
            dve.tensor_tensor(wsel[:, :, :], sel_t, over_cols(wcol[:, :], SAMPLE), ALU.mult
                              ).then_inc(s["tables_made"], 1)
            with dve.Fori(0, chunks) as c:
                for p in range(pairs):
                    n = c * pairs + p
                    dve.wait_ge(s["turned"], n + 1)
                    dve.wait_ge(s["dotted"], n - 1 if p >= 2 else c * pairs)
                    dve.tensor_copy(kt[:, p % 2, :], turned[:, p % 2, :]).then_inc(s["kt_copied"], 1)
                dve.wait_ge(s["weighed"], c * pairs + pairs)
                dve.tensor_copy(scores[:, bass.ts(c, 512)], total[0:SAMPLE, :]).then_inc(s["total_copied"], 1)
            dve.wait_ge(s["new_weighed"], 1)
            dve.tensor_tensor(scores[:, PAST:KEYS], total[0:SAMPLE, 0:DEC_T], later, ALU.add)


TOP_BITS = 31


def top_items():
    return [(i, w, "dve") for i, w in enumerate(WIDTHS)] + [(-1, KEYS, "act")]


def top_tables():
    cols = []
    for _, w, eng in top_items():
        a = eng == "act"
        cols.append([w - TOPK + 1, 2 * TOPK - 1 - w, 2 if a else 1, -w if a else 0])
    table = np.broadcast_to(np.array(cols, np.float32).T[None], (P, 4, len(cols)))
    ints = [1 << b for b in reversed(range(TOP_BITS))] + [-1 << 31 if eng == "act" else 0 for _, _, eng in top_items()]
    bits = np.broadcast_to(np.array(ints, np.int32)[None], (P, len(ints)))
    return np.ascontiguousarray(table), np.ascontiguousarray(bits)


def top_keys(nc, table, bits, scores_p, scores_s, bias_p, bias_s):
    items = top_items()
    n = len(items)
    with ExitStack() as ctx:
        sc = Scope(nc, ctx, "top")
        equal = sc.sb("equal", [P, KEYS], BF16)
        rank = sc.sb("rank", [P, KEYS])
        found, cand, hit, low, high = (sc.sb(i, [P, n], I32) for i in ("found", "cand", "hit", "low", "high"))
        count, sign, limit, exact, thr, above, need = (
            sc.sb(i, [P, n]) for i in ("count", "sign", "limit", "exact", "thr", "above", "need"))
        s = Named(sc)
        block = ctx.enter_context(nc.Block())

        def rows(i):
            return slice(0, P) if items[i][0] >= 0 else slice(0, SAMPLE)

        def score(i):
            t, w, _ = items[i]
            return scores_p[:, STARTS[t]:STARTS[t] + w] if t >= 0 else scores_s[:, :]

        def bias(i):
            t, w, _ = items[i]
            return bias_p[:, STARTS[t]:STARTS[t] + w] if t >= 0 else bias_s[:, :]

        of_act = [i for i in range(n) if items[i][2] == "act"]

        @block.scalar
        def _(act):
            with act.Fori(0, TOP_BITS) as bit:
                act.wait_ge(s["cand_made"], bit + 1)
                for i in of_act:
                    ins = act.activation(bias(i), score(i), ACT.Sign,
                                         bias=cand[rows(i), i:i + 1].bitcast(F32), accum_out=count[rows(i), i:i + 1])
                ins.then_inc(s["act_counted"], 1)
            for i in range(n):
                act.wait_ge(s["chosen"], i + 1)
                act.activation(bias(i), score(i), ACT.Copy, scale=BIG, bias=-BIG)

        @block.vector
        def _(dve):
            own = own_chain(dve, s, "own")

            def count_all(which, level, op, into=None):
                into = count if into is None else into
                for i in which:
                    r = rows(i)
                    ins = dve.tensor_scalar(bias(i), score(i), level(r, i), 0.0, op, ALU.add,
                                            accum_out=into[r, i:i + 1])
                return ins

            for t in (count, above):
                dve.memset(t[:, :], 0.0)
            own(dve.tensor_copy(found[:, :], bits[:, TOP_BITS:TOP_BITS + n]))
            own(count_all(range(n), lambda r, i: 0.0, ALU.is_ge))
            own(dve.tensor_scalar(sign[:, :], count[:, :], float(TOPK), None, ALU.is_ge))
            own(dve.tensor_tensor(exact[:, :], sign[:, :], table[:, 1, :], ALU.mult))
            own(dve.tensor_tensor(exact[:, :], exact[:, :], table[:, 0, :], ALU.add))
            own(dve.tensor_scalar(sign[:, :], sign[:, :], 2.0, -1.0, ALU.mult, ALU.add))
            own(dve.tensor_tensor(limit[:, :], exact[:, :], table[:, 2, :], ALU.mult))
            own(dve.tensor_tensor(limit[:, :], limit[:, :], table[:, 3, :], ALU.add))
            for i in range(n):
                ins = dve.tensor_scalar(score(i), score(i), sign[rows(i), i:i + 1], None, ALU.mult)
            own(ins)
            dve.wait_ge(s["own"], 9)
            with dve.Fori(0, TOP_BITS) as bit:
                this_bit = bits[:, bass.ds(bit, 1)].to_broadcast([P, n])
                dve.tensor_tensor(cand[:, :], found[:, :], this_bit, ALU.bitwise_or).then_inc(s["cand_made"], 1)
                dve.wait_ge(s["cand_made"], bit + 1)
                count_all([i for i in range(n) if i not in of_act],
                          lambda r, i: cand[r, i:i + 1].bitcast(F32), ALU.is_ge).then_inc(s["loop_step"], 1)
                dve.wait_ge(s["loop_step"], bit * 4 + 1)
                dve.wait_ge(s["act_counted"], bit + 1)
                dve.tensor_tensor(hit[:, :], count[:, :], limit[:, :], ALU.is_ge).then_inc(s["loop_step"], 1)
                dve.wait_ge(s["loop_step"], bit * 4 + 2)
                dve.tensor_tensor(hit[:, :], hit[:, :], this_bit, ALU.mult).then_inc(s["loop_step"], 1)
                dve.wait_ge(s["loop_step"], bit * 4 + 3)
                dve.tensor_tensor(found[:, :], found[:, :], hit[:, :], ALU.bitwise_or).then_inc(s["loop_step"], 1)
                dve.wait_ge(s["loop_step"], bit * 4 + 4)
            own(dve.tensor_scalar(found[:, :], found[:, :], 0x7FFFFFFF, None, ALU.bitwise_and))
            own(dve.tensor_scalar(low[:, :], found[:, :], 0xFFFFF, None, ALU.bitwise_and))
            own(dve.tensor_scalar(high[:, :], found[:, :], 0x7FF00000, None, ALU.bitwise_and))
            own(dve.tensor_scalar(low[:, :], low[:, :], 1, None, ALU.add))
            own(dve.tensor_scalar(hit[:, :], low[:, :], 0x100000, None, ALU.bitwise_and))
            own(dve.tensor_tensor(high[:, :], high[:, :], hit[:, :], ALU.add))
            own(dve.tensor_scalar(low[:, :], low[:, :], 0xFFFFF, None, ALU.bitwise_and))
            own(dve.tensor_tensor(cand[:, :], high[:, :], low[:, :], ALU.bitwise_or))
            own(count_all(range(n), lambda r, i: cand[r, i:i + 1].bitcast(F32), ALU.is_ge))
            own(dve.tensor_tensor(hit[:, :], count[:, :], exact[:, :], ALU.is_ge))
            own(dve.copy_predicated(found[:, :], hit[:, :], cand[:, :]))
            own(dve.tensor_tensor(thr[:, :], found[:, :].bitcast(F32), sign[:, :], ALU.mult))
            for i in range(n):
                ins = dve.tensor_scalar(score(i), score(i), sign[rows(i), i:i + 1], None, ALU.mult)
            own(ins)
            own(count_all(range(n), lambda r, i: thr[r, i:i + 1], ALU.is_gt, above))
            own(dve.tensor_scalar(need[:, :], above[:, :], -1.0, float(TOPK), ALU.mult, ALU.add))
            for i in range(n):
                r, w = rows(i), items[i][1]
                eq, rk = equal[r, 0:w], rank[r, 0:w]
                own(dve.tensor_scalar(eq, score(i), thr[r, i:i + 1], None, ALU.is_equal))
                own(dve.tensor_tensor_scan(rk, eq, eq, 0.0, ALU.add, ALU.max))
                own(dve.scalar_tensor_tensor(rk, rk, need[r, i:i + 1], eq, ALU.is_le, ALU.mult))
                dve.scalar_tensor_tensor(score(i), score(i), thr[r, i:i + 1], rk, ALU.is_gt, ALU.add
                                         ).then_inc(s["chosen"], 1)
                dve.wait_ge(s["chosen"], i + 1)


def attend_prompt(nc, ident, ident_bf, causal_bf, q_in, k_t, v_tok, bias_p, mix_hi, mix_lo):
    tiles = TILES - 1
    work = [(t, h) for t in range(tiles) for h in range(8)]
    groups = [(t + 4) // 4 for t, _ in work]
    before = [sum(groups[:n]) for n in range(len(work) + 1)]
    with ExitStack() as ctx:
        sc = Scope(nc, ctx, "att")
        q = sc.sb("q", [P, 4, NT])
        probs = sc.sb("probs", [P, 2, PROMPT])
        probs_t = sc.sb("probs_t", [P, 2, 8, P])
        top, low = sc.sb("top", [P, 2]), sc.sb("low", [P, 2])
        sums = sc.sb("sums", [P, 2, 8])
        out = sc.sb("out", [P, 2, 8, HD])
        dots = sc.ps("dots", [P, 2, PROMPT])
        turned = sc.ps("turned", [P, 2, 4, P])
        values = sc.ps("values", [P, 8, HD])
        out_t = sc.ps("out_t", [P, 4, P])
        s = Named(sc)
        block = ctx.enter_context(nc.Block())

        @block.sync
        def _(sp):
            for j in range(4):
                sp.dma_start(q[:, j, :], q_in[j]).then_inc(s["q_in"], 16)

        @block.tensor
        def _(pe):
            pe.wait_ge(s["q_in"], 64)

            def dot(n):
                t, h = work[n]
                rows, w = slice(h // 4 * HD, h // 4 * HD + HD), (t + 1) * P
                if n >= 2:
                    pe.wait_ge(s["exps_done"], n - 1)
                for lo in range(0, w, 512):
                    hi = min(lo + 512, w)
                    cut = t > 1 or hi == w
                    last = pe.matmul(dots[:, n % 2, lo:hi], q[rows, h % 4, t * P:(t + 1) * P], k_t[rows, lo:hi],
                                     start=True, stop=not cut)
                    if t > 1:
                        start = STARTS[t - 2]
                        last = pe.matmul(dots[:, n % 2, lo:hi], ident_bf, bias_p[:, start + lo:start + hi],
                                         start=False, stop=True)
                    elif cut:
                        last = pe.matmul(dots[:, n % 2, w - P:w], ident_bf, causal_bf, start=False, stop=True)
                last.then_inc(s["dotted"], 1)

            def turn(n):
                t, _ = work[n]
                pe.wait_ge(s["exps_done"], n + 1)
                for g in range(groups[n]):
                    i = before[n] + g
                    if i >= 2:
                        pe.wait_ge(s["turned_copied"], i - 1)
                    for kb in range(4 * g, min(4 * g + 4, t + 1)):
                        last = pe.transpose(turned[:, i % 2, kb % 4, :], probs[:, n % 2, kb * P:(kb + 1) * P], ident)
                    last.then_inc(s["turned"], 1)

            def weigh(n):
                t, h = work[n]
                pe.wait_ge(s["turned_copied"], before[n + 1])
                if h == 0 and t > 0:
                    pe.wait_ge(s["scaled"], t)
                for kb in range(t + 1):
                    last = pe.matmul(values[:, h, :], probs_t[:, n % 2, kb, :],
                                     v_tok[:, kb, h // 4 * HD:h // 4 * HD + HD], start=kb == 0, stop=kb == t)
                last.then_inc(s["weighed"], 1)

            def turn_out(t):
                pe.wait_ge(s["scaled"], t + 1)
                if t > 0:
                    pe.wait_ge(s["lo_done"], t)
                for j in range(4):
                    last = pe.transpose(out_t[:, j, :], out[:, t % 2, 2 * j:2 * j + 2, :].rearrange("p h d -> p (h d)"),
                                        ident)
                last.then_inc(s["out_turned"], 1)

            dot(0)
            for n, (t, h) in enumerate(work):
                if n + 1 < len(work):
                    dot(n + 1)
                if n >= 1:
                    weigh(n - 1)
                if h == 1 and t > 0:
                    turn_out(t - 1)
                turn(n)
            weigh(len(work) - 1)
            turn_out(tiles - 1)

        @block.scalar
        def _(act):
            def hi(t):
                act.wait_ge(s["out_turned"], t + 1)
                act.activation(mix_hi[:, 0:4, t * P:(t + 1) * P], out_t[:, :, :], ACT.Copy).then_inc(s["hi_done"], 1)

            for n, (t, h) in enumerate(work):
                act.wait_ge(s["max_done"], n + 1)
                if n >= 2:
                    act.wait_ge(s["turned"], before[n - 1])
                if h == 0 and t >= 2:
                    act.wait_ge(s["scaled"], t - 1)
                act.activation(probs[:, n % 2, 0:(t + 1) * P], dots[:, n % 2, 0:(t + 1) * P], ACT.Exp,
                               scale=HD ** -0.5, bias=low[:, n % 2:n % 2 + 1], accum_out=sums[:, t % 2, h:h + 1]
                               ).then_inc(s["exps_done"], 1)
                if h == 3 and t > 0:
                    hi(t - 1)
            hi(tiles - 1)

        @block.vector
        def _(dve):
            own = own_chain(dve, s, "own")

            def low_part(t):
                dve.wait_ge(s["hi_done"], t + 1)
                cols = slice(t * P, (t + 1) * P)
                dve.tensor_tensor(mix_lo[:, 0:4, cols], out_t[:, :, :], mix_hi[:, 0:4, cols].bitcast(F32),
                                  ALU.subtract).then_inc(s["lo_done"], 1)

            def scale(t):
                dve.wait_ge(s["weighed"], t * 8 + 8)
                own(dve.reciprocal(sums[:, t % 2, :], sums[:, t % 2, :]))
                if t >= 2:
                    dve.wait_ge(s["out_turned"], t - 1)
                dve.tensor_tensor(out[:, t % 2], values[:, :, :], over_cols(sums[:, t % 2, :], HD), ALU.mult
                                  ).then_inc(s["scaled"], 1)

            def maximum(n):
                t, _ = work[n]
                dve.wait_ge(s["dotted"], n + 1)
                own(dve.tensor_reduce(top[:, n % 2:n % 2 + 1], dots[:, n % 2, 0:(t + 1) * P], AX.X, ALU.max))
                dve.tensor_scalar(low[:, n % 2:n % 2 + 1], top[:, n % 2:n % 2 + 1], -(HD ** -0.5), None, ALU.mult
                                  ).then_inc(s["max_done"], 1)

            def copy(n):
                t, _ = work[n]
                if n >= 2:
                    dve.wait_ge(s["weighed"], n - 1)
                for g in range(groups[n]):
                    i, kbs = before[n] + g, slice(4 * g, min(4 * g + 4, t + 1))
                    dve.wait_ge(s["turned"], i + 1)
                    dve.tensor_copy(probs_t[:, n % 2, kbs, :], turned[:, i % 2, 0:kbs.stop - kbs.start, :]
                                    ).then_inc(s["turned_copied"], 1)

            maximum(0)
            for n, (t, h) in enumerate(work):
                if n + 1 < len(work):
                    if n >= 1:
                        dve.wait_ge(s["exps_done"], n)
                    maximum(n + 1)
                if h == 0 and t > 0:
                    scale(t - 1)
                if h == 4 and t > 0:
                    low_part(t - 1)
                copy(n)
            scale(tiles - 1)
            low_part(tiles - 1)


def attend_sample(nc, ident, cache_k, cache_v, q_in, k_t, v_tok, sel_bf, pages, bias_s, mix_hi, mix_lo):
    pairs, chunks = DEC_B // 2, PAGES // 4
    order = [("A", 0), ("A", 1), ("B", 0), ("A", 2), ("B", 1), ("A", 3), ("B", 2), ("B", 3)]
    with ExitStack() as ctx:
        sc = Scope(nc, ctx, "ats")
        q = sc.sb("q", [P, 4, SAMPLE])
        qs = sc.sb("qs", [P, pairs, 2, 2, 2, 4, DEC_T])
        k_raw = sc.sb("k_raw", [P, 2, 2, 4, P])
        v_raw = sc.sb("v_raw", [P, 2, 2, 4, P])
        kt = sc.sb("kt", [P, 2, 2, 512])
        scores = sc.sb("scores", [P, 2, KEYS])
        probs = sc.sb("probs", [P, 2, 512])
        probs_t = sc.sb("probs_t", [P, 2, 4, P])
        new_probs = sc.sb("new_probs", [P, pairs, SAMPLE])
        new_probs_t = sc.sb("new_probs_t", [SAMPLE, P])
        tops = sc.sb("tops", [P, 2, chunks + 1])
        low = sc.sb("low", [P, 2])
        sums = sc.sb("sums", [P, 4])
        out = sc.sb("out", [P, 2, HD])
        turned = sc.ps("turned", [P, 2, 512])
        dots = sc.ps("dots", [P, 2, 512])
        probs_ps = sc.ps("probs_ps", [P, 2, 4, P])
        values = sc.ps("values", [P, P])
        small = sc.ps("small", [P, 512])
        s = Named(sc)
        block = ctx.enter_context(nc.Block())

        def new_keys(p, b2):
            return slice(PROMPT + (2 * p + b2) * DEC_T, PROMPT + (2 * p + b2 + 1) * DEC_T)

        def pages_of(eng, kind, p, which):
            cache, raw, used = (cache_k, k_raw, "turned1") if kind == "A" else (cache_v, v_raw, "v_used")

            def one(i, par, first):
                n = p * chunks + i * 2 + par
                if not first:
                    eng.wait_ge(s[used], n - 1)
                for b2, g in which:
                    load_page(eng, cache, pages, (p * 2 + b2) * PAGES + (i * 2 + par) * 4 + g,
                              raw[:, par, b2, g, :], s[f"{kind}_in_{eng.engine.name}{par}"])

            if p == 0:
                one(0, 0, True)
                one(0, 1, True)
            with eng.Fori(1 if p == 0 else 0, chunks // 2) as i:
                one(i, 0, False)
                one(i, 1, False)

        v_pool = [(0, 3), (1, 3)]
        all_pages = [(b2, g) for b2 in range(2) for g in range(4)]
        v_sync = [x for x in all_pages if x not in v_pool]

        @block.sync
        def _(sp):
            for j in range(4):
                sp.dma_start(q[:, j, :], q_in[j, :, PROMPT:NT]).then_inc(s["q_in"], 16)
            for kind, p in order:
                pages_of(sp, kind, p, all_pages if kind == "A" else v_sync)

        @block.gpsimd
        def _(pool):
            for kind, p in order:
                if kind == "B":
                    pages_of(pool, kind, p, v_pool)

        @block.tensor
        def _(pe):
            pe.wait_ge(s["tables_made"], 1)

            def part_a(p):
                with pe.Fori(0, chunks // 2) as i:
                    for par in range(2):
                        n = p * chunks + i * 2 + par
                        pe.wait_ge(s[f"A_in_{nc.sync.engine.name}{par}"], (p * chunks // 2 + i + 1) * 16 * 8)
                        for b2 in range(2):
                            pe.wait_ge(s[f"kt_copied{b2}"], n)
                            for g in range(4):
                                last = pe.transpose(turned[:, b2, g * P:(g + 1) * P], k_raw[:, par, b2, g, :], ident)
                            last.then_inc(s[f"turned{b2}"], 1)
                        pe.wait_ge(s["tops_read"], n - 1 if p > 0 else i * 2)
                        for b2 in range(2):
                            pe.wait_ge(s[f"kt_copied{b2}"], n + 1)
                            pe.matmul(dots[:, par, :], qs[:, p, b2].rearrange("p a k g t -> p (a k g t)"),
                                      kt[:, par, b2, :], start=b2 == 0, stop=False)
                        pe.matmul(dots[:, par, :], sel_bf[:, p, :], bias_s[:, bass.ts(i * 2 + par, 512)],
                                  start=False, stop=True).then_inc(s["dotted"], 1)
                if p == 1:
                    pe.wait_ge(s["new_dots_read"], 1)
                elif p >= 2:
                    pe.wait_ge(s["lo_done"], p - 1)
                for b2 in range(2):
                    pe.matmul(small[:, 0:DEC_T], qs[:, p, b2].rearrange("p a k g t -> p (a k g t)"),
                              k_t[:, new_keys(p, b2)], start=b2 == 0, stop=False)
                pe.matmul(small[:, 0:DEC_T], sel_bf[:, p, :], bias_s[:, PAST:KEYS], start=False, stop=True
                          ).then_inc(s["new_dotted"], 1)

            def part_b(p):
                pe.wait_ge(s["new_dots_read"], min(p + 2, pairs))
                if p == pairs - 1:
                    pe.wait_ge(s["lo_done"], p)
                pe.wait_ge(s["new_probs_made"], p + 1)
                pe.transpose(small[0:SAMPLE, 0:P], new_probs[:, p, :], ident).then_inc(s["new_probs_turned"], 1)
                pe.wait_ge(s["new_probs_copied"], p + 1)
                if p >= 1:
                    pe.wait_ge(s["scaled"], p)
                pe.matmul(values[:, :], new_probs_t[:, :], v_tok[0:SAMPLE, TILES - 1, :], start=True, stop=False)

                def chunk(i, par, stop):
                    n = p * chunks + i * 2 + par
                    pe.wait_ge(s["exps_done"], n + 1)
                    pe.wait_ge(s["probs_copied"], n - 1 if p > 0 else i * 2)
                    for g in range(4):
                        last = pe.transpose(probs_ps[:, par, g, :], probs[:, par, g * P:(g + 1) * P], ident)
                    last.then_inc(s["probs_turned"], 1)
                    pe.wait_ge(s["probs_copied"], n + 1)
                    seen = (p * chunks // 2 + i + 1) * 16
                    pe.wait_ge(s[f"B_in_{nc.sync.engine.name}{par}"], seen * len(v_sync))
                    pe.wait_ge(s[f"B_in_{nc.gpsimd.engine.name}{par}"], seen * len(v_pool))
                    for b2 in range(2):
                        rows = slice(b2 * HD, (b2 + 1) * HD)
                        for g in range(4):
                            last = pe.matmul(values[rows, :], probs_t[:, par, g, rows], v_raw[:, par, b2, g, :],
                                             start=False, stop=stop and g == 3)
                    last.then_inc(s["v_used"], 1)

                with pe.Fori(0, chunks // 2 - 1) as i:
                    chunk(i, 0, False)
                    chunk(i, 1, False)
                chunk(chunks // 2 - 1, 0, False)
                chunk(chunks // 2 - 1, 1, True)
                pe.wait_ge(s["scaled"], p + 1)
                pe.transpose(small[:, 0:P], out[:, :, :].rearrange("p a d -> p (a d)"), ident
                             ).then_inc(s["out_turned"], 1)

            for kind, p in order:
                (part_a if kind == "A" else part_b)(p)

        def mix_view(mix, rows, p):
            return mix[rows, 0:4, PROMPT + 16 * p:PROMPT + 16 * (p + 1)].rearrange("d j (b t) -> d j b t", b=2)

        def out_view(rows, e):
            return small[rows, 0:P].rearrange("d (b j e t) -> d j e b t", b=2, j=4, e=2)[:, :, e, :, :]

        @block.scalar
        def _(act):
            def part_a(p):
                if p >= 2:
                    act.wait_ge(s["exps_done"], (p - 1) * chunks)
                with act.Fori(0, chunks // 2) as i:
                    for par in range(2):
                        n = p * chunks + i * 2 + par
                        act.wait_ge(s["turned0"], n + 1)
                        act.wait_ge(s["dotted"], n - 1 if p > 0 else i * 2)
                        act.activation(kt[:, par, 0, :], turned[:, 0, :], ACT.Copy).then_inc(s["kt_copied0"], 1)
                        act.wait_ge(s["dotted"], n + 1)
                        act.activation(scores[:, p % 2, bass.ts(i * 2 + par, 512)], dots[:, par, :], ACT.Copy
                                       ).then_inc(s["dots_read"], 1)

            def part_b(p):
                act.wait_ge(s["low_made"], p + 1)
                act.wait_ge(s["dots_read"], (p + 1) * chunks)
                act.wait_ge(s["new_dots_read"], p + 1)
                if p >= 1:
                    act.wait_ge(s["new_probs_copied"], p)
                    act.wait_ge(s["sums_moved"], p)
                for b2 in range(2):
                    rows = slice(b2 * HD, (b2 + 1) * HD)
                    last = act.activation(new_probs[rows, p, (2 * p + b2) * DEC_T:(2 * p + b2 + 1) * DEC_T],
                                          scores[rows, p % 2, PAST:KEYS], ACT.Exp, scale=HD ** -0.5,
                                          bias=low[rows, p % 2:p % 2 + 1], accum_out=sums[rows, 2:3])
                last.then_inc(s["new_probs_made"], 1)
                with act.Fori(0, chunks // 2) as i:
                    for par in range(2):
                        n = p * chunks + i * 2 + par
                        act.wait_ge(s["probs_turned"], n - 1 if p > 0 else i * 2)
                        act.wait_ge(s["sums_added"], n - 1 if p > 0 else i * 2)
                        act.activation(probs[:, par, :], scores[:, p % 2, bass.ts(i * 2 + par, 512)], ACT.Exp,
                                       scale=HD ** -0.5, bias=low[:, p % 2:p % 2 + 1], accum_out=sums[:, par:par + 1]
                                       ).then_inc(s["exps_done"], 1)
                act.wait_ge(s["out_turned"], p + 1)
                for e in range(2):
                    rows = slice(e * HD, (e + 1) * HD)
                    ins = act.activation(mix_view(mix_hi, rows, p), out_view(rows, e), ACT.Copy)
                ins.then_inc(s["hi_done"], 1)

            for kind, p in order:
                (part_a if kind == "A" else part_b)(p)

        @block.vector
        def _(dve):
            own = own_chain(dve, s, "own")
            own(dve.memset(qs[:, :, :, :, :, :, :], 0.0))
            dve.memset(new_probs[:, :, :], 0.0)
            dve.wait_ge(s["q_in"], 64)
            for b2 in range(2):
                for kv in range(2):
                    rows = slice(kv * HD, (kv + 1) * HD)
                    q8 = q[rows, :, :].rearrange("d j (p b t) -> d p b j t", p=pairs, b=2)
                    ins = dve.tensor_copy(qs[rows, :, b2, b2, kv, :, :], q8[:, :, b2, :, :])
            ins.then_inc(s["tables_made"], 1)

            def part_a(p):
                if p >= 2:
                    dve.wait_ge(s["low_made"], p - 1)
                with dve.Fori(0, chunks // 2) as i:
                    for par in range(2):
                        n = p * chunks + i * 2 + par
                        dve.wait_ge(s["turned1"], n + 1)
                        dve.wait_ge(s["dotted"], n - 1 if p > 0 else i * 2)
                        dve.tensor_copy(kt[:, par, 1, :], turned[:, 1, :]).then_inc(s["kt_copied1"], 1)
                        dve.wait_ge(s["dots_read"], n + 1)
                        dve.tensor_reduce(tops[:, p % 2, bass.ds(i * 2 + par, 1)], dots[:, par, :], AX.X, ALU.max
                                          ).then_inc(s["tops_read"], 1)
                dve.wait_ge(s["new_dotted"], p + 1)
                own(dve.tensor_copy(scores[:, p % 2, PAST:KEYS], small[:, 0:DEC_T]))
                dve.tensor_reduce(tops[:, p % 2, chunks:chunks + 1], small[:, 0:DEC_T], AX.X, ALU.max
                                  ).then_inc(s["new_dots_read"], 1)
                dve.wait_ge(s["new_dots_read"], p + 1)
                dve.wait_ge(s["tops_read"], (p + 1) * chunks)
                if p >= 2:
                    dve.wait_ge(s["exps_done"], (p - 1) * chunks)
                own(dve.tensor_reduce(low[:, p % 2:p % 2 + 1], tops[:, p % 2, :], AX.X, ALU.max))
                dve.tensor_scalar(low[:, p % 2:p % 2 + 1], low[:, p % 2:p % 2 + 1], -(HD ** -0.5), None, ALU.mult
                                  ).then_inc(s["low_made"], 1)

            def part_b(p):
                dve.wait_ge(s["new_probs_turned"], p + 1)
                if p >= 1:
                    dve.wait_ge(s["v_used"], p * chunks)
                dve.tensor_copy(new_probs_t[:, :], small[0:SAMPLE, 0:P]).then_inc(s["new_probs_copied"], 1)
                dve.tensor_copy(sums[:, 3:4], sums[:, 2:3]).then_inc(s["sums_moved"], 1)
                dve.wait_ge(s["sums_moved"], p + 1)
                with dve.Fori(0, chunks // 2) as i:
                    for par in range(2):
                        n = p * chunks + i * 2 + par
                        dve.wait_ge(s["exps_done"], n + 1)
                        dve.wait_ge(s["sums_added"], n)
                        dve.tensor_tensor(sums[:, 3:4], sums[:, 3:4], sums[:, par:par + 1], ALU.add
                                          ).then_inc(s["sums_added"], 1)
                        dve.wait_ge(s["probs_turned"], n + 1)
                        dve.wait_ge(s["v_used"], n - 1 if p > 0 else i * 2)
                        dve.tensor_copy(probs_t[:, par, :, :], probs_ps[:, par, :, :]).then_inc(s["probs_copied"], 1)
                dve.wait_ge(s["sums_added"], (p + 1) * chunks)
                own(dve.reciprocal(sums[:, 3:4], sums[:, 3:4]))
                dve.wait_ge(s["v_used"], (p + 1) * chunks)
                if p >= 1:
                    dve.wait_ge(s["out_turned"], p)
                for b2 in range(2):
                    for kv in range(2):
                        rows = slice(b2 * HD + kv * 32, b2 * HD + kv * 32 + 32)
                        ins = dve.tensor_scalar(out[rows, :, :],
                                                values[rows, kv * HD:(kv + 1) * HD].unsqueeze(1).to_broadcast(
                                                    [32, 2, HD]), sums[rows, 3:4], None, ALU.mult)
                ins.then_inc(s["scaled"], 1)
                dve.wait_ge(s["hi_done"], p + 1)
                for e in range(2):
                    rows = slice(e * HD, (e + 1) * HD)
                    ins = dve.tensor_tensor(mix_view(mix_lo, rows, p), out_view(rows, e),
                                            mix_view(mix_hi, rows, p).bitcast(F32), ALU.subtract)
                ins.then_inc(s["lo_done"], 1)

            for kind, p in order:
                (part_a if kind == "A" else part_b)(p)


def mixer_output(nc, w_o, res_in, mix_hi, mix_lo, res):
    with ExitStack() as ctx:
        sc = Scope(nc, ctx, "wo")
        raw = sc.sb("raw", [P, 2, 1024])
        w_hi = sc.sb("w_hi", [P, 2, 1024], F32R)
        w_lo = sc.sb("w_lo", [P, 2, 1024], F32R)
        ps = [sc.ps("ps_a", [P, SLICES, 512]), sc.ps("ps_b", [P, SLICES, 512])]
        s = Named(sc)
        block = ctx.enter_context(nc.Block())

        @block.sync
        def _(sp):
            for m in range(KT):
                if m >= 2:
                    sp.wait_ge(s["lo_made"], m - 1)
                sp.dma_start(raw[:, m % 2, :].rearrange("p (k f) -> p k f", k=KT),
                             w_o[0, :, m * P:(m + 1) * P].rearrange("(k p) f -> p k f", p=P)
                             ).then_inc(s[f"raw_in{m % 2}"], 16)

        @block.gpsimd
        def _(pool):
            for m in range(KT):
                pool.dma_start(res[:, m, :], res_in[m]).then_inc(s["res_in"], 16)

        @block.tensor
        def _(pe):
            pe.wait_ge(s["mix_padded"], 1)
            with pe.Fori(0, KT // 2) as i:
                for par in range(2):
                    pe.wait_ge(s["lo_made"], i * 2 + par + 1)
                    pe.wait_ge(s["added"], i * 2)
                    three_pass(pe, ps[par], lambda k: w_hi[:, par, k * P:(k + 1) * P],
                               lambda k: w_lo[:, par, k * P:(k + 1) * P], lambda k: mix_hi[:, k],
                               lambda k: mix_lo[:, k], range(KT)).then_inc(s["filled"], 1)

        @block.scalar
        def _(act):
            for m in range(KT):
                act.wait_ge(s[f"raw_in{m % 2}"], 16 * (m // 2 + 1))
                if m >= 2:
                    act.wait_ge(s["filled"], m - 1)
                act.activation(w_hi[:, m % 2, :], raw[:, m % 2, :], ACT.Copy).then_inc(s["hi_made"], 1)

        @block.vector
        def _(dve):
            for mix in (mix_hi, mix_lo):
                ins = dve.memset(mix[:, 0:4, NT:TP].bitcast(F32), 0.0)
            ins.then_inc(s["mix_padded"], 1)

            def low(m):
                dve.wait_ge(s["hi_made"], m + 1)
                dve.tensor_tensor(w_lo[:, m % 2, :], raw[:, m % 2, :], w_hi[:, m % 2, :].bitcast(F32),
                                  ALU.subtract).then_inc(s["lo_made"], 1)

            low(0)
            low(1)
            dve.wait_ge(s["res_in"], 16 * KT)
            for m in range(KT):
                dve.wait_ge(s["filled"], m + 1)
                r = res[:, m, :].rearrange("p (s c) -> p s c", s=SLICES)
                dve.tensor_tensor(r, r, ps[m % 2][:, :, 0:SL], ALU.add).then_inc(s["added"], 1)
                if m + 2 < KT:
                    low(m + 2)


def shape_tables():
    i = np.arange(P)
    later = i[None, :] > i[:, None]
    t = {"ident": np.eye(P, dtype=np.float32), "ones": np.ones((P, P), np.float32),
         "ones_mean": np.full((P, P), 1.0 / D, np.float32)}
    t["cos"], t["sin"] = rope_tables()
    upper, strict, causal_t, levels = delta_masks(P, P)
    t["delta_tables"] = np.stack([upper, strict, causal_t] + levels, 1)
    upper, strict, causal_t, levels = delta_masks(SAMPLE, DEC_T)
    j = np.arange(SAMPLE)
    same = (j[:, None] // DEC_T == j[None, :] // DEC_T).astype(np.float32)
    t["delta_tables_s"] = np.stack([upper, strict, causal_t] + levels + [same], 1)
    t["member"] = (j[:, None] // DEC_T == np.arange(DEC_B)[None, :]).astype(np.float32)
    t["later_low"] = np.where(later, LOWEST, 0.0).astype(np.float32)
    t["later_big"] = np.where(later, -BIG, 0.0).astype(np.float32)
    t["sel"], t["sel_t"], t["head_of"], t["later_new"] = sample_tables()
    t["top_table"], t["top_bits"] = top_tables()
    return t


def load_constants(nc, name, pairs, casts=()):
    with ExitStack() as ctx:
        sc = Scope(nc, ctx, name)
        s = Named(sc)
        block = ctx.enter_context(nc.Block())

        @block.sync
        def _(sp):
            for dst, src in pairs:
                sp.dma_start(dst, src).then_inc(s["in"], 16)
            sp.wait_ge(s["in"], 16 * len(pairs))

        @block.vector
        def _(dve):
            dve.wait_ge(s["in"], 16 * len(pairs))
            for dst, src in casts:
                dve.tensor_copy(dst, src)


def zero(nc, buf):
    with nc.Block() as block:
        @block.vector
        def _(dve):
            dve.memset(buf[:, :, :], 0.0)


def store(nc, dst, src):
    with ExitStack() as ctx:
        stored = Scope(nc, ctx, "state").sem("stored")
        block = ctx.enter_context(nc.Block())

        @block.sync
        def _(sp):
            sp.dma_start(dst, src).then_inc(stored, 16)
            sp.wait_ge(stored, 16)


def decoder_step(nc, a, t, out):

    def dram(name, shape):
        return nc.dram_tensor(name, shape, F32).ap()

    q_d, qi_d, z_d = (dram(n, [4, P, NT]) for n in ("scratch_q", "scratch_qi", "scratch_z"))
    res_d = dram("scratch_res", [KT, P, TP])
    qkv_d = dram("scratch_qkv", [P, QKV_BLOCKS, NT])
    with ExitStack() as ctx:
        sc = Scope(nc, ctx, "main")
        ident, ones, ones_mean = (sc.sb(n, [P, P]) for n in ("ident", "ones", "ones_mean"))
        k_t, ki_t = sc.sb("k_t", [P, TP]), sc.sb("ki_t", [P, TP])
        v_tok = sc.sb("v_tok", [P, TILES, P])
        wi_tok = sc.sb("wi_tok", [P, TILES, 8])
        beta, gate = sc.sb("beta", [P, TILES, GH]), sc.sb("gate", [P, TILES, GH])
        unit = sc.sb("unit", [P, TILES, 8])
        with nc.cleanup_on_exit():
            load_constants(nc, "tables", [(ident[:, :], t["ident"]), (ones[:, :], t["ones"]),
                                          (ones_mean[:, :], t["ones_mean"])])

        with ExitStack() as c1:
            m = Scope(nc, c1, "first")
            x_hi = m.sb("x_hi", [P, KT, TP], F32R)
            x_lo = m.sb("x_lo", [P, KT, TP], F32R)
            with ExitStack() as c2:
                res = Scope(nc, c2, "first").sb("res", [P, KT, TP])
                with nc.cleanup_on_exit():
                    load_tokens(nc, a["x_prompt"], a["x_sample"], ident, res, x_hi, x_lo)
                with nc.cleanup_on_exit():
                    ffn(nc, "ffn1", a["ffn1_w_gate"], a["ffn1_w_up"], a["ffn1_w_down"], res, x_hi, x_lo)
                with nc.cleanup_on_exit():
                    norm(nc, "ln1", a["ln1_g"], a["ln1_b"], ones_mean, res, x_hi, x_lo, resid_out=res_d)
            qkv_t = m.sb("qkv_t", [P, QKV_BLOCKS, NT])
            v_t, wba_t = m.sb("v_t", [P, TP]), m.sb("wba_t", [16, TP])
            taps, samp = m.sb("taps", [P, QKV_BLOCKS, CONV_K]), m.sb("samp", [P, QKV_BLOCKS, DEC_B, 11])
            conv_tail = m.sb("conv_tail", [P, QKV_BLOCKS, 3])
            with nc.cleanup_on_exit():
                conv_taps(nc, a["conv_w"], a["state_conv"], ident, taps, samp)
            with nc.cleanup_on_exit():
                project(nc, a["w_in"], t["cos"], t["sin"], x_hi, x_lo, taps, samp, k_t, v_t, ki_t, wba_t,
                        qkv_t, conv_tail, q_d, qi_d, z_d)
            with nc.cleanup_on_exit():
                projection_tail(
                    nc, ident, ones, k_t, v_t, ki_t, wba_t, qkv_t, conv_tail, samp, taps, a["a_log"],
                    a["dt_bias"], v_tok, wi_tok, beta, gate, unit,
                    (out["k_prompt"].rearrange("l b s k d -> (l b s) (k d)"),
                     out["k_sample"].rearrange("l b s k d -> (l b s) (k d)")),
                    (out["v_prompt"].rearrange("l b s k d -> (l b s) (k d)"),
                     out["v_sample"].rearrange("l b s k d -> (l b s) (k d)")),
                    (out["kidx_prompt"].rearrange("l b s d -> (l b s) d"),
                     out["kidx_sample"].rearrange("l b s d -> (l b s) d")),
                    (out["conv_prompt"].rearrange("l b r c -> (l b r) c"),
                     out["conv_sample"].rearrange("l b r c -> (l b r) c")), qkv_d)

        with ExitStack() as c1:
            m = Scope(nc, c1, "mixer")
            mix_hi = m.sb("mix_hi", [P, KT, TP], F32R)
            mix_lo = m.sb("mix_lo", [P, KT, TP], F32R)

            with ExitStack() as c2:
                g = Scope(nc, c2, "heads")
                o_all = g.sb("o_all", [P, TILES, GH, P])
                with ExitStack() as c3:
                    g = Scope(nc, c3, "gdn")
                    state = g.sb("state", [P, GH, P])
                    tab = g.sb("tab", [P, 10, P])
                    with nc.cleanup_on_exit():
                        load_constants(nc, "delta_tables", [(tab[:, :, :], t["delta_tables"])])
                    with nc.cleanup_on_exit():
                        zero(nc, state)
                    with nc.cleanup_on_exit():
                        delta_prompt(nc, ident, ones, (tab[:, 0], tab[:, 1], tab[:, 2],
                                                       [tab[:, 3 + l] for l in range(7)]),
                                     qkv_d, beta, gate, unit, state, o_all)
                    with nc.cleanup_on_exit():
                        store(nc, out["gdn_prompt"].rearrange("l b h k v -> k (l b h) v"), state[:, :, :])
                with ExitStack() as c3:
                    g = Scope(nc, c3, "gdn_s")
                    tab_s = g.sb("tab_s", [SAMPLE, 7, SAMPLE])
                    member = g.sb("member", [SAMPLE, DEC_B])
                    with nc.cleanup_on_exit():
                        load_constants(nc, "sample_tables", [(tab_s[:, :, :], t["delta_tables_s"]),
                                                             (member[:, :], t["member"])])
                    with nc.cleanup_on_exit():
                        delta_sample(nc, ident, ones, (tab_s[:, 0], tab_s[:, 1], tab_s[:, 2],
                                                       [tab_s[:, 3 + l] for l in range(3)]), tab_s[:, 6],
                                     member[:, :], qkv_d, beta, gate, unit, a["state_gdn"][0],
                                     out["gdn_sample"].rearrange("l b h k v -> (l b) h k v"), o_all)
                with nc.cleanup_on_exit():
                    delta_finish(nc, ident, a["gdn_norm_w"], z_d, o_all, mix_hi, mix_lo)

            with ExitStack() as c3:
                b = Scope(nc, c3, "cut")
                bias_p, bias_s = b.sb("bias_p", [P, sum(WIDTHS)], BF16), b.sb("bias_s", [SAMPLE, KEYS], BF16)
                sel_bf = b.sb("sel_bf", [SAMPLE, 4, P], BF16)
                ident_bf, later_bf = b.sb("ident_bf", [P, P], BF16), b.sb("later_bf", [P, P], BF16)
                pages = b.sb("pages", [1, DEC_B * PAGES], I32)
                with ExitStack() as c4:
                    i = Scope(nc, c4, "index")
                    scores_p, scores_s = i.sb("scores_p", [P, sum(WIDTHS)]), i.sb("scores_s", [SAMPLE, KEYS])
                    top_table, top_bits = i.sb("top_table", [P, 4, 7]), i.sb("top_bits", [P, TOP_BITS + 7], I32)
                    with ExitStack() as c5:
                        j = Scope(nc, c5, "qi")
                        qi = j.sb("qi", [P, 4, NT])
                        later_low, later_big = j.sb("later_low", [P, P]), j.sb("later_big", [P, P])
                        sel, sel_t = j.sb("sel", [SAMPLE, 4, P]), j.sb("sel_t", [P, 4, SAMPLE])
                        head_of, later_new = j.sb("head_of", [P, 8]), j.sb("later_new", [SAMPLE, DEC_T])
                        with nc.cleanup_on_exit():
                            load_constants(nc, "index_tables", [
                                (later_low[:, :], t["later_low"]), (later_big[:, :], t["later_big"]),
                                (sel[:, :, :], t["sel"]), (sel_t[:, :, :], t["sel_t"]), (head_of[:, :], t["head_of"]),
                                (later_new[:, :], t["later_new"]), (top_table[:, :, :], t["top_table"]),
                                (top_bits[:, :], t["top_bits"]),
                                (pages[:, :], a["page_table"].rearrange("b p -> (b p)").unsqueeze(0))],
                                [(ident_bf[:, :], ident[:, :]), (later_bf[:, :], later_big[:, :]),
                                 (sel_bf[:, :, :], sel[:, :, :])])
                        with nc.cleanup_on_exit():
                            index_prompt(nc, qi_d, ki_t, wi_tok, later_low[:, :], qi, scores_p)
                        with nc.cleanup_on_exit():
                            index_sample(nc, ident[:, :], a["cache_kidx"], qi, ki_t, wi_tok, sel[:, :, :],
                                         sel_t[:, :, :], head_of[:, :], later_new[:, :], pages, scores_s)
                    with nc.cleanup_on_exit():
                        top_keys(nc, top_table[:, :, :], top_bits[:, :], scores_p, scores_s, bias_p, bias_s)
                with nc.cleanup_on_exit():
                    attend_prompt(nc, ident[:, :], ident_bf[:, :], later_bf[:, :], q_d, k_t, v_tok, bias_p,
                                  mix_hi, mix_lo)
                with nc.cleanup_on_exit():
                    attend_sample(nc, ident[:, :], a["cache_k"].rearrange("l n p k d -> l n p (k d)"),
                                  a["cache_v"].rearrange("l n p k d -> l n p (k d)"), q_d, k_t, v_tok, sel_bf, pages,
                                  bias_s, mix_hi, mix_lo)

            with ExitStack() as c2:
                res = Scope(nc, c2, "second").sb("res", [P, KT, TP])
                with nc.cleanup_on_exit():
                    mixer_output(nc, a["w_o"], res_d, mix_hi, mix_lo, res)
                with nc.cleanup_on_exit():
                    norm(nc, "ln2", a["ln2_g"], a["ln2_b"], ones_mean, res, mix_hi, mix_lo)
                with nc.cleanup_on_exit():
                    ffn(nc, "ffn2", a["ffn2_w_gate"], a["ffn2_w_up"], a["ffn2_w_down"], res, mix_hi, mix_lo)
                with nc.cleanup_on_exit():
                    norm(nc, "ln3", a["ln3_g"], a["ln3_b"], ones_mean, res, None, None)
                with nc.cleanup_on_exit():
                    store_tokens(nc, ident, res, out["y_prompt"], out["y_sample"])


_INS = ["x_prompt", "x_sample", "cache_k", "cache_v", "cache_kidx", "state_gdn", "state_conv", "page_table",
        "ffn1_w_gate", "ffn1_w_up", "ffn1_w_down", "ln1_g", "ln1_b", "w_in", "conv_w", "a_log", "dt_bias",
        "gdn_norm_w", "w_o", "ln2_g", "ln2_b", "ffn2_w_gate", "ffn2_w_up", "ffn2_w_down", "ln3_g", "ln3_b"]
_OUTS = {"y_prompt": (1, 1024, 1024), "y_sample": (8, 8, 1024), "k_prompt": (1, 1, 1024, 2, 64),
         "v_prompt": (1, 1, 1024, 2, 64), "kidx_prompt": (1, 1, 1024, 64), "gdn_prompt": (1, 1, 4, 128, 128),
         "conv_prompt": (1, 1, 3, 1536), "k_sample": (1, 8, 8, 2, 64), "v_sample": (1, 8, 8, 2, 64),
         "kidx_sample": (1, 8, 8, 64), "gdn_sample": (1, 8, 4, 128, 128), "conv_sample": (1, 8, 3, 1536)}


def kernel(**inputs):
    import concourse.bacc as _bacc
    from concourse.bass_utils import run_bass_kernel_spmd as _run

    nc = _bacc.Bacc("TRN2", target_bir_lowering=False, num_devices=1)
    arrays = {f"in_{name}": np.ascontiguousarray(inputs[name]) for name in _INS}
    tables = {f"table_{name}": np.ascontiguousarray(v) for name, v in shape_tables().items()}
    aps = {}
    for name, v in {**arrays, **tables}.items():
        aps[name] = nc.dram_tensor(name, v.shape, mybir.dt.from_np(v.dtype), kind="ExternalInput").ap()
    out = {n: nc.dram_tensor(f"out_{n}", shape, F32, kind="ExternalOutput").ap() for n, shape in _OUTS.items()}
    decoder_step(nc, {n[3:]: aps[n] for n in arrays}, {n[6:]: aps[n] for n in tables}, out)
    r = _run(nc, [{**arrays, **tables}], core_ids=[0])
    return tuple(r.results[0][f"out_{n}"] for n in _OUTS)
```

```python
from contextlib import ExitStack

import numpy as np

import concourse.bass as bass
from concourse import mybir

F32 = mybir.dt.float32
F32R = mybir.dt.float32r
BF16 = mybir.dt.bfloat16
I32 = mybir.dt.int32
ALU = mybir.AluOpType
ACT = mybir.ActivationFunctionType
AX = mybir.AxisListType

P = 128
D = 1024
KT = D // P
PROMPT = 1024
DEC_B, DEC_T = 8, 8
SAMPLE = DEC_B * DEC_T
NT = PROMPT + SAMPLE
SLICES = 3
SL = 364
TP = SLICES * SL
TILES = 9
D_FF = 2816
FB = D_FF // P
CHUNKS = FB // 2
ALPHA = 2.0 ** 0.25
LN_EPS = 1e-5
NORM_EPS = 1e-6


def tile_width(t):
    return P if t < PROMPT // P else SAMPLE


def slices(t):
    return [slice(s * SL, (s + 1) * SL) for s in range(t)]


class Scope:

    def __init__(self, nc, ctx, name):
        self.nc, self.ctx, self.name = nc, ctx, name

    def sb(self, name, shape, dt=F32):
        return self.ctx.enter_context(self.nc.sbuf_tensor(f"{self.name}_{name}", shape, dt))

    def ps(self, name, shape, dt=F32):
        return self.ctx.enter_context(self.nc.psum_tensor(f"{self.name}_{name}", shape, dt))

    def sem(self, name):
        return self.nc.alloc_semaphore(f"{self.name}_{name}")


class Named(dict):

    def __init__(self, sc):
        super().__init__()
        self.sc = sc

    def __missing__(self, name):
        self[name] = self.sc.sem(name)
        return self[name]


def three_pass(pe, out, w_hi, w_lo, x_hi, x_lo, ks, start=True, stop=True):
    last = None
    for n, k in enumerate(ks):
        for p, (w, x) in enumerate(((w_hi, x_hi), (w_hi, x_lo), (w_lo, x_hi))):
            for s in range(SLICES):
                last = pe.matmul(out[:, s, 0:SL], w(k), x(k)[:, s * SL:(s + 1) * SL],
                                 start=start and n == 0 and p == 0, stop=stop and n == len(ks) - 1 and p == 2)
    return last


def load_tokens(nc, x_prompt, x_sample, ident, res, x_hi, x_lo):
    with ExitStack() as ctx:
        sc = Scope(nc, ctx, "load")
        rows = sc.sb("rows", [P, 2, D])
        turned = sc.ps("turned", [P, 2, KT, P])
        rows_in = [sc.sem("rows_in0"), sc.sem("rows_in1")]
        turned_done, hi_done, lo_done, res_done, pads = (sc.sem(n) for n in (
            "turned_done", "hi_done", "lo_done", "res_done", "pads"))
        block = ctx.enter_context(nc.Block())

        @block.sync
        def _(sp):
            for t in range(TILES):
                w = tile_width(t)
                src = x_prompt[0, t * P:(t + 1) * P, :] if t < TILES - 1 else x_sample.rearrange("b t d -> (b t) d")
                if t >= 2:
                    sp.wait_ge(turned_done, t - 1)
                sp.dma_start(rows[0:w, t % 2, :], src).then_inc(rows_in[t % 2], 16)

        @block.tensor
        def _(pe):
            for t in range(TILES):
                w = tile_width(t)
                pe.wait_ge(rows_in[t % 2], 16 * (t // 2 + 1))
                if t >= 2:
                    pe.wait_ge(lo_done, t - 1)
                    pe.wait_ge(res_done, t - 1)
                for k in range(KT):
                    last = pe.transpose(turned[:, t % 2, k, 0:w], rows[0:w, t % 2, k * P:(k + 1) * P],
                                        ident[0:w, 0:w])
                last.then_inc(turned_done, 1)

        @block.scalar
        def _(act):
            for t in range(TILES):
                w, c = tile_width(t), t * P
                act.wait_ge(turned_done, t + 1)
                act.activation(x_hi[:, :, c:c + w], turned[:, t % 2, :, 0:w], ACT.Copy).then_inc(hi_done, 1)

        @block.vector
        def _(dve):
            for buf in (x_hi, x_lo, res):
                dve.memset(buf[:, :, NT:TP].bitcast(F32) if buf is not res else buf[:, :, NT:TP], 0.0)
            for t in range(TILES):
                w, c = tile_width(t), t * P
                dve.wait_ge(hi_done, t + 1)
                dve.tensor_scalar(res[:, :, c:c + w], turned[:, t % 2, :, 0:w], ALPHA, None,
                                  ALU.mult).then_inc(res_done, 1)
                dve.tensor_tensor(x_lo[:, :, c:c + w], turned[:, t % 2, :, 0:w],
                                  x_hi[:, :, c:c + w].bitcast(F32), ALU.subtract).then_inc(lo_done, 1)


def ffn(nc, name, w_gate, w_up, w_down, res, x_hi, x_lo):
    with ExitStack() as ctx:
        sc = Scope(nc, ctx, name)
        raw = {k: sc.sb(f"raw_{k}", [P, 1024]) for k in "gud"}
        hi = {k: sc.sb(f"hi_{k}", [P, 1024], F32R) for k in "gu"}
        lo = {k: sc.sb(f"lo_{k}", [P, 1024], F32R) for k in "gu"}
        d_hi = sc.sb("hi_d", [P, 2, 1024], F32R)
        d_lo = sc.sb("lo_d", [P, 2, 1024], F32R)
        act_buf = sc.sb("hidden", [P, 2, TP])
        h_hi = sc.sb("h_hi", [P, 2, 2, TP], F32R)
        h_lo = sc.sb("h_lo", [P, 2, 2, TP], F32R)
        ps_a = sc.ps("ps_a", [P, SLICES, 512])
        ps_b = sc.ps("ps_b", [P, SLICES, 512])
        raw_in = {k: sc.sem(f"raw_in_{k}") for k in "gud"}
        whi_done = {k: sc.sem(f"whi_done_{k}") for k in "gud"}
        wlo_done = {k: sc.sem(f"wlo_done_{k}") for k in "gud"}
        gate_filled, up_filled, down_filled = (sc.sem(n) for n in ("gate_filled", "up_filled", "down_filled"))
        silu_done, mul_done, hhi_done, hlo_done, down_added = (sc.sem(n) for n in (
            "silu_done", "mul_done", "hhi_done", "hlo_done", "down_added"))
        filled = {"g": gate_filled, "u": up_filled}
        block = ctx.enter_context(nc.Block())

        def weight_block(w, n):
            return w[0, :, bass.ts(n, P)].rearrange("(k p) f -> p k f", p=P)

        def load(eng, kind, n, first):
            if not first:
                eng.wait_ge(wlo_done[kind], n)
            if kind == "d":
                src = w_down[0, bass.ts(n, P), :]
                dst = raw["d"][:, :]
            else:
                src = weight_block(w_gate if kind == "g" else w_up, n)
                dst = raw[kind][:, :].rearrange("p (k f) -> p k f", k=KT)
            eng.dma_start(dst, src).then_inc(raw_in[kind], 16)

        @block.sync
        def _(sp):
            load(sp, "g", 0, True)
            load(sp, "u", 0, True)
            with sp.Fori(1, FB) as n:
                load(sp, "g", n, False)
                load(sp, "u", n, False)

        @block.gpsimd
        def _(pool):
            load(pool, "d", 0, True)
            with pool.Fori(1, FB) as n:
                load(pool, "d", n, False)

        @block.tensor
        def _(pe):
            def gates(g, par, first=False):
                for fb in range(2):
                    n = g * 2 + fb
                    pe.wait_ge(wlo_done["g"], n + 1)
                    if fb == 1 or not first:
                        pe.wait_ge(silu_done, n)
                    if fb == 0 and not first:
                        pe.wait_ge(down_added, g * 8 - 8)
                    three_pass(pe, ps_a, lambda k: hi["g"][:, k * P:(k + 1) * P],
                               lambda k: lo["g"][:, k * P:(k + 1) * P],
                               lambda k: x_hi[:, k], lambda k: x_lo[:, k], range(KT)).then_inc(gate_filled, 1)
                    pe.wait_ge(wlo_done["u"], n + 1)
                    if fb == 1 or not first:
                        pe.wait_ge(mul_done, n)
                    three_pass(pe, ps_b, lambda k: hi["u"][:, k * P:(k + 1) * P],
                               lambda k: lo["u"][:, k * P:(k + 1) * P],
                               lambda k: x_hi[:, k], lambda k: x_lo[:, k], range(KT)).then_inc(up_filled, 1)

            def down(d, par, last=False):
                pe.wait_ge(wlo_done["d"], d * 2 + 2)
                pe.wait_ge(hlo_done, d * 2 + 2)
                if last:
                    pe.wait_ge(down_added, d * 8)
                for m in range(8):
                    if m == 0:
                        pe.wait_ge(silu_done, d * 2 + (2 if last else 4))
                    elif m == 1:
                        pe.wait_ge(mul_done, d * 2 + (2 if last else 4))
                    else:
                        pe.wait_ge(down_added, d * 8 + m - 1)
                    three_pass(pe, ps_a if m % 2 == 0 else ps_b,
                               lambda k: d_hi[:, k, m * P:(m + 1) * P], lambda k: d_lo[:, k, m * P:(m + 1) * P],
                               lambda k: h_hi[:, par, k], lambda k: h_lo[:, par, k], range(2)
                               ).then_inc(down_filled, 1)

            gates(0, 0, first=True)
            with pe.Fori(0, CHUNKS // 2) as i:
                gates(i * 2 + 1, 1)
                down(i * 2, 0)
                gates(i * 2 + 2, 0)
                down(i * 2 + 1, 1)
            down(CHUNKS - 1, 0, last=True)

        def per_chunk(eng, gates, down):
            gates(0, 0, True, False)
            with eng.Fori(0, CHUNKS // 2 - 1) as i:
                gates(i * 2 + 1, 1, False, False)
                down(i * 2, False)
                gates(i * 2 + 2, 0, False, False)
                down(i * 2 + 1, False)
            gates(CHUNKS - 2, 1, False, False)
            down(CHUNKS - 3, False)
            gates(CHUNKS - 1, 0, False, True)
            down(CHUNKS - 2, False)
            down(CHUNKS - 1, True)

        @block.scalar
        def _(act):
            def weight_hi(kind, n, first=False):
                act.wait_ge(raw_in[kind], (n + 1) * 16)
                if not first:
                    act.wait_ge(filled[kind], n)
                act.activation(hi[kind][:, :], raw[kind][:, :], ACT.Copy).then_inc(whi_done[kind], 1)

            def down_hi(d, first=False):
                for k in range(2):
                    act.wait_ge(raw_in["d"], (d * 2 + k + 1) * 16)
                    if not first:
                        act.wait_ge(down_filled, d * 8)
                    act.activation(d_hi[:, k, :], raw["d"][:, :], ACT.Copy).then_inc(whi_done["d"], 1)

            def gates(g, par, first, last):
                for fb in range(2):
                    n = g * 2 + fb
                    act.wait_ge(gate_filled, n + 1)
                    if not first:
                        act.wait_ge(hlo_done, n - 1)
                    act.activation(act_buf[:, fb, :].rearrange("p (s c) -> p s c", s=SLICES), ps_a[:, :, 0:SL],
                                   ACT.Silu).then_inc(silu_done, 1)
                    if not (last and fb == 1):
                        weight_hi("g", n + 1)
                    act.wait_ge(mul_done, n + 1)
                    if not first:
                        act.wait_ge(down_filled, g * 8 - 8)
                    act.activation(h_hi[:, par, fb, :], act_buf[:, fb, :], ACT.Copy).then_inc(hhi_done, 1)
                    if not (last and fb == 1):
                        weight_hi("u", n + 1)

            weight_hi("g", 0, first=True)
            weight_hi("u", 0, first=True)
            down_hi(0, first=True)
            per_chunk(act, gates, lambda d, last: None if last else down_hi(d + 1))

        @block.vector
        def _(dve):
            def weight_lo(kind, n):
                dve.wait_ge(whi_done[kind], n + 1)
                dve.tensor_tensor(lo[kind][:, :], raw[kind][:, :], hi[kind][:, :].bitcast(F32),
                                  ALU.subtract).then_inc(wlo_done[kind], 1)

            def down_lo(d):
                for k in range(2):
                    dve.wait_ge(whi_done["d"], d * 2 + k + 1)
                    dve.tensor_tensor(d_lo[:, k, :], raw["d"][:, :], d_hi[:, k, :].bitcast(F32),
                                      ALU.subtract).then_inc(wlo_done["d"], 1)

            def gates(g, par, first, last):
                for fb in range(2):
                    n = g * 2 + fb
                    if not (last and fb == 1):
                        weight_lo("g", n + 1)
                    dve.wait_ge(silu_done, n + 1)
                    dve.wait_ge(up_filled, n + 1)
                    hid = act_buf[:, fb, :].rearrange("p (s c) -> p s c", s=SLICES)
                    dve.tensor_tensor(hid, hid, ps_b[:, :, 0:SL], ALU.mult).then_inc(mul_done, 1)
                    dve.wait_ge(hhi_done, n + 1)
                    dve.tensor_tensor(h_lo[:, par, fb, :], act_buf[:, fb, :], h_hi[:, par, fb, :].bitcast(F32),
                                      ALU.subtract).then_inc(hlo_done, 1)
                    if not (last and fb == 1):
                        weight_lo("u", n + 1)

            def down(d, last):
                dve.wait_ge(down_added, d * 8)
                for m in range(8):
                    dve.wait_ge(down_filled, d * 8 + m + 1)
                    r = res[:, m, :].rearrange("p (s c) -> p s c", s=SLICES)
                    dve.scalar_tensor_tensor(r, (ps_a if m % 2 == 0 else ps_b)[:, :, 0:SL], 0.5, r,
                                             ALU.mult, ALU.add).then_inc(down_added, 1)
                if not last:
                    down_lo(d + 1)

            weight_lo("g", 0)
            weight_lo("u", 0)
            down_lo(0)
            per_chunk(dve, gates, down)


def column_load(eng, dst, vec, sem):
    with eng.bass.allow_non_contiguous_dma(reason="a kilobyte or so of scales"):
        eng.dma_start(dst, vec.rearrange("(k p) -> p k", p=P)).then_inc(sem, 16)


def norm(nc, name, g, b, ones_mean, res, x_hi, x_lo, resid_out=None):
    with ExitStack() as ctx:
        sc = Scope(nc, ctx, name)
        gb = sc.sb("gb", [P, 2, KT])
        sq = sc.sb("sq", [P, 2, KT, SL])
        rstd = sc.sb("rstd", [P, TP])
        mean = sc.ps("mean", [P, SLICES, 512])
        var = sc.ps("var", [P, SLICES, 512])
        s = Named(sc)
        block = ctx.enter_context(nc.Block())
        cols = slices(SLICES)

        @block.sync
        def _(sp):
            column_load(sp, gb[:, 0, :], g[0], s["gb_in"])
            column_load(sp, gb[:, 1, :], b[0], s["gb_in"])
            if resid_out is not None:
                for i in range(SLICES):
                    sp.wait_ge(s["res_done"], i + 1)
                    sp.dma_start(resid_out[:, :, cols[i]].rearrange("k p c -> p k c"), res[:, :, cols[i]]
                                 ).then_inc(s["res_out"], 16)
                sp.wait_ge(s["res_out"], 16 * SLICES)

        @block.tensor
        def _(pe):
            def means(i):
                for k in range(KT):
                    last = pe.matmul(mean[:, i, 0:SL], ones_mean[:, :], res[:, k, cols[i]],
                                     start=k == 0, stop=k == KT - 1)
                last.then_inc(s["mean_done"], 1)

            means(0)
            for i in range(SLICES):
                if i + 1 < SLICES:
                    means(i + 1)
                pe.wait_ge(s["squared"], i + 1)
                for k in range(KT):
                    last = pe.matmul(var[:, i, 0:SL], ones_mean[:, :], sq[:, i % 2, k, :],
                                     start=k == 0, stop=k == KT - 1)
                last.then_inc(s["var_done"], 1)

        @block.scalar
        def _(act):
            def square(i):
                act.wait_ge(s["centred"], i + 1)
                if i >= 2:
                    act.wait_ge(s["var_done"], i - 1)
                act.activation(sq[:, i % 2, :, :], res[:, :, cols[i]], ACT.Square).then_inc(s["squared"], 1)

            def root(i):
                act.wait_ge(s["std_in"], i + 1)
                act.activation(rstd[:, cols[i]], rstd[:, cols[i]], ACT.Sqrt).then_inc(s["std_done"], 1)

            def scale(i):
                act.wait_ge(s["normed"], i + 1)
                for k in range(KT // 2, KT):
                    last = act.activation(res[:, k, cols[i]], res[:, k, cols[i]], ACT.Identity,
                                          scale=gb[:, 0, k:k + 1], bias=gb[:, 1, k:k + 1])
                last.then_inc(s["scaled_act"], 1)
                if x_hi is not None:
                    act.wait_ge(s["scaled_act"], i + 1)
                    act.wait_ge(s["scaled_dve"], i + 1)
                    act.activation(x_hi[:, :, cols[i]], res[:, :, cols[i]], ACT.Copy).then_inc(s["hi_done"], 1)

            def residual(i):
                act.wait_ge(s["lo_done"], i + 1)
                act.activation(res[:, :, cols[i]], res[:, :, cols[i]], ACT.Copy, scale=ALPHA
                               ).then_inc(s["res_done"], 1)

            square(0)
            square(1)
            root(0)
            act.wait_ge(s["gb_in"], 32)
            scale(0)
            for i in range(1, SLICES):
                if i + 1 < SLICES:
                    square(i + 1)
                root(i)
                scale(i)
                if x_hi is not None:
                    residual(i - 1)
            if x_hi is not None:
                residual(SLICES - 1)

        @block.vector
        def _(dve):
            def centre(i):
                dve.wait_ge(s["mean_done"], i + 1)
                dve.tensor_tensor(res[:, :, cols[i]], res[:, :, cols[i]],
                                  mean[:, i, 0:SL].unsqueeze(1).to_broadcast([P, KT, SL]),
                                  ALU.subtract).then_inc(s["centred"], 1)

            def normalise(i):
                dve.wait_ge(s["std_done"], i + 1)
                dve.reciprocal(rstd[:, cols[i]], rstd[:, cols[i]]).then_inc(s["rstd_done"], 1)
                dve.wait_ge(s["rstd_done"], i + 1)
                dve.wait_ge(s["centred"], i + 1)
                dve.wait_ge(s["squared"], i + 1)
                dve.tensor_tensor(res[:, :, cols[i]], res[:, :, cols[i]],
                                  rstd[:, cols[i]].unsqueeze(1).to_broadcast([P, KT, SL]),
                                  ALU.mult).then_inc(s["normed"], 1)
                dve.wait_ge(s["normed"], i + 1)
                for k in range(KT // 2):
                    last = dve.tensor_scalar(res[:, k, cols[i]], res[:, k, cols[i]], gb[:, 0, k:k + 1],
                                             gb[:, 1, k:k + 1], ALU.mult, ALU.add)
                last.then_inc(s["scaled_dve"], 1)

            def low(i):
                dve.wait_ge(s["hi_done"], i + 1)
                dve.tensor_tensor(x_lo[:, :, cols[i]], res[:, :, cols[i]], x_hi[:, :, cols[i]].bitcast(F32),
                                  ALU.subtract).then_inc(s["lo_done"], 1)

            def deviation(i):
                dve.wait_ge(s["var_done"], i + 1)
                dve.tensor_scalar(rstd[:, cols[i]], var[:, i, 0:SL], LN_EPS, None, ALU.add
                                  ).then_inc(s["std_in"], 1)

            centre(0)
            centre(1)
            deviation(0)
            dve.wait_ge(s["gb_in"], 32)
            normalise(0)
            for i in range(1, SLICES):
                if i + 1 < SLICES:
                    centre(i + 1)
                deviation(i)
                normalise(i)
                if x_hi is not None:
                    low(i - 1)
            if x_hi is not None:
                low(SLICES - 1)


def store_tokens(nc, ident, res, y_prompt, y_sample):
    with ExitStack() as ctx:
        sc = Scope(nc, ctx, "store")
        rows = sc.sb("rows", [P, 2, D])
        turned = sc.ps("turned", [P, 2, KT, P])
        turned_done, copied, out_done = (sc.sem(n) for n in ("turned_done", "copied", "out_done"))
        out_free = [sc.sem("out_even"), sc.sem("out_odd")]
        block = ctx.enter_context(nc.Block())

        @block.tensor
        def _(pe):
            for t in range(TILES):
                w = tile_width(t)
                if t >= 2:
                    pe.wait_ge(copied, t - 1)
                for k in range(KT):
                    last = pe.transpose(turned[0:w, t % 2, k, :], res[:, k, t * P:t * P + w], ident[:, :])
                last.then_inc(turned_done, 1)

        @block.vector
        def _(dve):
            for t in range(TILES):
                w = tile_width(t)
                dve.wait_ge(turned_done, t + 1)
                if t >= 2:
                    dve.wait_ge(out_free[t % 2], 16 * (t // 2))
                dve.tensor_copy(rows[0:w, t % 2, :].rearrange("p (k f) -> p k f", k=KT),
                                turned[0:w, t % 2, :, :]).then_inc(copied, 1)

        @block.sync
        def _(sp):
            for t in range(TILES):
                w = tile_width(t)
                dst = y_prompt[0, t * P:(t + 1) * P, :] if t < TILES - 1 else y_sample.rearrange("b t d -> (b t) d")
                sp.wait_ge(copied, t + 1)
                sp.dma_start(dst, rows[0:w, t % 2, :]).then_inc(out_free[t % 2], 16)
            sp.wait_ge(out_free[0], 16 * ((TILES + 1) // 2))
            sp.wait_ge(out_free[1], 16 * (TILES // 2))


HD = 64
ATT_H = 8
GH = 4
CONV_K = 4
QKV_BLOCKS = 12
W_Q, W_K, W_V, W_QI, W_KI, W_WI, W_QKV, W_Z, W_BA = 0, 512, 640, 768, 1280, 1344, 1352, 2888, 3400
ROT = HD // 4


def projection_plan():
    plan = [("ki", 0, [(0, W_KI, HD), (HD, W_KI, HD)])]
    plan += [("qi", j, [(0, W_QI + j * P, P)]) for j in range(4)]
    plan += [("wba", 0, [(0, W_WI, 8), (8, W_BA, 8)])]
    plan += [("k", 0, [(0, W_K, P)]), ("v", 0, [(0, W_V, P)])]
    plan += [("q", j, [(0, W_Q + j * HD, HD), (HD, W_Q + (4 + j) * HD, HD)]) for j in range(4)]
    plan += [("z", j, [(0, W_Z + j * P, P)]) for j in range(4)]
    plan += [("qkv", j, [(0, W_QKV + j * P, P)]) for j in range(QKV_BLOCKS)]
    return plan


def rope_tables():
    half = ROT // 2
    inv = (np.float32(500000.0) ** (-np.arange(half, dtype=np.float32) / np.float32(half))).astype(np.float32)
    pos = np.concatenate([np.arange(PROMPT), np.tile(4096 + np.arange(DEC_T), DEC_B)]).astype(np.float32)
    ang = (pos[None, :] * inv[:, None]).astype(np.float32)
    cos, sin = np.ones((P, NT), np.float32), np.zeros((P, NT), np.float32)
    for r in (0, HD):
        cos[r:r + half] = cos[r + half:r + ROT] = np.cos(ang)
        sin[r:r + half], sin[r + half:r + ROT] = -np.sin(ang), np.sin(ang)
    return cos, sin


ROPE_SWAP = list(range(8, 16)) + list(range(8)) + list(range(16, 32))


def conv_taps(nc, conv_w, state_conv, ident, taps, samp):
    with ExitStack() as ctx:
        sc = Scope(nc, ctx, "taps")
        rows = sc.sb("rows", [CONV_K, 12 * P])
        srows = sc.sb("srows", [24, 12 * P])
        turned = sc.ps("turned", [P, 12, CONV_K])
        sturned = sc.ps("sturned", [P, 12, 24])
        rows_in, turned_done = sc.sem("rows_in"), sc.sem("turned_done")
        block = ctx.enter_context(nc.Block())

        @block.sync
        def _(sp):
            sp.dma_start(rows[:, :], conv_w[0]).then_inc(rows_in, 16)
            sp.dma_start(srows[:, :], state_conv[0].rearrange("b r c -> (b r) c")).then_inc(rows_in, 16)

        @block.tensor
        def _(pe):
            pe.wait_ge(rows_in, 32)
            for j in range(12):
                pe.transpose(turned[:, j, :], rows[:, j * P:(j + 1) * P], ident[0:CONV_K, 0:CONV_K])
                last = pe.transpose(sturned[:, j, :], srows[:, j * P:(j + 1) * P], ident[0:24, 0:24])
            last.then_inc(turned_done, 1)

        @block.vector
        def _(dve):
            dve.wait_ge(turned_done, 1)
            dve.tensor_copy(taps[:, :, :], turned[:, :, :])
            for j in range(12):
                dve.tensor_copy(samp[:, j, :, 0:3], sturned[:, j, :].rearrange("p (b r) -> p b r", b=DEC_B))


def project(nc, w_in, cos_in, sin_in, x_hi, x_lo, taps, samp, k_t, v_t, ki_t, wba_t, qkv_t, conv_tail,
            q_out, qi_out, z_out):
    plan = projection_plan()
    n_blocks = len(plan)
    assert n_blocks % 2 == 0
    with ExitStack() as ctx:
        sc = Scope(nc, ctx, "proj")
        raw = sc.sb("raw", [P, 2, 1024])
        w_hi = sc.sb("w_hi", [P, 2, 1024], F32R)
        w_lo = sc.sb("w_lo", [P, 2, 1024], F32R)
        cos = sc.sb("cos", [P, NT])
        sin = sc.sb("sin", [P, NT])
        copied = sc.sb("copied", [P, 2, TP])
        swapped = sc.sb("swapped", [P, NT])
        stage = sc.sb("stage", [P, 2, TP])
        ps = [sc.ps("ps_a", [P, SLICES, 512]), sc.ps("ps_b", [P, SLICES, 512])]
        raw_in = [sc.sem("raw_in0"), sc.sem("raw_in1")]
        stored = [sc.sem("stored0"), sc.sem("stored1")]
        tables_in, whi_done, wlo_done, filled, evacuated, vector_step, silu_done = (sc.sem(n) for n in (
            "tables_in", "whi_done", "wlo_done", "filled", "evacuated", "vector_step", "silu_done"))
        block = ctx.enter_context(nc.Block())
        arrived, total, vector_steps, steps = [], [0, 0], [], 0
        for n, (kind, _, parts) in enumerate(plan):
            total[n % 2] += 16 * len(parts)
            arrived.append(total[n % 2])
            steps += {"q": 4, "qi": 4, "k": 4, "ki": 4, "qkv": 5}.get(kind, 0)
            vector_steps.append(steps)
        staged = [n for n, (kind, _, _) in enumerate(plan) if kind in ("q", "qi", "z")]

        @block.sync
        def _(sp):
            sp.dma_start(cos[:, :], cos_in).then_inc(tables_in, 16)
            sp.dma_start(sin[:, :], sin_in).then_inc(tables_in, 16)
            for n, (_, _, parts) in enumerate(plan):
                if n >= 2:
                    sp.wait_ge(wlo_done, n - 1)
                for row, col, width in parts:
                    dst = raw[:, n % 2, :].rearrange("p (k f) -> p k f", k=KT)[:, :, row:row + width]
                    src = w_in[0, :, col:col + width].rearrange("(k p) f -> p k f", p=P)
                    sp.dma_start(dst, src).then_inc(raw_in[n % 2], 16)

        @block.gpsimd
        def _(pool):
            for i, n in enumerate(staged):
                kind, j, _ = plan[n]
                if kind == "z":
                    pool.wait_ge(evacuated, n + 1)
                else:
                    pool.wait_ge(vector_step, vector_steps[n])
                out = {"q": q_out, "qi": qi_out, "z": z_out}[kind]
                pool.dma_start(out[j], stage[:, i % 2, 0:NT]).then_inc(stored[i % 2], 16)
            pool.wait_ge(stored[0], 16 * ((len(staged) + 1) // 2))
            pool.wait_ge(stored[1], 16 * (len(staged) // 2))

        @block.tensor
        def _(pe):
            def pair(i, first=False):
                for par in range(2):
                    pe.wait_ge(wlo_done, i * 2 + par + 1)
                    if not first:
                        pe.wait_ge(evacuated, i * 2 + par - 1)
                    three_pass(pe, ps[par], lambda k: w_hi[:, par, k * P:(k + 1) * P],
                               lambda k: w_lo[:, par, k * P:(k + 1) * P], lambda k: x_hi[:, k],
                               lambda k: x_lo[:, k], range(KT)).then_inc(filled, 1)

            pair(0, first=True)
            with pe.Fori(1, n_blocks // 2) as i:
                pair(i)

        def whole(buf):
            return buf.rearrange("p (s c) -> p s c", s=SLICES)

        @block.scalar
        def _(act):
            def weight_hi(n):
                act.wait_ge(raw_in[n % 2], arrived[n])
                if n >= 2:
                    act.wait_ge(filled, n - 1)
                if plan[n][0] == "wba":
                    v = lambda b: b[:, n % 2, :].rearrange("p (k f) -> p k f", k=KT)[:, :, 0:16]
                    act.activation(v(w_hi), v(raw), ACT.Copy).then_inc(whi_done, 1)
                else:
                    act.activation(w_hi[:, n % 2, :], raw[:, n % 2, :], ACT.Copy).then_inc(whi_done, 1)

            weight_hi(0)
            weight_hi(1)
            for n, (kind, j, _) in enumerate(plan):
                src = ps[n % 2][:, :, 0:SL]
                act.wait_ge(filled, n + 1)
                if n >= 2 and vector_steps[n - 2]:
                    act.wait_ge(vector_step, vector_steps[n - 2])
                if kind == "wba":
                    act.activation(whole(wba_t[:, :]), ps[n % 2][0:16, :, 0:SL], ACT.Copy).then_inc(evacuated, 1)
                elif kind == "v":
                    act.activation(whole(v_t[:, :]), src, ACT.Copy).then_inc(evacuated, 1)
                elif kind == "z":
                    i = staged.index(n)
                    act.wait_ge(stored[i % 2], 16 * (i // 2))
                    act.activation(whole(stage[:, i % 2, :]), src, ACT.Silu).then_inc(evacuated, 1)
                elif kind == "qkv":
                    act.activation(samp[:, j, :, 3:11],
                                   ps[n % 2][:, 2, PROMPT - 2 * SL:NT - 2 * SL].rearrange("p (b t) -> p b t", b=DEC_B),
                                   ACT.Copy)
                    act.activation(whole(copied[:, n % 2, :]), src, ACT.Copy).then_inc(evacuated, 1)
                else:
                    act.activation(whole(copied[:, n % 2, :]), src, ACT.Copy).then_inc(evacuated, 1)
                if n + 2 < n_blocks:
                    weight_hi(n + 2)
                if kind == "qkv":
                    act.wait_ge(vector_step, vector_steps[n])
                    act.activation(qkv_t[:, j, 0:PROMPT], qkv_t[:, j, 0:PROMPT], ACT.Silu).then_inc(silu_done, 1)

        @block.vector
        def _(dve):
            count = [0]

            def step(ins, wait=True):
                count[0] += 1
                ins.then_inc(vector_step, 1)
                if wait:
                    dve.wait_ge(vector_step, count[0])

            def weight_lo(n):
                dve.wait_ge(whi_done, n + 1)
                if plan[n][0] == "wba":
                    v = lambda b: b[:, n % 2, :].rearrange("p (k f) -> p k f", k=KT)[:, :, 0:16]
                    dve.tensor_tensor(v(w_lo), v(raw), v(w_hi).bitcast(F32), ALU.subtract).then_inc(wlo_done, 1)
                else:
                    dve.tensor_tensor(w_lo[:, n % 2, :], raw[:, n % 2, :], w_hi[:, n % 2, :].bitcast(F32),
                                      ALU.subtract).then_inc(wlo_done, 1)

            weight_lo(0)
            weight_lo(1)
            dve.wait_ge(tables_in, 32)
            for n, (kind, j, _) in enumerate(plan):
                if n + 2 < n_blocks:
                    weight_lo(n + 2)
                if kind in ("v", "wba", "z"):
                    continue
                dve.wait_ge(evacuated, n + 1)
                c = copied[:, n % 2, 0:NT]
                if kind == "qkv":
                    y = qkv_t[:, j, 0:PROMPT]
                    step(dve.tensor_copy(conv_tail[:, j, :], c[:, PROMPT - 3:PROMPT]), wait=False)
                    step(dve.tensor_scalar(y, c[:, 0:PROMPT], taps[:, j, 3:4], None, ALU.mult))
                    for back in (1, 2, 3):
                        step(dve.scalar_tensor_tensor(qkv_t[:, j, back:PROMPT], c[:, 0:PROMPT - back],
                                                      taps[:, j, 3 - back:4 - back], qkv_t[:, j, back:PROMPT],
                                                      ALU.mult, ALU.add))
                    continue
                if kind in ("k", "ki"):
                    dst = {"k": k_t, "ki": ki_t}[kind][:, 0:NT]
                else:
                    i = staged.index(n)
                    dst = stage[:, i % 2, 0:NT]
                    if i >= 2:
                        dve.wait_ge(stored[i % 2], 16 * (i // 2))
                step(dve.stream_shuffle(swapped[:, :], c, ROPE_SWAP), wait=False)
                step(dve.tensor_tensor(dst, c, cos[:, :], ALU.mult))
                step(dve.tensor_tensor(swapped[:, :], swapped[:, :], sin[:, :], ALU.mult))
                step(dve.tensor_tensor(dst, dst, swapped[:, :], ALU.add))


def projection_tail(nc, ident, ones, k_t, v_t, ki_t, wba_t, qkv_t, conv_tail, samp, taps, a_log, dt_bias,
                    v_tok, wi_tok, beta, gate, unit, k_out, v_out, ki_out, conv_out, qkv_out):
    with ExitStack() as ctx:
        sc = Scope(nc, ctx, "tail")
        k_tok = sc.sb("k_tok", [P, TILES, P])
        ki_tok = sc.sb("ki_tok", [P, TILES, HD])
        wba = sc.sb("wba", [P, TILES, 16])
        ab = sc.sb("ab", [P, 2, GH])
        sums = sc.sb("sums", [P, TILES, 8])
        sq = sc.sb("sq", [P, 2, NT])
        acc = sc.sb("acc", [P, 12, DEC_B, DEC_T])
        tmp = sc.sb("tmp", [P, 12, DEC_B, DEC_T])
        g1 = sc.sb("g1", [P, TILES, GH])
        g2 = sc.sb("g2", [P, TILES, GH])
        rows = sc.sb("rows", [27, 12 * P])
        saved = sc.sb("saved", [P, 12, 27])
        turned = sc.ps("turned", [P, 4, 4, P])
        sum_ps = sc.ps("sum_ps", [P, 512])
        wba_ps = sc.ps("wba_ps", [P, 512])
        saved_ps = sc.ps("saved_ps", [27, 2, 512])
        consts_in, turned_done, tok_done, wba_done, squared, summed, vs, act_step, stored, saved_done, rows_done, \
            conv_ready, sums_ready, roots, gate_in, saved_turned = (
                sc.sem(n) for n in ("consts_in", "turned_done", "tok_done", "wba_done", "squared", "summed",
                                    "vector_step", "act_step", "stored", "saved_done", "rows_done", "conv_ready",
                                    "sums_ready", "roots", "gate_in", "saved_turned"))
        block = ctx.enter_context(nc.Block())
        kinds = [(k_t, P, k_tok), (v_t, P, v_tok), (ki_t, HD, ki_tok)]

        @block.sync
        def _(sp):
            sp.dma_start(ab[:, 0, :], a_log.partition_broadcast(P)[:, 0, :]).then_inc(consts_in, 16)
            sp.dma_start(ab[:, 1, :], dt_bias.partition_broadcast(P)[:, 0, :]).then_inc(consts_in, 16)
            sp.wait_ge(tok_done, 3 * 3)
            for tok, (prompt, sample) in ((k_tok, k_out), (v_tok, v_out), (ki_tok, ki_out)):
                sp.dma_start(prompt.rearrange("(t p) f -> p t f", p=P), tok[:, 0:TILES - 1, :]).then_inc(stored, 16)
                sp.dma_start(sample, tok[0:SAMPLE, TILES - 1, :]).then_inc(stored, 16)
            sp.wait_ge(act_step, 1)
            for j in range(12):
                sp.dma_start(qkv_out[:, j, :], qkv_t[:, j, :]).then_inc(stored, 16)
            sp.wait_ge(rows_done, 3)
            sp.dma_start(conv_out[0], rows[0:3, :]).then_inc(stored, 16)
            sp.dma_start(conv_out[1], rows[3:27, :]).then_inc(stored, 16)
            sp.wait_ge(stored, 16 * 20)

        @block.tensor
        def _(pe):
            for t in range(TILES):
                w = tile_width(t)
                last = pe.transpose(wba_ps[0:w, t * 16:(t + 1) * 16], wba_t[:, t * P:t * P + w], ident[0:16, 0:16])
            last.then_inc(wba_done, 1)
            n = 0
            for src, width, _ in kinds:
                for lo in (0, 4, 8):
                    if n >= 4:
                        pe.wait_ge(tok_done, n - 3)
                    for t in range(lo, min(lo + 4, TILES)):
                        w = tile_width(t)
                        last = pe.transpose(turned[0:w, n % 4, t - lo, 0:width], src[0:width, t * P:t * P + w],
                                            ident[0:width, 0:width])
                    last.then_inc(turned_done, 1)
                    n += 1
            for j in range(8):
                pe.wait_ge(squared, j + 1)
                for t in range(TILES):
                    w = tile_width(t)
                    last = pe.matmul(sum_ps[0:w, t * 8 + j:t * 8 + j + 1], sq[:, j % 2, t * P:t * P + w],
                                     ones[:, 0:1], start=True, stop=True)
                last.then_inc(summed, 1)
            for g in range(3):
                pe.wait_ge(saved_done, 1)
                if g == 2:
                    pe.wait_ge(rows_done, 1)
                for j in range(4 * g, 4 * g + 4):
                    last = pe.transpose(saved_ps[:, g % 2, (j % 4) * P:(j % 4 + 1) * P], saved[:, j, :], ident[:, :])
                last.then_inc(saved_turned, 1)

        @block.scalar
        def _(act):
            n = 0
            for _, width, tok in kinds:
                for lo in (0, 4, 8):
                    act.wait_ge(turned_done, n + 1)
                    if lo < 8:
                        act.activation(tok[:, lo:lo + 4, 0:width], turned[:, n % 4, :, 0:width],
                                       ACT.Copy).then_inc(tok_done, 1)
                    else:
                        act.activation(tok[0:SAMPLE, 8, 0:width], turned[0:SAMPLE, n % 4, 0, 0:width],
                                       ACT.Copy).then_inc(tok_done, 1)
                    n += 1
            act.wait_ge(conv_ready, 1)
            act.activation(qkv_t[:, :, PROMPT:NT], acc[:, :, :, :].rearrange("p j b t -> p j (b t)"),
                           ACT.Silu).then_inc(act_step, 1)
            act.wait_ge(act_step, 1)
            for j in range(8):
                if j >= 2:
                    act.wait_ge(summed, j - 1)
                act.activation(sq[:, j % 2, :], qkv_t[:, j, :], ACT.Square).then_inc(squared, 1)
            act.wait_ge(sums_ready, 1)
            act.activation(unit[:, :, :], sums[:, :, :], ACT.Sqrt).then_inc(roots, 1)
            act.wait_ge(consts_in, 32)
            act.wait_ge(gate_in, 1)
            act.activation(ab[:, 0, :], ab[:, 0, :], ACT.Exp)
            act.activation(beta[:, :, :], wba[:, :, 8:12], ACT.Exp, scale=-1.0).then_inc(act_step, 1)
            act.activation(g2[:, :, :], g1[:, :, :], ACT.Abs).then_inc(act_step, 1)
            act.wait_ge(act_step, 3)
            act.activation(g2[:, :, :], g2[:, :, :], ACT.Exp, scale=-1.0).then_inc(act_step, 1)
            act.wait_ge(act_step, 4)
            act.activation(g2[:, :, :], g2[:, :, :], ACT.Ln, bias=1.0).then_inc(act_step, 1)

        @block.vector
        def _(dve):
            count = [0]

            def step(ins, wait=True):
                count[0] += 1
                ins.then_inc(vs, 1)
                if wait:
                    dve.wait_ge(vs, count[0])

            def tap(k):
                return taps[:, :, k:k + 1].unsqueeze(3).to_broadcast([P, 12, DEC_B, DEC_T])

            def heads(v):
                return v.unsqueeze(1).to_broadcast([P, TILES, GH])

            step(dve.memset(wba[:, :, :], 0.0), wait=False)
            step(dve.memset(sums[:, :, :], 1.0), wait=False)
            step(dve.tensor_tensor(acc[:, :, :, :], samp[:, :, :, 3:11], tap(3), ALU.mult))
            for back in (1, 2, 3):
                step(dve.tensor_tensor(tmp[:, :, :, :], samp[:, :, :, 3 - back:11 - back], tap(3 - back), ALU.mult))
                ins = dve.tensor_tensor(acc[:, :, :, :], acc[:, :, :, :], tmp[:, :, :, :], ALU.add)
                if back < 3:
                    step(ins)
                else:
                    ins.then_inc(conv_ready, 1)
            dve.tensor_copy(saved[:, :, 0:3], conv_tail[:, :, :])
            for j in range(12):
                ins = dve.tensor_copy(saved[:, j, 3:27].rearrange("p (b r) -> p b r", b=DEC_B), samp[:, j, :, 8:11])
            ins.then_inc(saved_done, 1)
            dve.wait_ge(wba_done, 1)
            w9 = wba_ps[:, 0:TILES * 16].rearrange("p (t c) -> p t c", t=TILES)
            step(dve.tensor_copy(wba[:, 0:TILES - 1, :], w9[:, 0:TILES - 1, :]), wait=False)
            step(dve.tensor_copy(wba[0:SAMPLE, TILES - 1, :], w9[0:SAMPLE, TILES - 1, :]))
            step(dve.tensor_scalar(wi_tok[:, :, :], wba[:, :, 0:8], 8.0 ** -0.5, None, ALU.mult), wait=False)
            dve.wait_ge(consts_in, 32)
            dve.tensor_tensor(g1[:, :, :], wba[:, :, 12:16], heads(ab[:, 1, :]), ALU.add).then_inc(gate_in, 1)
            dve.wait_ge(summed, 8)
            s9 = sum_ps[:, 0:TILES * 8].rearrange("p (t c) -> p t c", t=TILES)
            step(dve.tensor_scalar(sums[:, 0:TILES - 1, :], s9[:, 0:TILES - 1, :], NORM_EPS, None, ALU.add),
                 wait=False)
            dve.tensor_scalar(sums[0:SAMPLE, TILES - 1, :], s9[0:SAMPLE, TILES - 1, :], NORM_EPS, None,
                              ALU.add).then_inc(sums_ready, 1)
            dve.wait_ge(act_step, 3)
            step(dve.tensor_scalar(beta[:, :, :], beta[:, :, :], 1.0, None, ALU.add))
            step(dve.reciprocal(beta[:, :, :], beta[:, :, :]), wait=False)
            step(dve.tensor_scalar(g1[:, :, :], g1[:, :, :], 0.0, None, ALU.max))
            dve.wait_ge(act_step, 5)
            step(dve.tensor_tensor(g1[:, :, :], g1[:, :, :], g2[:, :, :], ALU.add))
            step(dve.tensor_tensor(g1[:, :, :], g1[:, :, :], heads(ab[:, 0, :]), ALU.mult))
            step(dve.tensor_scalar(gate[:, :, :], g1[:, :, :], -1.0, None, ALU.mult), wait=False)
            for g in range(3):
                dve.wait_ge(saved_turned, g + 1)
                dve.tensor_copy(rows[:, g * 512:(g + 1) * 512], saved_ps[:, g % 2, :]).then_inc(rows_done, 1)
            dve.wait_ge(roots, 1)
            step(dve.reciprocal(unit[:, :, :], unit[:, :, :]))
            step(dve.tensor_scalar(unit[:, :, 0:4], unit[:, :, 0:4], float(P) ** -0.5, None, ALU.mult))


BIG = 1e30
LEVELS = 7


def delta_masks(n, group):
    i, j = np.arange(n)[:, None], np.arange(n)[None, :]
    same = (i // group) == (j // group)
    upper = ((i <= j) & same).astype(np.float32)
    strict = np.where((i > j) & same, 0.0, -BIG).astype(np.float32)
    causal_t = np.where((i <= j) & same, 0.0, -BIG).astype(np.float32)
    levels = [((i // (2 << l) == j // (2 << l)) & (i // (1 << l) % 2 == 1) & (j // (1 << l) % 2 == 0))
              for l in range(int(np.log2(group)))]
    return upper, strict, causal_t, [m.astype(np.float32) for m in levels]


def over_heads(m):
    return m.unsqueeze(1).to_broadcast([m.shape[0], GH, m.shape[1]])


def over_cols(v, n):
    return v.unsqueeze(2).to_broadcast([v.shape[0], v.shape[1], n])


def delta_prompt(nc, ident, ones, masks, qkv_in, beta, gate, unit, state, state_out, o_out, top):
    n_chunks = PROMPT // P
    per_chunk_bits = TOP_BITS // n_chunks
    search = {"gates": [(0, "start"), (0, 5)],
              "grams": [(0, 4), (0, 3)],
              1: [(0, 2), (0, 1), (0, 0)],
              2: [(0, "end"), (1, "start"), (1, 5)],
              3: [(1, 4), (1, 3)],
              4: [(1, 2), (1, 1), (1, 0)],
              5: [(1, "end"), (2, "start"), (2, 5)],
              6: [(2, 4), (2, 3)],
              "values": [(2, 2), (2, 1), (2, 0)],
              "outputs": [(2, "end"), (3, "start"), (3, 5)],
              "state": [(3, 4), (3, 3)],
              "last": [(3, 2), (3, 1), (3, 0), (3, "end")]}
    search_act = {0: [(0, 0)], 1: [(0, 1), (0, 2)], 2: [(1, 0), (1, 1)], 3: [(1, 2)], 4: [], 5: [(2, 0), (2, 1)],
                  6: [(2, 2)], 7: [(3, 0), (3, 1), (3, 2)]}
    upper, strict, causal_t, levels = masks
    with ExitStack() as ctx:
        sc = Scope(nc, ctx, "delta")
        cur = sc.sb("cur", [P, 12, P])
        q_n, k_n, q_t, k_t, v_b, m, pt, x, y, tt, r, o1, vn, vs = (sc.sb(n, [P, GH, P]) for n in (
            "q_n", "k_n", "q_t", "k_t", "v_b", "m", "pt", "x", "y", "tt", "r", "o1", "vn", "vs"))
        gu, x1 = vs, vn
        decay = sc.sb("decay", [P, 2, GH, P])
        ml = sc.sb("ml", [P, LEVELS, GH, P])
        sums = sc.sb("sums", [P, 3, GH])
        exps = sc.sb("exps", [P, 3, GH])
        eb = sc.sb("eb", [P, GH])
        o = sc.sb("o", [P, GH, P])
        b = [sc.ps(f"b{i}", [P, GH, P]) for i in range(8)]
        pair_heads = (slice(0, 2), slice(2, 4))
        t_bank, u_bank, x_bank = (b[0], b[4]), (b[1], b[3]), (b[2], b[7])
        names = ("staged", "turned", "qk_scaled", "qk_turned", "qk_ready", "gu_ready", "gates_summed", "sums_done",
                 "exps_done", "decay_in", "decay_done", "grams_done", "m_done", "pt_done", "level_ready", "x0_done",
                 "x_turned", "y0_done", "state_read", "t_done0", "t_copied0", "u_done0", "y_upd0", "x_upd0", "t_done1",
                 "t_copied1", "u_done1", "y_upd1", "x_upd1", "r_done",
                 "o1_done", "v_done", "vn_done", "vs_done", "o2_done", "su_done", "o_done",
                 "o_stored", "state_done", "state_stored", "own", "cand_made", "act_counted")
        s = {n: sc.sem(n) for n in names}
        block = ctx.enter_context(nc.Block())

        @block.sync
        def _(sp):
            with sp.Fori(0, n_chunks) as c:
                sp.wait_ge(s["turned"], c)
                sp.dma_start(cur[:, :, :], qkv_in[:, :, bass.ts(c, P)]).then_inc(s["staged"], 16)
            sp.wait_ge(s["state_done"], n_chunks)
            sp.dma_start(state_out, state[:, :, :]).then_inc(s["state_stored"], 16)
            sp.wait_ge(s["state_stored"], 16)

        @block.gpsimd
        def _(pool):
            with pool.Fori(0, n_chunks) as c:
                pool.wait_ge(s["m_done"], c + 1)
                pool.wait_ge(s["u_done1"], c * 6)
                for l in range(LEVELS):
                    pool.tensor_tensor(ml[:, l], m[:, :, :], over_heads(levels[l]), ALU.mult
                                       ).then_inc(s["level_ready"], 1)
                pool.wait_ge(s["o_done"], c + 1)
                pool.dma_start(o_out[bass.ds(c, 1)].rearrange("o p f -> (o p) f"),
                               o[:, :, :].rearrange("p h v -> p (h v)")).then_inc(s["o_stored"], 16)
            pool.wait_ge(s["o_stored"], 16 * n_chunks)

        @block.tensor
        def _(pe):
            with pe.Fori(0, n_chunks) as c:
                pe.wait_ge(s["staged"], c * 16 + 16)
                pe.wait_ge(s["t_copied0"], c * 6)
                pe.wait_ge(s["y_upd0"], c * 6)
                pe.wait_ge(s["x_upd0"], c * 5)
                for part in range(3):
                    for h in range(GH):
                        last = pe.transpose(b[part][:, h, :], cur[:, part * GH + h, :], ident[:, :])
                last.then_inc(s["turned"], 1)
                pe.wait_ge(s["gu_ready"], c + 1)
                pe.wait_ge(s["vn_done"], c)
                pe.wait_ge(s["state_done"], c)
                pe.matmul(b[3][:, :, :], ones[:, :], gu[:, :, :], start=True, stop=True)
                pe.matmul(b[4][:, 0, 0:GH], upper[:, :], gate[:, c, :], start=True, stop=True)
                pe.matmul(b[4][:, 0, GH:2 * GH], ones[:, :], gate[:, c, :], start=True,
                          stop=True).then_inc(s["gates_summed"], 1)
                pe.wait_ge(s["qk_scaled"], c * 2 + 2)
                for h in range(GH):
                    pe.transpose(b[0][:, h, :], q_n[:, h, :], ident[:, :])
                for h in range(GH):
                    last = pe.transpose(b[1][:, h, :], k_n[:, h, :], ident[:, :])
                last.then_inc(s["qk_turned"], 1)
                pe.wait_ge(s["qk_ready"], c * 2 + 2)
                pe.wait_ge(s["r_done"], c)
                pe.wait_ge(s["o1_done"], c)
                for h in range(GH):
                    pe.matmul(b[5][:, h, :], k_t[:, h, :], k_t[:, h, :], start=True, stop=True)
                for h in range(GH):
                    last = pe.matmul(b[6][:, h, :], k_t[:, h, :], q_t[:, h, :], start=True, stop=True)
                last.then_inc(s["grams_done"], 1)
                pe.wait_ge(s["x0_done"], c + 1)
                for h in range(GH):
                    last = pe.transpose(b[0][:, h, :], x[:, h, :], ident[:, :])
                last.then_inc(s["x_turned"], 1)
                pe.wait_ge(s["m_done"], c + 1)
                pe.wait_ge(s["pt_done"], c + 1)
                for h in range(GH):
                    pe.matmul(b[5][:, h, :], k_t[:, h, :], state[:, h, :], start=True, stop=True)
                for h in range(GH):
                    last = pe.matmul(b[6][:, h, :], q_t[:, h, :], state[:, h, :], start=True, stop=True)
                last.then_inc(s["state_read"], 1)
                for l in range(1, LEVELS):
                    pe.wait_ge(s["level_ready"], c * 7 + l + 1)
                    for g in range(2):
                        if l == 1:
                            pe.wait_ge(s["y0_done"], c + 1)
                            pe.wait_ge(s["sums_done"], c + 1)
                        else:
                            pe.wait_ge(s[f"y_upd{g}"], c * 6 + l - 1)
                            pe.wait_ge(s[f"x_upd{g}"], c * 5 + l - 1)
                        for h in (2 * g, 2 * g + 1):
                            last = pe.matmul(t_bank[g][:, h, :], ml[:, l, h, :], y[:, h, :], start=True, stop=True)
                        last.then_inc(s[f"t_done{g}"], 1)
                    if l == 1:
                        pe.wait_ge(s["decay_in"], c + 1)
                        pe.wait_ge(s["o_done"], c)
                    for g in range(2):
                        pe.wait_ge(s[f"t_copied{g}"], c * 6 + l)
                        for h in (2 * g, 2 * g + 1):
                            last = pe.matmul(u_bank[g][:, h, :], x[:, h, :], tt[:, h, :], start=True, stop=True)
                            if l < LEVELS - 1:
                                last = pe.matmul(x_bank[g][:, h, :], tt[:, h, :], x[:, h, :], start=True, stop=True)
                        last.then_inc(s[f"u_done{g}"], 1)
                pe.wait_ge(s["y_upd0"], c * 6 + 6)
                pe.wait_ge(s["y_upd1"], c * 6 + 6)
                pe.wait_ge(s["r_done"], c + 1)
                for h in range(GH):
                    last = pe.matmul(b[3][:, h, :], y[:, h, :], r[:, h, :], start=True, stop=True)
                last.then_inc(s["v_done"], 1)
                pe.wait_ge(s["vn_done"], c + 1)
                pe.wait_ge(s["x_upd1"], c * 5 + 5)
                for h in range(GH):
                    last = pe.matmul(b[7][:, h, :], pt[:, h, :], vn[:, h, :], start=True, stop=True)
                last.then_inc(s["o2_done"], 1)
                pe.wait_ge(s["vs_done"], c + 1)
                pe.wait_ge(s["t_copied1"], c * 6 + 6)
                for h in range(GH):
                    last = pe.matmul(b[4][:, h, :], k_n[:, h, :], vs[:, h, :], start=True, stop=True)
                last.then_inc(s["su_done"], 1)

        @block.scalar
        def _(act):
            with act.Fori(0, n_chunks) as c:
                def count_parts(place):
                    for k, part in search_act[place]:
                        top.count_act(act, c * per_chunk_bits + k, part, s["cand_made"], s["act_counted"])

                act.wait_ge(s["sums_done"], c + 1)
                act.activation(exps[:, :, :], sums[:, :, :], ACT.Exp).then_inc(s["exps_done"], 1)
                act.wait_ge(s["qk_turned"], c + 1)
                act.wait_ge(s["state_read"], c)
                act.activation(q_t[:, :, :], b[0][:, :, :], ACT.Copy).then_inc(s["qk_ready"], 1)
                act.activation(k_t[:, :, :], b[1][:, :, :], ACT.Copy).then_inc(s["qk_ready"], 1)
                act.wait_ge(s["decay_in"], c + 1)
                act.activation(decay[:, :, :, :], decay[:, :, :, :], ACT.Exp).then_inc(s["decay_done"], 1)
                act.wait_ge(s["x_turned"], c + 1)
                act.wait_ge(s["v_done"], c)
                act.activation(y[:, :, :], b[0][:, :, :], ACT.Copy).then_inc(s["y0_done"], 1)
                count_parts(0)
                for l in range(1, LEVELS):
                    for g, heads in enumerate(pair_heads):
                        act.wait_ge(s[f"t_done{g}"], c * 6 + l)
                        act.wait_ge(s[f"u_done{g}"], c * 6 + l - 1)
                        act.activation(tt[:, heads, :], t_bank[g][:, heads, :], ACT.Copy
                                       ).then_inc(s[f"t_copied{g}"], 1)
                    count_parts(l)
                act.wait_ge(s["v_done"], c + 1)
                act.wait_ge(s["o2_done"], c)
                act.activation(vn[:, :, :], b[3][:, :, :], ACT.Copy).then_inc(s["vn_done"], 1)
                count_parts(7)

        @block.vector
        def _(dve):
            per_chunk = 26
            with dve.Fori(0, n_chunks) as c:
                count = [0]

                def own(ins):
                    count[0] += 1
                    ins.then_inc(s["own"], 1)
                    dve.wait_ge(s["own"], c * per_chunk + count[0])

                def search_at(place):
                    for k, what in search[place]:
                        bit = c * per_chunk_bits + k
                        if what == "start":
                            top.start(dve, bit, s["cand_made"])
                        elif what == "end":
                            top.finish(dve, bit, own, s["act_counted"])
                        elif what == 0:
                            own(top.compare(dve, [what], top.candidates, ALU.is_ge))
                        else:
                            top.compare(dve, [what], top.candidates, ALU.is_ge)

                dve.wait_ge(s["su_done"], c)
                dve.wait_ge(s["o_done"], c)
                dve.tensor_tensor(gu[:, :, :], over_heads(upper[:, :]), over_cols(gate[:, c, :], P), ALU.mult
                                  ).then_inc(s["gu_ready"], 1)
                search_at("gates")
                dve.wait_ge(s["turned"], c + 1)
                dve.tensor_tensor(q_n[:, :, :], b[0][:, :, :], over_cols(unit[:, c, 0:GH], P), ALU.mult
                                  ).then_inc(s["qk_scaled"], 1)
                dve.tensor_tensor(k_n[:, :, :], b[1][:, :, :], over_cols(unit[:, c, GH:2 * GH], P), ALU.mult
                                  ).then_inc(s["qk_scaled"], 1)
                dve.tensor_tensor(v_b[:, :, :], b[2][:, :, :], over_cols(beta[:, c, :], P), ALU.mult)
                dve.wait_ge(s["gates_summed"], c + 1)
                own(dve.tensor_copy(sums[:, 0:2, :], b[4][:, 0, 0:2 * GH].rearrange("p (a h) -> p a h", a=2)))
                dve.tensor_tensor(sums[:, 2, :], sums[:, 1, :], sums[:, 0, :], ALU.subtract
                                  ).then_inc(s["sums_done"], 1)
                own(dve.tensor_tensor(x1[:, :, :], b[3][:, :, :], over_cols(sums[:, 0, :], P), ALU.subtract))
                dve.tensor_tensor(decay[:, 1], x1[:, :, :], over_heads(causal_t[:, :]), ALU.add)
                dve.scalar_tensor_tensor(decay[:, 0], x1[:, :, :], -1.0, over_heads(strict[:, :]),
                                         ALU.mult, ALU.add).then_inc(s["decay_in"], 1)
                dve.wait_ge(s["exps_done"], c + 1)
                own(dve.tensor_tensor(eb[:, :], exps[:, 0, :], beta[:, c, :], ALU.mult))
                search_at("grams")
                dve.wait_ge(s["grams_done"], c + 1)
                dve.wait_ge(s["decay_done"], c + 1)
                dve.wait_ge(s["level_ready"], c * 7)
                own(dve.tensor_tensor(m[:, :, :], b[5][:, :, :], decay[:, 0], ALU.mult))
                dve.tensor_tensor(m[:, :, :], m[:, :, :], over_cols(beta[:, c, :], P), ALU.mult
                                  ).then_inc(s["m_done"], 1)
                dve.tensor_tensor(pt[:, :, :], b[6][:, :, :], decay[:, 1], ALU.mult).then_inc(s["pt_done"], 1)
                dve.wait_ge(s["level_ready"], c * 7 + 1)
                dve.tensor_tensor(x[:, :, :], over_heads(ident[:, :]), ml[:, 0], ALU.subtract
                                  ).then_inc(s["x0_done"], 1)
                dve.wait_ge(s["state_read"], c + 1)
                own(dve.tensor_tensor(r[:, :, :], b[5][:, :, :], over_cols(eb[:, :], P), ALU.mult))
                dve.tensor_tensor(r[:, :, :], v_b[:, :, :], r[:, :, :], ALU.subtract).then_inc(s["r_done"], 1)
                dve.tensor_tensor(o1[:, :, :], b[6][:, :, :], over_cols(exps[:, 0, :], P), ALU.mult
                                  ).then_inc(s["o1_done"], 1)
                own(dve.tensor_tensor(state[:, :, :], state[:, :, :], over_cols(exps[:, 1, :], P), ALU.mult))
                for l in range(1, LEVELS):
                    search_at(l)
                    for g, heads in enumerate(pair_heads):
                        if l == 1:
                            dve.wait_ge(s["y0_done"], c + 1)
                            dve.wait_ge(s["x0_done"], c + 1)
                        else:
                            dve.wait_ge(s[f"y_upd{g}"], c * 6 + l - 1)
                            dve.wait_ge(s[f"x_upd{g}"], c * 5 + l - 1)
                        dve.wait_ge(s[f"u_done{g}"], c * 6 + l)
                        dve.tensor_tensor(y[:, heads, :], y[:, heads, :], u_bank[g][:, heads, :], ALU.subtract
                                          ).then_inc(s[f"y_upd{g}"], 1)
                        if l < LEVELS - 1:
                            dve.tensor_tensor(x[:, heads, :], x[:, heads, :], x_bank[g][:, heads, :], ALU.subtract
                                              ).then_inc(s[f"x_upd{g}"], 1)
                search_at("values")
                dve.wait_ge(s["vn_done"], c + 1)
                dve.tensor_tensor(vs[:, :, :], vn[:, :, :], over_cols(exps[:, 2, :], P), ALU.mult
                                  ).then_inc(s["vs_done"], 1)
                search_at("outputs")
                dve.wait_ge(s["o2_done"], c + 1)
                dve.wait_ge(s["o_stored"], c * 16)
                dve.tensor_tensor(o[:, :, :], o1[:, :, :], b[7][:, :, :], ALU.add).then_inc(s["o_done"], 1)
                search_at("state")
                dve.wait_ge(s["su_done"], c + 1)
                dve.tensor_tensor(state[:, :, :], state[:, :, :], b[4][:, :, :], ALU.add
                                  ).then_inc(s["state_done"], 1)
                search_at("last")
                assert count[0] == per_chunk, count


def delta_sample(nc, ident, ones, masks, same, member, qkv_in, beta, gate, unit, state_in, state_out, o_out):
    n, t0 = SAMPLE, TILES - 1
    cols = slice(PROMPT, NT)
    upper, strict, causal_t, levels = masks
    with ExitStack() as ctx:
        sc = Scope(nc, ctx, "sdelta")
        state = sc.sb("state", [P, DEC_B, GH, P])
        cur = sc.sb("cur", [P, 12, SAMPLE])
        o = sc.sb("o", [n, GH, P])
        q_n, k_n, v_b, r, o1, vn, vs = (sc.sb(i, [n, GH, P]) for i in ("q_n", "k_n", "v_b", "r", "o1", "vn", "vs"))
        q_t, k_t, ks_t, qs_t = (sc.sb(i, [P, GH, n]) for i in ("q_t", "k_t", "ks_t", "qs_t"))
        gu, x1, m, pt, x, y, tt = (sc.sb(i, [n, GH, n]) for i in ("gu", "x1", "m", "pt", "x", "y", "tt"))
        gm = sc.sb("gm", [n, DEC_B, GH])
        decay = sc.sb("decay", [n, 2, GH, n])
        ml = sc.sb("ml", [n, 3, GH, n])
        sums, exps = sc.sb("sums", [n, 3, GH]), sc.sb("exps", [n, 3, GH])
        totals = sc.sb("totals", [P, DEC_B * GH])
        eb = sc.sb("eb", [n, GH])
        vsb = sc.sb("vsb", [n, 2, DEC_B, P])
        wide = sc.ps("wide", [P, 2, DEC_B, P])
        b = [wide[:, 0, 0:4, :], wide[:, 0, 4:8, :], wide[:, 1, 0:4, :], wide[:, 1, 4:8, :]] + \
            [sc.ps(f"b{i}", [P, GH, P])[:, :, :] for i in range(4)]
        s = Named(sc)
        block = ctx.enter_context(nc.Block())
        state_rows = state[:, :, :, :].rearrange("p b h v -> p (b h) v")

        @block.sync
        def _(sp):
            sp.dma_start(cur[:, :, :], qkv_in[:, :, cols]).then_inc(s["staged"], 16)
            sp.dma_start(state_rows, state_in.rearrange("b h k v -> k (b h) v")).then_inc(s["state_loaded"], 16)
            sp.wait_ge(s["o_done"], 1)
            sp.dma_start(o_out, o[:, :, :].rearrange("p h v -> p (h v)")).then_inc(s["stored"], 16)
            sp.wait_ge(s["state_added"], GH)
            sp.dma_start(state_out.rearrange("b h k v -> k (b h) v"), state_rows).then_inc(s["stored"], 16)
            sp.wait_ge(s["stored"], 32)

        @block.tensor
        def _(pe):
            pe.wait_ge(s["staged"], 16)
            for part in range(3):
                for h in range(GH):
                    last = pe.transpose(b[part][0:n, h, :], cur[:, part * GH + h, :], ident[:, :])
            last.then_inc(s["turned"], 1)
            pe.wait_ge(s["gu_ready"], 1)
            pe.matmul(b[3][0:n, :, 0:n], ones[0:n, 0:n], gu[:, :, :], start=True, stop=True)
            pe.matmul(b[4][0:n, 0, 0:GH], upper, gate[0:n, t0, :], start=True, stop=True)
            pe.matmul(b[4][0:n, 0, GH:2 * GH], same, gate[0:n, t0, :], start=True, stop=True)
            pe.matmul(b[4][:, 1, 0:DEC_B * GH], ones[0:n, :], gm[:, :, :].rearrange("p b h -> p (b h)"),
                      start=True, stop=True).then_inc(s["gates_summed"], 1)
            pe.wait_ge(s["scaled"], 3)
            for h in range(GH):
                pe.transpose(b[0][:, h, 0:n], q_n[:, h, :], ident[0:n, 0:n])
            for h in range(GH):
                last = pe.transpose(b[1][:, h, 0:n], k_n[:, h, :], ident[0:n, 0:n])
            last.then_inc(s["qk_turned"], 1)
            pe.wait_ge(s["qk_ready"], 2)
            for h in range(GH):
                pe.matmul(b[5][0:n, h, 0:n], k_t[:, h, :], k_t[:, h, :], start=True, stop=True)
            for h in range(GH):
                last = pe.matmul(b[6][0:n, h, 0:n], k_t[:, h, :], q_t[:, h, :], start=True, stop=True)
            last.then_inc(s["grams_done"], 1)
            pe.wait_ge(s["state_loaded"], 16)
            for i in range(DEC_B):
                ts = slice(i * DEC_T, (i + 1) * DEC_T)
                for h in range(GH):
                    pe.matmul(b[2][:, h, ts], state[:, i, h, :], k_t[:, h, ts], start=True, stop=True)
                    last = pe.matmul(b[7][:, h, ts], state[:, i, h, :], q_t[:, h, ts], start=True, stop=True)
            last.then_inc(s["state_read"], 1)
            pe.wait_ge(s["x0_done"], 1)
            for h in range(GH):
                last = pe.transpose(b[0][0:n, h, 0:n], x[:, h, :], ident[0:n, 0:n])
            last.then_inc(s["x_turned"], 1)
            pe.wait_ge(s["reads_copied"], 2)
            pe.wait_ge(s["pt_done"], 1)
            for h in range(GH):
                pe.transpose(b[5][0:n, h, :], ks_t[:, h, :], ident[:, :])
            for h in range(GH):
                last = pe.transpose(b[6][0:n, h, :], qs_t[:, h, :], ident[:, :])
            last.then_inc(s["reads_turned"], 1)
            pe.wait_ge(s["y0_done"], 1)
            pe.wait_ge(s["sums_done"], 1)
            for l in (1, 2):
                pe.wait_ge(s["level_ready"], l + 1)
                if l == 2:
                    pe.wait_ge(s["xy_upd"], 2)
                for h in range(GH):
                    last = pe.matmul(b[0][0:n, h, 0:n], ml[:, l, h, :], y[:, h, :], start=True, stop=True)
                last.then_inc(s["t_done"], 1)
                pe.wait_ge(s["t_copied"], l)
                for h in range(GH):
                    pe.matmul(b[1][0:n, h, 0:n], x[:, h, :], tt[:, h, :], start=True, stop=True)
                for h in range(GH):
                    last = pe.matmul(b[4][0:n, h, 0:n], tt[:, h, :], x[:, h, :], start=True, stop=True)
                last.then_inc(s["u_done"], 1)
            pe.wait_ge(s["xy_upd"], 4)
            pe.wait_ge(s["r_done"], 1)
            for h in range(GH):
                last = pe.matmul(b[3][0:n, h, :], y[:, h, :], r[:, h, :], start=True, stop=True)
            last.then_inc(s["v_done"], 1)
            pe.wait_ge(s["vn_done"], 1)
            for h in range(GH):
                last = pe.matmul(b[5][0:n, h, :], pt[:, h, :], vn[:, h, :], start=True, stop=True)
            last.then_inc(s["o2_done"], 1)
            for h in range(GH):
                pe.wait_ge(s["masked"], h + 1)
                if h >= 2:
                    pe.wait_ge(s["state_added"], h - 1)
                for half in range(2):
                    last = pe.matmul(wide[:, h % 2, 4 * half:4 * half + 4, :], k_n[:, h, :],
                                     vsb[:, h % 2, 4 * half:4 * half + 4, :], start=True, stop=True)
                last.then_inc(s["su_done"], 1)

        @block.scalar
        def _(act):
            act.wait_ge(s["sums_done"], 1)
            act.activation(exps[:, :, :], sums[:, :, :], ACT.Exp)
            act.activation(totals[:, :], totals[:, :], ACT.Exp).then_inc(s["exps_done"], 1)
            act.wait_ge(s["qk_turned"], 1)
            act.activation(q_t[:, :, :], b[0][:, :, 0:n], ACT.Copy).then_inc(s["qk_ready"], 1)
            act.activation(k_t[:, :, :], b[1][:, :, 0:n], ACT.Copy).then_inc(s["qk_ready"], 1)
            act.wait_ge(s["decay_in"], 1)
            act.activation(decay[:, :, :, :], decay[:, :, :, :], ACT.Exp).then_inc(s["decay_done"], 1)
            act.wait_ge(s["state_read"], 1)
            act.activation(ks_t[:, :, :], b[2][:, :, 0:n], ACT.Copy).then_inc(s["reads_copied"], 1)
            act.activation(qs_t[:, :, :], b[7][:, :, 0:n], ACT.Copy).then_inc(s["reads_copied"], 1)
            act.wait_ge(s["x_turned"], 1)
            act.activation(y[:, :, :], b[0][0:n, :, 0:n], ACT.Copy).then_inc(s["y0_done"], 1)
            for l in (1, 2):
                act.wait_ge(s["t_done"], l)
                if l == 2:
                    act.wait_ge(s["u_done"], 1)
                act.activation(tt[:, :, :], b[0][0:n, :, 0:n], ACT.Copy).then_inc(s["t_copied"], 1)
            act.wait_ge(s["v_done"], 1)
            act.activation(vn[:, :, :], b[3][0:n, :, :], ACT.Copy).then_inc(s["vn_done"], 1)

        @block.vector
        def _(dve):
            count = [0]

            def own(ins):
                count[0] += 1
                ins.then_inc(s["own"], 1)
                dve.wait_ge(s["own"], count[0])

            g = gate[0:n, t0, :]
            own(dve.tensor_tensor(gm[:, :, :], g.unsqueeze(1).to_broadcast([n, DEC_B, GH]), over_cols(member, GH),
                                  ALU.mult))
            dve.tensor_tensor(gu[:, :, :], over_heads(upper), over_cols(g, n), ALU.mult).then_inc(s["gu_ready"], 1)
            dve.wait_ge(s["turned"], 1)
            for dst, src, scale in ((q_n, b[0], unit[0:n, t0, 0:GH]), (k_n, b[1], unit[0:n, t0, GH:2 * GH]),
                                    (v_b, b[2], beta[0:n, t0, :])):
                dve.tensor_tensor(dst[:, :, :], src[0:n], over_cols(scale, P), ALU.mult).then_inc(s["scaled"], 1)
            dve.wait_ge(s["gates_summed"], 1)
            dve.tensor_copy(totals[:, :], b[4][:, 1, 0:DEC_B * GH])
            own(dve.tensor_copy(sums[:, 0:2, :], b[4][0:n, 0, 0:2 * GH].rearrange("p (a h) -> p a h", a=2)))
            dve.tensor_tensor(sums[:, 2, :], sums[:, 1, :], sums[:, 0, :], ALU.subtract).then_inc(s["sums_done"], 1)
            own(dve.tensor_tensor(x1[:, :, :], b[3][0:n, :, 0:n], over_cols(sums[:, 0, :], n), ALU.subtract))
            dve.tensor_tensor(decay[:, 1], x1[:, :, :], over_heads(causal_t), ALU.add)
            dve.scalar_tensor_tensor(decay[:, 0], x1[:, :, :], -1.0, over_heads(strict), ALU.mult, ALU.add
                                     ).then_inc(s["decay_in"], 1)
            dve.wait_ge(s["exps_done"], 1)
            own(dve.tensor_tensor(eb[:, :], exps[:, 0, :], beta[0:n, t0, :], ALU.mult))
            dve.wait_ge(s["grams_done"], 1)
            dve.wait_ge(s["decay_done"], 1)
            own(dve.tensor_tensor(m[:, :, :], b[5][0:n, :, 0:n], decay[:, 0], ALU.mult))
            own(dve.tensor_tensor(m[:, :, :], m[:, :, :], over_cols(beta[0:n, t0, :], n), ALU.mult))
            dve.tensor_tensor(pt[:, :, :], b[6][0:n, :, 0:n], decay[:, 1], ALU.mult).then_inc(s["pt_done"], 1)
            for l in range(3):
                dve.tensor_tensor(ml[:, l], m[:, :, :], over_heads(levels[l]), ALU.mult
                                  ).then_inc(s["level_ready"], 1)
            dve.wait_ge(s["level_ready"], 3)
            dve.tensor_tensor(x[:, :, :], over_heads(ident[0:n, 0:n]), ml[:, 0], ALU.subtract
                              ).then_inc(s["x0_done"], 1)
            dve.wait_ge(s["reads_turned"], 1)
            own(dve.tensor_tensor(r[:, :, :], b[5][0:n], over_cols(eb[:, :], P), ALU.mult))
            dve.tensor_tensor(r[:, :, :], v_b[:, :, :], r[:, :, :], ALU.subtract).then_inc(s["r_done"], 1)
            own(dve.tensor_tensor(o1[:, :, :], b[6][0:n], over_cols(exps[:, 0, :], P), ALU.mult))
            own(dve.tensor_tensor(state_rows, state_rows, over_cols(totals[:, :], P), ALU.mult))
            for l in (1, 2):
                dve.wait_ge(s["u_done"], l)
                dve.tensor_tensor(y[:, :, :], y[:, :, :], b[1][0:n, :, 0:n], ALU.subtract).then_inc(s["xy_upd"], 1)
                dve.tensor_tensor(x[:, :, :], x[:, :, :], b[4][0:n, :, 0:n], ALU.subtract).then_inc(s["xy_upd"], 1)
                dve.wait_ge(s["xy_upd"], 2 * l)
            dve.wait_ge(s["vn_done"], 1)
            own(dve.tensor_tensor(vs[:, :, :], vn[:, :, :], over_cols(exps[:, 2, :], P), ALU.mult))
            dve.wait_ge(s["o2_done"], 1)
            dve.tensor_tensor(o[:, :, :], o1[:, :, :], b[5][0:n], ALU.add).then_inc(s["o_done"], 1)
            for h in range(GH + 2):
                if h < GH:
                    if h >= 2:
                        dve.wait_ge(s["su_done"], h - 1)
                    dve.tensor_tensor(vsb[:, h % 2], vs[:, h, :].unsqueeze(1).to_broadcast([n, DEC_B, P]),
                                      over_cols(member, P), ALU.mult).then_inc(s["masked"], 1)
                if h >= 1 and h - 1 < GH:
                    g_ = h - 1
                    dve.wait_ge(s["su_done"], g_ + 1)
                    dve.tensor_tensor(state[:, :, g_, :], state[:, :, g_, :], wide[:, g_ % 2], ALU.add
                                      ).then_inc(s["state_added"], 1)


def delta_finish(nc, ident, norm_w, z_in, o_in, mix_hi, mix_lo):
    with ExitStack() as ctx:
        sc = Scope(nc, ctx, "fin")
        o_all = sc.sb("o_all", [P, TILES, GH, P])
        sq = sc.sb("sq", [P, 2, GH, P])
        ms = sc.sb("ms", [P, TILES, GH])
        nw = sc.sb("nw", [P, 1])
        z = sc.sb("z", [P, GH, TP])
        b = sc.ps("turned", [P, 4, GH, P])
        s = Named(sc)
        block = ctx.enter_context(nc.Block())

        @block.sync
        def _(sp):
            with nc.allow_non_contiguous_dma(reason="128 weights"):
                sp.dma_start(nw[:, :], norm_w.rearrange("o p -> p o")).then_inc(s["nw_in"], 16)
            for t in range(TILES):
                w = tile_width(t)
                sp.dma_start(o_all[0:w, t].rearrange("p h v -> p (h v)"), o_in[t, 0:w]).then_inc(s["o_in"], 16)
            for h in range(GH):
                sp.dma_start(z[:, h, 0:NT], z_in[h]).then_inc(s["z_in"], 16)

        @block.scalar
        def _(act):
            act.wait_ge(s["means"], 1)
            act.activation(ms[:, :, :], ms[:, :, :], ACT.Sqrt).then_inc(s["roots"], 1)
            for h in range(GH):
                act.wait_ge(s["gated"], TILES)
                act.activation(mix_hi[:, GH + h, :], z[:, h, :], ACT.Copy).then_inc(s["hi_done"], 1)

        @block.tensor
        def _(pe):
            for t in range(TILES):
                w = tile_width(t)
                pe.wait_ge(s["scaled"], t + 1)
                if t >= 4:
                    pe.wait_ge(s["gated"], t - 3)
                for h in range(GH):
                    last = pe.transpose(b[:, t % 4, h, 0:w], o_all[0:w, t, h, :], ident[0:w, 0:w])
                last.then_inc(s["turned"], 1)

        @block.vector
        def _(dve):
            count = [0]

            def own(ins):
                count[0] += 1
                ins.then_inc(s["own"], 1)
                dve.wait_ge(s["own"], count[0])

            own(dve.memset(o_all[SAMPLE:P, TILES - 1], 1.0))
            own(dve.memset(z[:, :, NT:TP], 0.0))
            dve.wait_ge(s["o_in"], 16 * TILES)
            for t in range(TILES):
                own(dve.tensor_tensor(sq[:, t % 2], o_all[:, t], o_all[:, t], ALU.mult))
                own(dve.tensor_reduce(ms[:, t, :], sq[:, t % 2], AX.X, ALU.add))
            dve.tensor_scalar(ms[:, :, :], ms[:, :, :], 1.0 / P, NORM_EPS, ALU.mult, ALU.add).then_inc(s["means"], 1)
            dve.wait_ge(s["roots"], 1)
            own(dve.reciprocal(ms[:, :, :], ms[:, :, :]))
            dve.wait_ge(s["nw_in"], 16)
            dve.wait_ge(s["z_in"], 16 * GH)
            for t in range(TILES + 1):
                if t < TILES:
                    dve.tensor_tensor(o_all[:, t], o_all[:, t], over_cols(ms[:, t, :], P), ALU.mult
                                      ).then_inc(s["scaled"], 1)
                if t >= 1:
                    u, w = t - 1, tile_width(t - 1)
                    dve.wait_ge(s["turned"], t)
                    zt = z[:, :, u * P:u * P + w]
                    dve.scalar_tensor_tensor(zt, b[:, u % 4, :, 0:w], nw[:, 0:1], zt, ALU.mult, ALU.mult
                                             ).then_inc(s["gated"], 1)
            for h in range(GH):
                dve.wait_ge(s["hi_done"], h + 1)
                dve.tensor_tensor(mix_lo[:, GH + h, :], z[:, h, :], mix_hi[:, GH + h, :].bitcast(F32),
                                  ALU.subtract)


TOPK = 256
PAST = 4096
PAGES = 32
N_POOL = 320
KEYS = PAST + DEC_T
LOWEST = -3e38
TOP_TILES = list(range(2, TILES - 1))
WIDTHS = [(t + 1) * P for t in TOP_TILES]
STARTS = [sum(WIDTHS[:i]) for i in range(len(WIDTHS))]


def index_prompt(nc, q_in, ki_t, wi_tok, causal, qi, scores):
    with ExitStack() as ctx:
        sc = Scope(nc, ctx, "ixp")
        rel = sc.sb("rel", [P, 3, PROMPT])
        ps = sc.ps("ps", [P, 3, PROMPT])
        s = Named(sc)
        block = ctx.enter_context(nc.Block())
        work = [(t, h) for t in TOP_TILES for h in range(8)]

        @block.sync
        def _(sp):
            for j in range(4):
                sp.dma_start(qi[:, j, :], q_in[j]).then_inc(s["qi_in"], 16)

        @block.tensor
        def _(pe):
            pe.wait_ge(s["qi_in"], 64)
            for n, (t, h) in enumerate(work):
                rows = slice(h % 2 * HD, h % 2 * HD + HD)
                if n >= 3:
                    pe.wait_ge(s["rectified"], n - 2)
                for lo in range(0, (t + 1) * P, 512):
                    hi = min(lo + 512, (t + 1) * P)
                    last = pe.matmul(ps[:, n % 3, lo:hi], qi[rows, h // 2, t * P:(t + 1) * P], ki_t[rows, lo:hi],
                                     start=True, stop=True)
                last.then_inc(s["dotted"], 1)

        @block.scalar
        def _(act):
            for n, (t, h) in enumerate(work):
                act.wait_ge(s["dotted"], n + 1)
                if n >= 3:
                    act.wait_ge(s["summed"], n - 2)
                act.activation(rel[:, n % 3, 0:(t + 1) * P], ps[:, n % 3, 0:(t + 1) * P], ACT.Relu,
                               scale=HD ** -0.5).then_inc(s["rectified"], 1)

        @block.vector
        def _(dve):
            for n, (t, h) in enumerate(work):
                w = (t + 1) * P
                out = scores[:, STARTS[t - 2]:STARTS[t - 2] + w]
                dve.wait_ge(s["rectified"], n + 1)
                if h == 0:
                    dve.tensor_scalar(out, rel[:, n % 3, 0:w], wi_tok[:, t, 0:1], None, ALU.mult
                                      ).then_inc(s["summed"], 1)
                else:
                    dve.wait_ge(s["summed"], n)
                    dve.scalar_tensor_tensor(out, rel[:, n % 3, 0:w], wi_tok[:, t, h:h + 1], out,
                                             ALU.mult, ALU.add).then_inc(s["summed"], 1)
                if h == 7:
                    dve.wait_ge(s["summed"], n + 1)
                    diag = scores[:, STARTS[t - 2] + t * P:STARTS[t - 2] + w]
                    dve.tensor_tensor(diag, diag, causal, ALU.add)


def own_chain(eng, s, name):
    count = [0]

    def own(ins):
        count[0] += 1
        ins.then_inc(s[name], 1)
        eng.wait_ge(s[name], count[0])

    return own


def sample_tables():
    bt, row = np.arange(SAMPLE), np.arange(P)
    sel = np.stack([((bt[:, None] // DEC_T == 2 * p + row[None, :] // SAMPLE) &
                     (bt[:, None] % DEC_T == row[None, :] % DEC_T)) for p in range(4)], 1).astype(np.float32)
    head_of = (row[:, None] // DEC_T % 8 == np.arange(8)[None, :]).astype(np.float32)
    later = np.where(np.arange(DEC_T)[None, :] > bt[:, None] % DEC_T, LOWEST, 0.0).astype(np.float32)
    return sel, np.ascontiguousarray(sel.transpose(2, 1, 0)), head_of, later


def load_page(eng, cache, pages, slot, dst, sem):
    page = eng.value_load(pages[0:1, bass.ds(slot, 1)])
    eng.dma_start(dst, cache[0, bass.ds(page, 1)].rearrange("o p ... -> (o p) ...")).then_inc(sem, 16)


def index_sample(nc, ident, cache_kidx, qi, ki_t, wi_tok, sel, sel_t, head_of, later, pages, scores):
    pairs, chunks = DEC_B // 2, PAGES // 4
    with ExitStack() as ctx:
        sc = Scope(nc, ctx, "ixs")
        raw = sc.sb("raw", [P, pairs, 4, P])
        kt = sc.sb("kt", [P, 2, 512])
        rel = sc.sb("rel", [P, 2, 512])
        qd = sc.sb("qd", [P, pairs, 2, 8, DEC_T])
        kn = sc.sb("kn", [P, pairs, DEC_T])
        wpick = sc.sb("wpick", [P, pairs, 8])
        wcol = sc.sb("wcol", [P, pairs])
        wsel = sc.sb("wsel", [P, pairs, SAMPLE])
        turned = sc.ps("turned", [P, 2, 512])
        dots = sc.ps("dots", [P, 2, 512])
        total = sc.ps("total", [P, 512])
        small = sc.ps("small", [P, pairs, 8])
        s = Named(sc)
        block = ctx.enter_context(nc.Block())

        share = {"sp": [(0, 0), (0, 1), (0, 2)], "pool": [(0, 3), (1, 0), (1, 1)], "act": [(1, 2), (1, 3)]}

        def load_step(eng, who, c, p, first=False):
            if not first:
                eng.wait_ge(s["turned"], c * pairs + p - pairs + 1)
            for b2, g in share[who]:
                load_page(eng, cache_kidx, pages, (p * 2 + b2) * PAGES + c * 4 + g,
                          raw[:, p, g, b2 * HD:(b2 + 1) * HD], s[f"raw_in_{who}{p}"])

        def load_all(eng, who):
            for p in range(pairs):
                load_step(eng, who, 0, p, first=True)
            with eng.Fori(1, chunks) as c:
                for p in range(pairs):
                    load_step(eng, who, c, p)

        @block.sync
        def _(sp):
            load_all(sp, "sp")

        @block.gpsimd
        def _(pool):
            load_all(pool, "pool")

        @block.tensor
        def _(pe):
            for p in range(pairs):
                last = pe.matmul(small[:, p, :], sel[:, p, :], wi_tok[0:SAMPLE, TILES - 1, :], start=True, stop=True)
            last.then_inc(s["picked"], 1)
            pe.wait_ge(s["tables_made"], 1)

            def weigh(n, p):
                pe.wait_ge(s["rectified"], n + 1)
                pe.matmul(total[0:SAMPLE, :], wsel[:, p, :], rel[:, p % 2, :], start=p == 0, stop=p == pairs - 1
                          ).then_inc(s["weighed"], 1)

            with pe.Fori(0, chunks) as c:
                for p in range(pairs):
                    n = c * pairs + p
                    for who, which in share.items():
                        pe.wait_ge(s[f"raw_in_{who}{p}"], (c + 1) * 16 * len(which))
                    if p >= 2:
                        pe.wait_ge(s["kt_copied"], n - 1)
                    else:
                        pe.wait_ge(s["kt_copied"], c * pairs)
                    for g in range(4):
                        last = pe.transpose(turned[:, p % 2, g * P:(g + 1) * P], raw[:, p, g, :], ident)
                    last.then_inc(s["turned"], 1)
                    if p >= 1:
                        if p == 1:
                            pe.wait_ge(s["total_copied"], c)
                        weigh(n - 1, p - 1)
                    pe.wait_ge(s["kt_copied"], n + 1)
                    pe.matmul(dots[:, p % 2, :], qd[:, p, :, :, :].rearrange("p b h t -> p (b h t)"), kt[:, p % 2, :],
                              start=True, stop=True).then_inc(s["dotted"], 1)
                weigh(c * pairs + pairs - 1, pairs - 1)
            for p in range(pairs):
                last = pe.matmul(dots[:, 0, p * DEC_T:(p + 1) * DEC_T],
                                 qd[:, p, :, :, :].rearrange("p b h t -> p (b h t)"), kn[:, p, :],
                                 start=True, stop=True)
            last.then_inc(s["new_dotted"], 1)
            pe.wait_ge(s["new_rectified"], 1)
            pe.wait_ge(s["total_copied"], chunks)
            for p in range(pairs):
                last = pe.matmul(total[0:SAMPLE, 0:DEC_T], wsel[:, p, :], rel[:, 0, p * DEC_T:(p + 1) * DEC_T],
                                 start=p == 0, stop=p == pairs - 1)
            last.then_inc(s["new_weighed"], 1)

        @block.scalar
        def _(act):
            def rectify(c, p):
                n = c * pairs + p
                act.wait_ge(s["dotted"], n + 1)
                act.wait_ge(s["weighed"], n - 1 if p >= 2 else c * pairs)
                act.activation(rel[:, p % 2, :], dots[:, p % 2, :], ACT.Relu, scale=HD ** -0.5
                               ).then_inc(s["rectified"], 1)

            for p in range(pairs):
                load_step(act, "act", 0, p, first=True)
            with act.Fori(0, chunks - 1) as c:
                for p in range(pairs):
                    rectify(c, p)
                    load_step(act, "act", c + 1, p)
            for p in range(pairs):
                rectify(chunks - 1, p)
            act.wait_ge(s["new_dotted"], 1)
            act.wait_ge(s["weighed"], chunks * pairs)
            act.activation(rel[:, 0, 0:pairs * DEC_T], dots[:, 0, 0:pairs * DEC_T], ACT.Relu, scale=HD ** -0.5
                           ).then_inc(s["new_rectified"], 1)

        @block.vector
        def _(dve):
            own = own_chain(dve, s, "own")
            own(dve.memset(qd[:, :, :, :, :], 0.0))
            for b2 in range(2):
                rows = slice(b2 * HD, (b2 + 1) * HD)
                q8 = qi[:, :, PROMPT:NT].rearrange("d j (p b t) -> d j p b t", p=pairs, b=2)
                for hp in range(2):
                    for p in range(pairs):
                        dst = qd[rows, p, b2, :, :].rearrange("d (j e) t -> d j e t", e=2)[:, :, hp, :]
                        dve.tensor_copy(dst, q8[hp * HD:(hp + 1) * HD, :, p, b2, :])
                k8 = ki_t[:, PROMPT:NT].rearrange("d (p b t) -> d p b t", p=pairs, b=2)
                dve.tensor_copy(kn[rows, :, :], k8[rows, :, b2, :])
            dve.wait_ge(s["picked"], 1)
            own(dve.tensor_tensor(wpick[:, :, :], small[:, :, :], head_of.unsqueeze(1).to_broadcast([P, pairs, 8]),
                                  ALU.mult))
            own(dve.tensor_reduce(wcol[:, :], wpick[:, :, :], AX.X, ALU.add))
            dve.tensor_tensor(wsel[:, :, :], sel_t, over_cols(wcol[:, :], SAMPLE), ALU.mult
                              ).then_inc(s["tables_made"], 1)
            with dve.Fori(0, chunks) as c:
                for p in range(pairs):
                    n = c * pairs + p
                    dve.wait_ge(s["turned"], n + 1)
                    dve.wait_ge(s["dotted"], n - 1 if p >= 2 else c * pairs)
                    dve.tensor_copy(kt[:, p % 2, :], turned[:, p % 2, :]).then_inc(s["kt_copied"], 1)
                dve.wait_ge(s["weighed"], c * pairs + pairs)
                dve.tensor_copy(scores[:, bass.ts(c, 512)], total[0:SAMPLE, :]).then_inc(s["total_copied"], 1)
            dve.wait_ge(s["new_weighed"], 1)
            dve.tensor_tensor(scores[:, PAST:KEYS], total[0:SAMPLE, 0:DEC_T], later, ALU.add)


ACT_PARTS = 3
TOP_BITS = 32


def top_items():
    return [(i, w, "dve") for i, w in enumerate(WIDTHS)] + [(-1, KEYS, "act")]


def top_tables():
    cols = []
    for _, w, eng in top_items():
        a = eng == "act"
        cols.append([w - TOPK + 1, 2 * TOPK - 1 - w, 2 if a else 1, -w if a else 0])
    table = np.broadcast_to(np.array(cols, np.float32).T[None], (P, 4, len(cols)))
    ints = [1 << b for b in reversed(range(TOP_BITS - 1))] + [0]
    ints += [-1 << 31 if eng == "act" else 0 for _, _, eng in top_items()]
    bits = np.broadcast_to(np.array(ints, np.int32)[None], (P, len(ints)))
    return np.ascontiguousarray(table), np.ascontiguousarray(bits)


class TopSearch:

    def __init__(self, nc, ctx, table, bits, scores_p, scores_s, bias_p, bias_s):
        sc = Scope(nc, ctx, "top")
        self.items = top_items()
        n = self.n = len(self.items)
        self.table, self.bits = table, bits
        self.scores_p, self.scores_s, self.bias_p, self.bias_s = scores_p, scores_s, bias_p, bias_s
        self.found, self.cand, self.hit, self.low, self.high = (
            sc.sb(i, [P, n], I32) for i in ("found", "cand", "hit", "low", "high"))
        self.count, self.sign, self.limit, self.exact, self.thr, self.above, self.need = (
            sc.sb(i, [P, n]) for i in ("count", "sign", "limit", "exact", "thr", "above", "need"))
        self.parts = sc.sb("parts", [SAMPLE, ACT_PARTS])

    def rows(self, i):
        return slice(0, P) if self.items[i][0] >= 0 else slice(0, SAMPLE)

    def score(self, i):
        t, w, _ = self.items[i]
        return self.scores_p[:, STARTS[t]:STARTS[t] + w] if t >= 0 else self.scores_s[:, :]

    def bias(self, i):
        t, w, _ = self.items[i]
        return self.bias_p[:, STARTS[t]:STARTS[t] + w] if t >= 0 else self.bias_s[:, :]

    def compare(self, dve, which, level, op, into=None):
        into = self.count if into is None else into
        for i in which:
            r = self.rows(i)
            ins = dve.tensor_scalar(self.bias(i), self.score(i), level(r, i), 0.0, op, ALU.add,
                                    accum_out=into[r, i:i + 1])
        return ins

    def candidates(self, r, i):
        return self.cand[r, i:i + 1].bitcast(F32)

    def this_bit(self, bit):
        return self.bits[:, bass.ds(bit, 1)].to_broadcast([P, self.n])

    def start(self, dve, bit, cand_made):
        dve.tensor_tensor(self.cand[:, :], self.found[:, :], self.this_bit(bit), ALU.bitwise_or
                          ).then_inc(cand_made, 1)
        dve.wait_ge(cand_made, bit + 1)

    def count_act(self, act, bit, part, cand_made, act_counted):
        i, w = self.n - 1, KEYS // ACT_PARTS
        if part == 0:
            act.wait_ge(cand_made, bit + 1)
        keys = slice(part * w, (part + 1) * w)
        act.activation(self.bias_s[:, keys], self.scores_s[:, keys], ACT.Sign, bias=self.candidates(self.rows(i), i),
                       accum_out=self.parts[:, part:part + 1]).then_inc(act_counted, 1)

    def finish(self, dve, bit, own, act_counted):
        dve.wait_ge(act_counted, (bit + 1) * ACT_PARTS)
        own(dve.tensor_reduce(self.count[0:SAMPLE, self.n - 1:self.n], self.parts[:, :], AX.X, ALU.add))
        own(dve.tensor_tensor(self.hit[:, :], self.count[:, :], self.limit[:, :], ALU.is_ge))
        own(dve.tensor_tensor(self.hit[:, :], self.hit[:, :], self.this_bit(bit), ALU.mult))
        own(dve.tensor_tensor(self.found[:, :], self.found[:, :], self.hit[:, :], ALU.bitwise_or))

    def next_floats(self, dve, own):
        found, low, high, hit = (x[:, :] for x in (self.found, self.low, self.high, self.hit))
        own(dve.tensor_scalar(found, found, 0x7FFFFFFF, None, ALU.bitwise_and))
        own(dve.tensor_scalar(low, found, 0xFFFFF, None, ALU.bitwise_and))
        own(dve.tensor_scalar(high, found, 0x7FF00000, None, ALU.bitwise_and))
        own(dve.tensor_scalar(low, low, 1, None, ALU.add))
        own(dve.tensor_scalar(hit, low, 0x100000, None, ALU.bitwise_and))
        own(dve.tensor_tensor(high, high, hit, ALU.add))
        own(dve.tensor_scalar(low, low, 0xFFFFF, None, ALU.bitwise_and))
        own(dve.tensor_tensor(self.cand[:, :], high, low, ALU.bitwise_or))

    def choose(self, dve, own, i, step, equal, rank, chosen):
        r, w, col = self.rows(i), self.items[i][1], slice(i, i + 1)
        eq, rk, score = equal[r, 0:w], rank[r, 0:w], self.score(i)
        if step == 0:
            own(self.compare(dve, [i], self.candidates, ALU.is_ge))
            own(dve.tensor_tensor(self.hit[:, col], self.count[:, col], self.exact[:, col], ALU.is_ge))
            own(dve.copy_predicated(self.found[:, col], self.hit[:, col], self.cand[:, col]))
            own(dve.tensor_tensor(self.thr[:, col], self.found[:, col].bitcast(F32), self.sign[:, col], ALU.mult))
        elif step == 1:
            own(dve.tensor_scalar(score, score, self.sign[r, col], None, ALU.mult))
            own(self.compare(dve, [i], lambda r, i: self.thr[r, i:i + 1], ALU.is_gt, self.above))
            own(dve.tensor_scalar(self.need[:, col], self.above[:, col], -1.0, float(TOPK), ALU.mult, ALU.add))
        elif step == 2:
            own(dve.tensor_scalar(eq, score, self.thr[r, col], None, ALU.is_equal))
        elif step == 3:
            own(dve.tensor_tensor_scan(rk, eq, eq, 0.0, ALU.add, ALU.max))
        elif step == 4:
            own(dve.scalar_tensor_tensor(rk, rk, self.need[r, col], eq, ALU.is_le, ALU.mult))
        else:
            dve.scalar_tensor_tensor(score, score, self.thr[r, col], rk, ALU.is_gt, ALU.add).then_inc(chosen, 1)


def top_begin(nc, top):
    with ExitStack() as ctx:
        s = Named(Scope(nc, ctx, "topb"))
        block = ctx.enter_context(nc.Block())

        @block.vector
        def _(dve):
            own = own_chain(dve, s, "own")
            for t in (top.count, top.above):
                dve.memset(t[:, :], 0.0)
            own(dve.tensor_copy(top.found[:, :], top.bits[:, TOP_BITS:TOP_BITS + top.n]))
            own(top.compare(dve, range(top.n), lambda r, i: 0.0, ALU.is_ge))
            own(dve.tensor_scalar(top.sign[:, :], top.count[:, :], float(TOPK), None, ALU.is_ge))
            own(dve.tensor_tensor(top.exact[:, :], top.sign[:, :], top.table[:, 1, :], ALU.mult))
            own(dve.tensor_tensor(top.exact[:, :], top.exact[:, :], top.table[:, 0, :], ALU.add))
            own(dve.tensor_scalar(top.sign[:, :], top.sign[:, :], 2.0, -1.0, ALU.mult, ALU.add))
            own(dve.tensor_tensor(top.limit[:, :], top.exact[:, :], top.table[:, 2, :], ALU.mult))
            own(dve.tensor_tensor(top.limit[:, :], top.limit[:, :], top.table[:, 3, :], ALU.add))
            for i in range(top.n):
                dve.tensor_scalar(top.score(i), top.score(i), top.sign[top.rows(i), i:i + 1], None, ALU.mult)


def attend_prompt(nc, ident, ident_bf, causal_bf, q_in, k_t, v_tok, top, mix_hi, mix_lo):
    bias_p = top.bias_p
    cut_steps = 6
    tiles = TILES - 1
    work = [(t, h) for t in range(tiles) for h in range(8)]
    groups = [(t + 4) // 4 for t, _ in work]
    before = [sum(groups[:n]) for n in range(len(work) + 1)]
    with ExitStack() as ctx:
        sc = Scope(nc, ctx, "att")
        q = sc.sb("q", [P, 4, NT])
        probs = sc.sb("probs", [P, 2, PROMPT])
        probs_t = sc.sb("probs_t", [P, 2, 8, P])
        peak, low = sc.sb("peak", [P, 2]), sc.sb("low", [P, 2])
        sums = sc.sb("sums", [P, 2, 8])
        out = sc.sb("out", [P, 2, 8, HD])
        equal = sc.sb("equal", [P, KEYS], BF16)
        rank = sc.sb("rank", [P, KEYS])
        dots = sc.ps("dots", [P, 2, PROMPT])
        turned = sc.ps("turned", [P, 2, 4, P])
        values = sc.ps("values", [P, 8, HD])
        out_t = sc.ps("out_t", [P, 4, P])
        s = Named(sc)
        block = ctx.enter_context(nc.Block())

        @block.sync
        def _(sp):
            for j in range(4):
                sp.dma_start(q[:, j, :], q_in[j]).then_inc(s["q_in"], 16)

        @block.tensor
        def _(pe):
            pe.wait_ge(s["q_in"], 64)

            def dot(n):
                t, h = work[n]
                rows, w = slice(h // 4 * HD, h // 4 * HD + HD), (t + 1) * P
                if h == 0 and t > 1:
                    pe.wait_ge(s["cut_made"], t - 1)
                if n >= 2:
                    pe.wait_ge(s["exps_done"], n - 1)
                for lo in range(0, w, 512):
                    hi = min(lo + 512, w)
                    cut = t > 1 or hi == w
                    last = pe.matmul(dots[:, n % 2, lo:hi], q[rows, h % 4, t * P:(t + 1) * P], k_t[rows, lo:hi],
                                     start=True, stop=not cut)
                    if t > 1:
                        start = STARTS[t - 2]
                        last = pe.matmul(dots[:, n % 2, lo:hi], ident_bf, bias_p[:, start + lo:start + hi],
                                         start=False, stop=True)
                    elif cut:
                        last = pe.matmul(dots[:, n % 2, w - P:w], ident_bf, causal_bf, start=False, stop=True)
                last.then_inc(s["dotted"], 1)

            def turn(n):
                t, _ = work[n]
                pe.wait_ge(s["exps_done"], n + 1)
                for g in range(groups[n]):
                    i = before[n] + g
                    if i >= 2:
                        pe.wait_ge(s["turned_copied"], i - 1)
                    for kb in range(4 * g, min(4 * g + 4, t + 1)):
                        last = pe.transpose(turned[:, i % 2, kb % 4, :], probs[:, n % 2, kb * P:(kb + 1) * P], ident)
                    last.then_inc(s["turned"], 1)

            def weigh(n):
                t, h = work[n]
                pe.wait_ge(s["turned_copied"], before[n + 1])
                if h == 0 and t > 0:
                    pe.wait_ge(s["scaled"], t)
                for kb in range(t + 1):
                    last = pe.matmul(values[:, h, :], probs_t[:, n % 2, kb, :],
                                     v_tok[:, kb, h // 4 * HD:h // 4 * HD + HD], start=kb == 0, stop=kb == t)
                last.then_inc(s["weighed"], 1)

            def turn_out(t):
                pe.wait_ge(s["scaled"], t + 1)
                if t > 0:
                    pe.wait_ge(s["lo_done"], t)
                for j in range(4):
                    last = pe.transpose(out_t[:, j, :], out[:, t % 2, 2 * j:2 * j + 2, :].rearrange("p h d -> p (h d)"),
                                        ident)
                last.then_inc(s["out_turned"], 1)

            dot(0)
            for n, (t, h) in enumerate(work):
                if n + 1 < len(work):
                    dot(n + 1)
                if n >= 1:
                    weigh(n - 1)
                if h == 1 and t > 0:
                    turn_out(t - 1)
                turn(n)
            weigh(len(work) - 1)
            turn_out(tiles - 1)

        @block.scalar
        def _(act):
            def hi(t):
                act.wait_ge(s["out_turned"], t + 1)
                act.activation(mix_hi[:, 0:4, t * P:(t + 1) * P], out_t[:, :, :], ACT.Copy).then_inc(s["hi_done"], 1)

            for n, (t, h) in enumerate(work):
                act.wait_ge(s["max_done"], n + 1)
                if n >= 2:
                    act.wait_ge(s["turned"], before[n - 1])
                if h == 0 and t >= 2:
                    act.wait_ge(s["scaled"], t - 1)
                act.activation(probs[:, n % 2, 0:(t + 1) * P], dots[:, n % 2, 0:(t + 1) * P], ACT.Exp,
                               scale=HD ** -0.5, bias=low[:, n % 2:n % 2 + 1], accum_out=sums[:, t % 2, h:h + 1]
                               ).then_inc(s["exps_done"], 1)
                if h == 3 and t > 0:
                    hi(t - 1)
                if h == cut_steps and t > 0:
                    act.wait_ge(s["chosen"], t)
                    act.activation(top.bias(t - 1), top.score(t - 1), ACT.Copy, scale=BIG, bias=-BIG
                                   ).then_inc(s["cut_made"], 1)
            hi(tiles - 1)

        @block.vector
        def _(dve):
            own = own_chain(dve, s, "own")

            def low_part(t):
                dve.wait_ge(s["hi_done"], t + 1)
                cols = slice(t * P, (t + 1) * P)
                dve.tensor_tensor(mix_lo[:, 0:4, cols], out_t[:, :, :], mix_hi[:, 0:4, cols].bitcast(F32),
                                  ALU.subtract).then_inc(s["lo_done"], 1)

            def scale(t):
                dve.wait_ge(s["weighed"], t * 8 + 8)
                own(dve.reciprocal(sums[:, t % 2, :], sums[:, t % 2, :]))
                if t >= 2:
                    dve.wait_ge(s["out_turned"], t - 1)
                dve.tensor_tensor(out[:, t % 2], values[:, :, :], over_cols(sums[:, t % 2, :], HD), ALU.mult
                                  ).then_inc(s["scaled"], 1)

            def maximum(n):
                t, _ = work[n]
                dve.wait_ge(s["dotted"], n + 1)
                own(dve.tensor_reduce(peak[:, n % 2:n % 2 + 1], dots[:, n % 2, 0:(t + 1) * P], AX.X, ALU.max))
                dve.tensor_scalar(low[:, n % 2:n % 2 + 1], peak[:, n % 2:n % 2 + 1], -(HD ** -0.5), None, ALU.mult
                                  ).then_inc(s["max_done"], 1)

            def copy(n):
                t, _ = work[n]
                if n >= 2:
                    dve.wait_ge(s["weighed"], n - 1)
                for g in range(groups[n]):
                    i, kbs = before[n] + g, slice(4 * g, min(4 * g + 4, t + 1))
                    dve.wait_ge(s["turned"], i + 1)
                    dve.tensor_copy(probs_t[:, n % 2, kbs, :], turned[:, i % 2, 0:kbs.stop - kbs.start, :]
                                    ).then_inc(s["turned_copied"], 1)

            top.next_floats(dve, own)
            maximum(0)
            for n, (t, h) in enumerate(work):
                if n + 1 < len(work):
                    if n >= 1:
                        dve.wait_ge(s["exps_done"], n)
                    maximum(n + 1)
                if h == 0 and t > 0:
                    scale(t - 1)
                if h == 4 and t > 0:
                    low_part(t - 1)
                copy(n)
                if t > 0 and h < cut_steps:
                    if h == 2 and t > 1:
                        dve.wait_ge(s["chosen"], t - 1)
                    top.choose(dve, own, t - 1, h, equal, rank, s["chosen"])
            scale(tiles - 1)
            low_part(tiles - 1)


def attend_sample(nc, ident, cache_k, cache_v, q_in, k_t, v_tok, sel_bf, pages, bias_s, mix_hi, mix_lo):
    pairs, chunks = DEC_B // 2, PAGES // 4
    bufs = 4
    order = [("A", 0), ("A", 1), ("B", 0), ("A", 2), ("B", 1), ("A", 3), ("B", 2), ("B", 3)]
    with ExitStack() as ctx:
        sc = Scope(nc, ctx, "ats")
        q = sc.sb("q", [P, 4, SAMPLE])
        qs = sc.sb("qs", [P, pairs, 2, 2, 2, 4, DEC_T])
        k_raw = sc.sb("k_raw", [P, bufs, 2, 4, P])
        v_raw = sc.sb("v_raw", [P, bufs, 2, 4, P])
        kt = sc.sb("kt", [P, 2, 2, 512])
        scores = sc.sb("scores", [P, 2, KEYS])
        probs = sc.sb("probs", [P, 2, 512])
        probs_t = sc.sb("probs_t", [P, 2, 4, P])
        new_probs = sc.sb("new_probs", [P, pairs, SAMPLE])
        new_probs_t = sc.sb("new_probs_t", [SAMPLE, P])
        tops = sc.sb("tops", [P, 2, chunks + 1])
        low = sc.sb("low", [P, 2])
        sums = sc.sb("sums", [P, 4])
        out = sc.sb("out", [P, 2, HD])
        turned = sc.ps("turned", [P, 2, 512])
        dots = sc.ps("dots", [P, 2, 512])
        probs_ps = sc.ps("probs_ps", [P, 2, 4, P])
        values = sc.ps("values", [P, P])
        small = sc.ps("small", [P, 512])
        s = Named(sc)
        block = ctx.enter_context(nc.Block())

        def new_keys(p, b2):
            return slice(PROMPT + (2 * p + b2) * DEC_T, PROMPT + (2 * p + b2 + 1) * DEC_T)

        share = {"A": {"sp": [(0, 0), (0, 1), (0, 2), (0, 3)], "pool": [(1, 0), (1, 1), (1, 2), (1, 3)]},
                 "B": {"sp": [(0, 0), (0, 1), (0, 2), (0, 3)], "pool": [(1, 0), (1, 1), (1, 2)], "act": [(1, 3)]}}

        def load_chunk(eng, who, kind, p, i, par, first=False):
            if who not in share[kind]:
                return
            cache, raw, used = (cache_k, k_raw, "turned1") if kind == "A" else (cache_v, v_raw, "v_used")
            if not first:
                eng.wait_ge(s[used], p * chunks + i * bufs + par - bufs + 1)
            for b2, g in share[kind][who]:
                load_page(eng, cache, pages, (p * 2 + b2) * PAGES + (i * bufs + par) * 4 + g,
                          raw[:, par, b2, g, :], s[f"{kind}_in_{who}{par}"])

        def load_all(eng, who):
            for kind, p in order:
                if p == 0:
                    for par in range(bufs):
                        load_chunk(eng, who, kind, p, 0, par, first=True)
                with eng.Fori(1 if p == 0 else 0, chunks // bufs) as i:
                    for par in range(bufs):
                        load_chunk(eng, who, kind, p, i, par)

        def pages_in(pe, kind, p, i, par):
            for who, which in share[kind].items():
                pe.wait_ge(s[f"{kind}_in_{who}{par}"], (p * chunks // bufs + i + 1) * 16 * len(which))

        @block.sync
        def _(sp):
            for j in range(4):
                sp.dma_start(q[:, j, :], q_in[j, :, PROMPT:NT]).then_inc(s["q_in"], 16)
            load_all(sp, "sp")

        @block.gpsimd
        def _(pool):
            load_all(pool, "pool")

        @block.tensor
        def _(pe):
            pe.wait_ge(s["tables_made"], 1)

            def part_a(p):
                with pe.Fori(0, chunks // bufs) as i:
                    for par in range(bufs):
                        n = p * chunks + i * bufs + par
                        pages_in(pe, "A", p, i, par)
                        for b2 in range(2):
                            pe.wait_ge(s[f"kt_copied{b2}"], n)
                            for g in range(4):
                                last = pe.transpose(turned[:, b2, g * P:(g + 1) * P], k_raw[:, par, b2, g, :], ident)
                            last.then_inc(s[f"turned{b2}"], 1)
                        pe.wait_ge(s["tops_read"], n - 1 if p > 0 or par > 0 else i * bufs)
                        for b2 in range(2):
                            pe.wait_ge(s[f"kt_copied{b2}"], n + 1)
                            pe.matmul(dots[:, par % 2, :], qs[:, p, b2].rearrange("p a k g t -> p (a k g t)"),
                                      kt[:, par % 2, b2, :], start=b2 == 0, stop=False)
                        pe.matmul(dots[:, par % 2, :], sel_bf[:, p, :], bias_s[:, bass.ts(i * bufs + par, 512)],
                                  start=False, stop=True).then_inc(s["dotted"], 1)
                if p == 1:
                    pe.wait_ge(s["new_dots_read"], 1)
                elif p >= 2:
                    pe.wait_ge(s["lo_done"], p - 1)
                for b2 in range(2):
                    pe.matmul(small[:, 0:DEC_T], qs[:, p, b2].rearrange("p a k g t -> p (a k g t)"),
                              k_t[:, new_keys(p, b2)], start=b2 == 0, stop=False)
                pe.matmul(small[:, 0:DEC_T], sel_bf[:, p, :], bias_s[:, PAST:KEYS], start=False, stop=True
                          ).then_inc(s["new_dotted"], 1)

            def part_b(p):
                pe.wait_ge(s["new_dots_read"], min(p + 2, pairs))
                if p == pairs - 1:
                    pe.wait_ge(s["lo_done"], p)
                pe.wait_ge(s["new_probs_made"], p + 1)
                pe.transpose(small[0:SAMPLE, 0:P], new_probs[:, p, :], ident).then_inc(s["new_probs_turned"], 1)
                pe.wait_ge(s["new_probs_copied"], p + 1)
                if p >= 1:
                    pe.wait_ge(s["scaled"], p)
                pe.matmul(values[:, :], new_probs_t[:, :], v_tok[0:SAMPLE, TILES - 1, :], start=True, stop=False)

                def chunk(i, par, stop):
                    n = p * chunks + i * bufs + par
                    pe.wait_ge(s["exps_done"], n + 1)
                    pe.wait_ge(s["probs_copied"], n - 1 if p > 0 or par > 0 else i * bufs)
                    for g in range(4):
                        last = pe.transpose(probs_ps[:, par % 2, g, :], probs[:, par % 2, g * P:(g + 1) * P], ident)
                    last.then_inc(s["probs_turned"], 1)
                    pe.wait_ge(s["probs_copied"], n + 1)
                    pages_in(pe, "B", p, i, par)
                    for b2 in range(2):
                        rows = slice(b2 * HD, (b2 + 1) * HD)
                        for g in range(4):
                            last = pe.matmul(values[rows, :], probs_t[:, par % 2, g, rows], v_raw[:, par, b2, g, :],
                                             start=False, stop=stop and g == 3)
                    last.then_inc(s["v_used"], 1)

                with pe.Fori(0, chunks // bufs - 1) as i:
                    for par in range(bufs):
                        chunk(i, par, False)
                for par in range(bufs):
                    chunk(chunks // bufs - 1, par, par == bufs - 1)
                pe.wait_ge(s["scaled"], p + 1)
                pe.transpose(small[:, 0:P], out[:, :, :].rearrange("p a d -> p (a d)"), ident
                             ).then_inc(s["out_turned"], 1)

            for kind, p in order:
                (part_a if kind == "A" else part_b)(p)

        def mix_view(mix, rows, p):
            return mix[rows, 0:4, PROMPT + 16 * p:PROMPT + 16 * (p + 1)].rearrange("d j (b t) -> d j b t", b=2)

        def out_view(rows, e):
            return small[rows, 0:P].rearrange("d (b j e t) -> d j e b t", b=2, j=4, e=2)[:, :, e, :, :]

        @block.scalar
        def _(act):
            def part_a(p):
                if p >= 2:
                    act.wait_ge(s["exps_done"], (p - 1) * chunks)

                def chunk(i, par):
                    n = p * chunks + i * bufs + par
                    act.wait_ge(s["turned0"], n + 1)
                    act.wait_ge(s["dotted"], n - 1 if p > 0 or par > 0 else i * bufs)
                    act.activation(kt[:, par % 2, 0, :], turned[:, 0, :], ACT.Copy).then_inc(s["kt_copied0"], 1)
                    act.wait_ge(s["dotted"], n + 1)
                    act.activation(scores[:, p % 2, bass.ts(i * bufs + par, 512)], dots[:, par % 2, :], ACT.Copy
                                   ).then_inc(s["dots_read"], 1)

                with act.Fori(0, chunks // bufs - 1) as i:
                    for par in range(bufs):
                        chunk(i, par)
                        load_chunk(act, "act", "A", p, i + 1, par)
                for par in range(bufs):
                    chunk(chunks // bufs - 1, par)
                    if p + 1 < pairs:
                        load_chunk(act, "act", "A", p + 1, 0, par)

            def part_b(p):
                act.wait_ge(s["low_made"], p + 1)
                act.wait_ge(s["dots_read"], (p + 1) * chunks)
                act.wait_ge(s["new_dots_read"], p + 1)
                if p >= 1:
                    act.wait_ge(s["new_probs_copied"], p)
                    act.wait_ge(s["sums_moved"], p)
                for b2 in range(2):
                    rows = slice(b2 * HD, (b2 + 1) * HD)
                    last = act.activation(new_probs[rows, p, (2 * p + b2) * DEC_T:(2 * p + b2 + 1) * DEC_T],
                                          scores[rows, p % 2, PAST:KEYS], ACT.Exp, scale=HD ** -0.5,
                                          bias=low[rows, p % 2:p % 2 + 1], accum_out=sums[rows, 2:3])
                last.then_inc(s["new_probs_made"], 1)

                def chunk(i, par, first=False):
                    n = p * chunks + i * bufs + par
                    if not first:
                        act.wait_ge(s["probs_turned"], n - 1)
                        act.wait_ge(s["sums_added"], n - 1)
                    act.activation(probs[:, par % 2, :], scores[:, p % 2, bass.ts(i * bufs + par, 512)], ACT.Exp,
                                   scale=HD ** -0.5, bias=low[:, p % 2:p % 2 + 1], accum_out=sums[:, par % 2:par % 2 + 1]
                                   ).then_inc(s["exps_done"], 1)

                for par in range(bufs):
                    chunk(0, par, first=p == 0 and par < 2)
                with act.Fori(1, chunks // bufs) as i:
                    for par in range(bufs):
                        chunk(i, par)
                        load_chunk(act, "act", "B", p, i, par)
                act.wait_ge(s["out_turned"], p + 1)
                for e in range(2):
                    rows = slice(e * HD, (e + 1) * HD)
                    ins = act.activation(mix_view(mix_hi, rows, p), out_view(rows, e), ACT.Copy)
                ins.then_inc(s["hi_done"], 1)
                if p + 1 < pairs:
                    for par in range(bufs):
                        load_chunk(act, "act", "B", p + 1, 0, par)

            for kind in "AB":
                for par in range(bufs):
                    load_chunk(act, "act", kind, 0, 0, par, first=True)
            for kind, p in order:
                (part_a if kind == "A" else part_b)(p)

        @block.vector
        def _(dve):
            own = own_chain(dve, s, "own")
            own(dve.memset(qs[:, :, :, :, :, :, :], 0.0))
            dve.memset(new_probs[:, :, :], 0.0)
            dve.wait_ge(s["q_in"], 64)
            for b2 in range(2):
                for kv in range(2):
                    rows = slice(kv * HD, (kv + 1) * HD)
                    q8 = q[rows, :, :].rearrange("d j (p b t) -> d p b j t", p=pairs, b=2)
                    ins = dve.tensor_copy(qs[rows, :, b2, b2, kv, :, :], q8[:, :, b2, :, :])
            ins.then_inc(s["tables_made"], 1)

            def part_a(p):
                if p >= 2:
                    dve.wait_ge(s["low_made"], p - 1)
                with dve.Fori(0, chunks // bufs) as i:
                    for par in range(bufs):
                        n = p * chunks + i * bufs + par
                        dve.wait_ge(s["turned1"], n + 1)
                        dve.wait_ge(s["dotted"], n - 1 if p > 0 or par > 0 else i * bufs)
                        dve.tensor_copy(kt[:, par % 2, 1, :], turned[:, 1, :]).then_inc(s["kt_copied1"], 1)
                        dve.wait_ge(s["dots_read"], n + 1)
                        dve.tensor_reduce(tops[:, p % 2, bass.ds(i * bufs + par, 1)], dots[:, par % 2, :], AX.X, ALU.max
                                          ).then_inc(s["tops_read"], 1)
                dve.wait_ge(s["new_dotted"], p + 1)
                own(dve.tensor_copy(scores[:, p % 2, PAST:KEYS], small[:, 0:DEC_T]))
                dve.tensor_reduce(tops[:, p % 2, chunks:chunks + 1], small[:, 0:DEC_T], AX.X, ALU.max
                                  ).then_inc(s["new_dots_read"], 1)
                dve.wait_ge(s["new_dots_read"], p + 1)
                dve.wait_ge(s["tops_read"], (p + 1) * chunks)
                if p >= 2:
                    dve.wait_ge(s["exps_done"], (p - 1) * chunks)
                own(dve.tensor_reduce(low[:, p % 2:p % 2 + 1], tops[:, p % 2, :], AX.X, ALU.max))
                dve.tensor_scalar(low[:, p % 2:p % 2 + 1], low[:, p % 2:p % 2 + 1], -(HD ** -0.5), None, ALU.mult
                                  ).then_inc(s["low_made"], 1)

            def part_b(p):
                dve.wait_ge(s["new_probs_turned"], p + 1)
                if p >= 1:
                    dve.wait_ge(s["v_used"], p * chunks)
                dve.tensor_copy(new_probs_t[:, :], small[0:SAMPLE, 0:P]).then_inc(s["new_probs_copied"], 1)
                dve.tensor_copy(sums[:, 3:4], sums[:, 2:3]).then_inc(s["sums_moved"], 1)
                dve.wait_ge(s["sums_moved"], p + 1)
                with dve.Fori(0, chunks // bufs) as i:
                    for par in range(bufs):
                        n = p * chunks + i * bufs + par
                        dve.wait_ge(s["exps_done"], n + 1)
                        dve.wait_ge(s["sums_added"], n)
                        dve.tensor_tensor(sums[:, 3:4], sums[:, 3:4], sums[:, par % 2:par % 2 + 1], ALU.add
                                          ).then_inc(s["sums_added"], 1)
                        dve.wait_ge(s["probs_turned"], n + 1)
                        dve.wait_ge(s["v_used"], n - 1 if p > 0 or par > 0 else i * bufs)
                        dve.tensor_copy(probs_t[:, par % 2, :, :], probs_ps[:, par % 2, :, :]).then_inc(s["probs_copied"], 1)
                dve.wait_ge(s["sums_added"], (p + 1) * chunks)
                own(dve.reciprocal(sums[:, 3:4], sums[:, 3:4]))
                dve.wait_ge(s["v_used"], (p + 1) * chunks)
                if p >= 1:
                    dve.wait_ge(s["out_turned"], p)
                for b2 in range(2):
                    for kv in range(2):
                        rows = slice(b2 * HD + kv * 32, b2 * HD + kv * 32 + 32)
                        ins = dve.tensor_scalar(out[rows, :, :],
                                                values[rows, kv * HD:(kv + 1) * HD].unsqueeze(1).to_broadcast(
                                                    [32, 2, HD]), sums[rows, 3:4], None, ALU.mult)
                ins.then_inc(s["scaled"], 1)
                dve.wait_ge(s["hi_done"], p + 1)
                for e in range(2):
                    rows = slice(e * HD, (e + 1) * HD)
                    ins = dve.tensor_tensor(mix_view(mix_lo, rows, p), out_view(rows, e),
                                            mix_view(mix_hi, rows, p).bitcast(F32), ALU.subtract)
                ins.then_inc(s["lo_done"], 1)

            for kind, p in order:
                (part_a if kind == "A" else part_b)(p)


def mixer_output(nc, w_o, res_in, mix_hi, mix_lo, res):
    with ExitStack() as ctx:
        sc = Scope(nc, ctx, "wo")
        raw = sc.sb("raw", [P, 2, 1024])
        w_hi = sc.sb("w_hi", [P, 2, 1024], F32R)
        w_lo = sc.sb("w_lo", [P, 2, 1024], F32R)
        ps = [sc.ps("ps_a", [P, SLICES, 512]), sc.ps("ps_b", [P, SLICES, 512])]
        s = Named(sc)
        block = ctx.enter_context(nc.Block())

        @block.sync
        def _(sp):
            for m in range(KT):
                if m >= 2:
                    sp.wait_ge(s["lo_made"], m - 1)
                sp.dma_start(raw[:, m % 2, :].rearrange("p (k f) -> p k f", k=KT),
                             w_o[0, :, m * P:(m + 1) * P].rearrange("(k p) f -> p k f", p=P)
                             ).then_inc(s[f"raw_in{m % 2}"], 16)

        @block.gpsimd
        def _(pool):
            for m in range(KT):
                pool.dma_start(res[:, m, :], res_in[m]).then_inc(s["res_in"], 16)

        @block.tensor
        def _(pe):
            pe.wait_ge(s["mix_padded"], 1)

            def pair(i, first=False):
                for par in range(2):
                    pe.wait_ge(s["lo_made"], i * 2 + par + 1)
                    if not first:
                        pe.wait_ge(s["added"], i * 2 + par - 1)
                    three_pass(pe, ps[par], lambda k: w_hi[:, par, k * P:(k + 1) * P],
                               lambda k: w_lo[:, par, k * P:(k + 1) * P], lambda k: mix_hi[:, k],
                               lambda k: mix_lo[:, k], range(KT)).then_inc(s["filled"], 1)

            pair(0, first=True)
            with pe.Fori(1, KT // 2) as i:
                pair(i)

        @block.scalar
        def _(act):
            for m in range(KT):
                act.wait_ge(s[f"raw_in{m % 2}"], 16 * (m // 2 + 1))
                if m >= 2:
                    act.wait_ge(s["filled"], m - 1)
                act.activation(w_hi[:, m % 2, :], raw[:, m % 2, :], ACT.Copy).then_inc(s["hi_made"], 1)

        @block.vector
        def _(dve):
            for mix in (mix_hi, mix_lo):
                ins = dve.memset(mix[:, 0:4, NT:TP].bitcast(F32), 0.0)
            ins.then_inc(s["mix_padded"], 1)

            def low(m):
                dve.wait_ge(s["hi_made"], m + 1)
                dve.tensor_tensor(w_lo[:, m % 2, :], raw[:, m % 2, :], w_hi[:, m % 2, :].bitcast(F32),
                                  ALU.subtract).then_inc(s["lo_made"], 1)

            low(0)
            low(1)
            dve.wait_ge(s["res_in"], 16 * KT)
            for m in range(KT):
                dve.wait_ge(s["filled"], m + 1)
                r = res[:, m, :].rearrange("p (s c) -> p s c", s=SLICES)
                dve.tensor_tensor(r, r, ps[m % 2][:, :, 0:SL], ALU.add).then_inc(s["added"], 1)
                if m + 2 < KT:
                    low(m + 2)


def shape_tables():
    i = np.arange(P)
    later = i[None, :] > i[:, None]
    t = {"ident": np.eye(P, dtype=np.float32), "ones": np.ones((P, P), np.float32),
         "ones_mean": np.full((P, P), 1.0 / D, np.float32)}
    t["cos"], t["sin"] = rope_tables()
    upper, strict, causal_t, levels = delta_masks(P, P)
    t["delta_tables"] = np.stack([upper, strict, causal_t] + levels, 1)
    upper, strict, causal_t, levels = delta_masks(SAMPLE, DEC_T)
    j = np.arange(SAMPLE)
    same = (j[:, None] // DEC_T == j[None, :] // DEC_T).astype(np.float32)
    t["delta_tables_s"] = np.stack([upper, strict, causal_t] + levels + [same], 1)
    t["member"] = (j[:, None] // DEC_T == np.arange(DEC_B)[None, :]).astype(np.float32)
    t["later_low"] = np.where(later, LOWEST, 0.0).astype(np.float32)
    t["later_big"] = np.where(later, -BIG, 0.0).astype(np.float32)
    t["sel"], t["sel_t"], t["head_of"], t["later_new"] = sample_tables()
    t["top_table"], t["top_bits"] = top_tables()
    return t


def load_constants(nc, name, pairs, casts=(), zeros=()):
    with ExitStack() as ctx:
        sc = Scope(nc, ctx, name)
        s = Named(sc)
        block = ctx.enter_context(nc.Block())

        @block.sync
        def _(sp):
            for dst, src in pairs:
                sp.dma_start(dst, src).then_inc(s["in"], 16)
            sp.wait_ge(s["in"], 16 * len(pairs))

        @block.vector
        def _(dve):
            for buf in zeros:
                dve.memset(buf[:, :, :], 0.0)
            dve.wait_ge(s["in"], 16 * len(pairs))
            for dst, src in casts:
                dve.tensor_copy(dst, src)


def decoder_step(nc, a, t, out):

    def dram(name, shape):
        return nc.dram_tensor(name, shape, F32).ap()

    q_d, qi_d, z_d = (dram(n, [4, P, NT]) for n in ("scratch_q", "scratch_qi", "scratch_z"))
    res_d = dram("scratch_res", [KT, P, TP])
    qkv_d = dram("scratch_qkv", [P, QKV_BLOCKS, NT])
    o_d = dram("scratch_o", [TILES, P, GH * P])
    with ExitStack() as ctx:
        sc = Scope(nc, ctx, "main")
        ident, ones, ones_mean = (sc.sb(n, [P, P]) for n in ("ident", "ones", "ones_mean"))
        k_t, ki_t = sc.sb("k_t", [P, TP]), sc.sb("ki_t", [P, TP])
        v_tok = sc.sb("v_tok", [P, TILES, P])
        wi_tok = sc.sb("wi_tok", [P, TILES, 8])
        beta, gate = sc.sb("beta", [P, TILES, GH]), sc.sb("gate", [P, TILES, GH])
        unit = sc.sb("unit", [P, TILES, 8])
        with nc.cleanup_on_exit():
            load_constants(nc, "tables", [(ident[:, :], t["ident"]), (ones[:, :], t["ones"]),
                                          (ones_mean[:, :], t["ones_mean"])])

        with ExitStack() as c1:
            m = Scope(nc, c1, "first")
            x_hi = m.sb("x_hi", [P, KT, TP], F32R)
            x_lo = m.sb("x_lo", [P, KT, TP], F32R)
            with ExitStack() as c2:
                res = Scope(nc, c2, "first").sb("res", [P, KT, TP])
                with nc.cleanup_on_exit():
                    load_tokens(nc, a["x_prompt"], a["x_sample"], ident, res, x_hi, x_lo)
                with nc.cleanup_on_exit():
                    ffn(nc, "ffn1", a["ffn1_w_gate"], a["ffn1_w_up"], a["ffn1_w_down"], res, x_hi, x_lo)
                with nc.cleanup_on_exit():
                    norm(nc, "ln1", a["ln1_g"], a["ln1_b"], ones_mean, res, x_hi, x_lo, resid_out=res_d)
            qkv_t = m.sb("qkv_t", [P, QKV_BLOCKS, NT])
            v_t, wba_t = m.sb("v_t", [P, TP]), m.sb("wba_t", [16, TP])
            taps, samp = m.sb("taps", [P, QKV_BLOCKS, CONV_K]), m.sb("samp", [P, QKV_BLOCKS, DEC_B, 11])
            conv_tail = m.sb("conv_tail", [P, QKV_BLOCKS, 3])
            with nc.cleanup_on_exit():
                conv_taps(nc, a["conv_w"], a["state_conv"], ident, taps, samp)
            with nc.cleanup_on_exit():
                project(nc, a["w_in"], t["cos"], t["sin"], x_hi, x_lo, taps, samp, k_t, v_t, ki_t, wba_t,
                        qkv_t, conv_tail, q_d, qi_d, z_d)
            with nc.cleanup_on_exit():
                projection_tail(
                    nc, ident, ones, k_t, v_t, ki_t, wba_t, qkv_t, conv_tail, samp, taps, a["a_log"],
                    a["dt_bias"], v_tok, wi_tok, beta, gate, unit,
                    (out["k_prompt"].rearrange("l b s k d -> (l b s) (k d)"),
                     out["k_sample"].rearrange("l b s k d -> (l b s) (k d)")),
                    (out["v_prompt"].rearrange("l b s k d -> (l b s) (k d)"),
                     out["v_sample"].rearrange("l b s k d -> (l b s) (k d)")),
                    (out["kidx_prompt"].rearrange("l b s d -> (l b s) d"),
                     out["kidx_sample"].rearrange("l b s d -> (l b s) d")),
                    (out["conv_prompt"].rearrange("l b r c -> (l b r) c"),
                     out["conv_sample"].rearrange("l b r c -> (l b r) c")), qkv_d)

        with ExitStack() as c1:
            m = Scope(nc, c1, "mixer")
            mix_hi = m.sb("mix_hi", [P, KT, TP], F32R)
            mix_lo = m.sb("mix_lo", [P, KT, TP], F32R)

            with ExitStack() as c2:
                g = Scope(nc, c2, "gdn_s")
                tab_s = g.sb("tab_s", [SAMPLE, 7, SAMPLE])
                member = g.sb("member", [SAMPLE, DEC_B])
                with nc.cleanup_on_exit():
                    load_constants(nc, "sample_tables", [(tab_s[:, :, :], t["delta_tables_s"]),
                                                         (member[:, :], t["member"])])
                with nc.cleanup_on_exit():
                    delta_sample(nc, ident, ones, (tab_s[:, 0], tab_s[:, 1], tab_s[:, 2],
                                                   [tab_s[:, 3 + l] for l in range(3)]), tab_s[:, 6],
                                 member[:, :], qkv_d, beta, gate, unit, a["state_gdn"][0],
                                 out["gdn_sample"].rearrange("l b h k v -> (l b) h k v"),
                                 o_d[TILES - 1, 0:SAMPLE])

            with ExitStack() as c2:
                b = Scope(nc, c2, "cut")
                bias_p, bias_s = b.sb("bias_p", [P, sum(WIDTHS)], BF16), b.sb("bias_s", [SAMPLE, KEYS], BF16)
                sel_bf = b.sb("sel_bf", [SAMPLE, 4, P], BF16)
                ident_bf, later_bf = b.sb("ident_bf", [P, P], BF16), b.sb("later_bf", [P, P], BF16)
                pages = b.sb("pages", [1, DEC_B * PAGES], I32)
                with ExitStack() as c3:
                    i = Scope(nc, c3, "index")
                    scores_p, scores_s = i.sb("scores_p", [P, sum(WIDTHS)]), i.sb("scores_s", [SAMPLE, KEYS])
                    top_table, top_bits = i.sb("top_table", [P, 4, 7]), i.sb("top_bits", [P, TOP_BITS + 7], I32)
                    with ExitStack() as c4:
                        j = Scope(nc, c4, "qi")
                        qi = j.sb("qi", [P, 4, NT])
                        later_low, later_big = j.sb("later_low", [P, P]), j.sb("later_big", [P, P])
                        sel, sel_t = j.sb("sel", [SAMPLE, 4, P]), j.sb("sel_t", [P, 4, SAMPLE])
                        head_of, later_new = j.sb("head_of", [P, 8]), j.sb("later_new", [SAMPLE, DEC_T])
                        with nc.cleanup_on_exit():
                            load_constants(nc, "index_tables", [
                                (later_low[:, :], t["later_low"]), (later_big[:, :], t["later_big"]),
                                (sel[:, :, :], t["sel"]), (sel_t[:, :, :], t["sel_t"]), (head_of[:, :], t["head_of"]),
                                (later_new[:, :], t["later_new"]), (top_table[:, :, :], t["top_table"]),
                                (top_bits[:, :], t["top_bits"]),
                                (pages[:, :], a["page_table"].rearrange("b p -> (b p)").unsqueeze(0))],
                                [(ident_bf[:, :], ident[:, :]), (later_bf[:, :], later_big[:, :]),
                                 (sel_bf[:, :, :], sel[:, :, :])])
                        with nc.cleanup_on_exit():
                            index_prompt(nc, qi_d, ki_t, wi_tok, later_low[:, :], qi, scores_p)
                        with nc.cleanup_on_exit():
                            index_sample(nc, ident[:, :], a["cache_kidx"], qi, ki_t, wi_tok, sel[:, :, :],
                                         sel_t[:, :, :], head_of[:, :], later_new[:, :], pages, scores_s)
                    top = TopSearch(nc, c3, top_table[:, :, :], top_bits[:, :], scores_p, scores_s, bias_p, bias_s)
                    with nc.cleanup_on_exit():
                        top_begin(nc, top)
                    with ExitStack() as c4:
                        g = Scope(nc, c4, "gdn")
                        state = g.sb("state", [P, GH, P])
                        tab = g.sb("tab", [P, 10, P])
                        with nc.cleanup_on_exit():
                            load_constants(nc, "delta_tables", [(tab[:, :, :], t["delta_tables"])], zeros=(state,))
                        with nc.cleanup_on_exit():
                            delta_prompt(nc, ident, ones, (tab[:, 0], tab[:, 1], tab[:, 2],
                                                           [tab[:, 3 + l] for l in range(7)]),
                                         qkv_d, beta, gate, unit, state,
                                         out["gdn_prompt"].rearrange("l b h k v -> k (l b h) v"), o_d, top)
                    with nc.cleanup_on_exit():
                        delta_finish(nc, ident, a["gdn_norm_w"], z_d, o_d, mix_hi, mix_lo)
                    with nc.cleanup_on_exit():
                        attend_prompt(nc, ident[:, :], ident_bf[:, :], later_bf[:, :], q_d, k_t, v_tok, top,
                                      mix_hi, mix_lo)

                with nc.cleanup_on_exit():
                    attend_sample(nc, ident[:, :], a["cache_k"].rearrange("l n p k d -> l n p (k d)"),
                                  a["cache_v"].rearrange("l n p k d -> l n p (k d)"), q_d, k_t, v_tok, sel_bf, pages,
                                  bias_s, mix_hi, mix_lo)

            with ExitStack() as c2:
                res = Scope(nc, c2, "second").sb("res", [P, KT, TP])
                with nc.cleanup_on_exit():
                    mixer_output(nc, a["w_o"], res_d, mix_hi, mix_lo, res)
                with nc.cleanup_on_exit():
                    norm(nc, "ln2", a["ln2_g"], a["ln2_b"], ones_mean, res, mix_hi, mix_lo)
                with nc.cleanup_on_exit():
                    ffn(nc, "ffn2", a["ffn2_w_gate"], a["ffn2_w_up"], a["ffn2_w_down"], res, mix_hi, mix_lo)
                with nc.cleanup_on_exit():
                    norm(nc, "ln3", a["ln3_g"], a["ln3_b"], ones_mean, res, None, None)
                with nc.cleanup_on_exit():
                    store_tokens(nc, ident, res, out["y_prompt"], out["y_sample"])


_INS = ["x_prompt", "x_sample", "cache_k", "cache_v", "cache_kidx", "state_gdn", "state_conv", "page_table",
        "ffn1_w_gate", "ffn1_w_up", "ffn1_w_down", "ln1_g", "ln1_b", "w_in", "conv_w", "a_log", "dt_bias",
        "gdn_norm_w", "w_o", "ln2_g", "ln2_b", "ffn2_w_gate", "ffn2_w_up", "ffn2_w_down", "ln3_g", "ln3_b"]
_OUTS = {"y_prompt": (1, 1024, 1024), "y_sample": (8, 8, 1024), "k_prompt": (1, 1, 1024, 2, 64),
         "v_prompt": (1, 1, 1024, 2, 64), "kidx_prompt": (1, 1, 1024, 64), "gdn_prompt": (1, 1, 4, 128, 128),
         "conv_prompt": (1, 1, 3, 1536), "k_sample": (1, 8, 8, 2, 64), "v_sample": (1, 8, 8, 2, 64),
         "kidx_sample": (1, 8, 8, 64), "gdn_sample": (1, 8, 4, 128, 128), "conv_sample": (1, 8, 3, 1536)}


def kernel(**inputs):
    import concourse.bacc as _bacc
    from concourse.bass_utils import run_bass_kernel_spmd as _run

    nc = _bacc.Bacc("TRN2", target_bir_lowering=False, num_devices=1)
    arrays = {f"in_{name}": np.ascontiguousarray(inputs[name]) for name in _INS}
    tables = {f"table_{name}": np.ascontiguousarray(v) for name, v in shape_tables().items()}
    aps = {}
    for name, v in {**arrays, **tables}.items():
        aps[name] = nc.dram_tensor(name, v.shape, mybir.dt.from_np(v.dtype), kind="ExternalInput").ap()
    out = {n: nc.dram_tensor(f"out_{n}", shape, F32, kind="ExternalOutput").ap() for n, shape in _OUTS.items()}
    decoder_step(nc, {n[3:]: aps[n] for n in arrays}, {n[6:]: aps[n] for n in tables}, out)
    r = _run(nc, [{**arrays, **tables}], core_ids=[0])
    return tuple(r.results[0][f"out_{n}"] for n in _OUTS)
```
